# Optimizing a Trainium2 kernel written in Bass

```python
import numpy as np
import jax, jax.numpy as jnp
from jax import lax

D_MODEL = 1024
BATCH = 1
SEQ = 256
DEPTH = 2

SSD_HEADS = 8
SSD_HEAD_DIM = 64
SSD_INNER = SSD_HEADS * SSD_HEAD_DIM
SSD_GROUPS = 2
SSD_STATE = 128
SSD_CONV = 4
SSD_CHUNK = 128
SSD_XBC = SSD_INNER + 2 * SSD_GROUPS * SSD_STATE
RET_HEADS = 4
RET_QK_DIM = 64
RET_V_DIM = 128
RET_CHUNK = 128
MLA_HEADS = 8
MLA_Q_LORA = 256
MLA_KV_LORA = 128
MLA_NOPE = 64
MLA_ROPE = 32
MLA_V = 64
ATTN_BLOCK = 128
GLA_HEADS = 4
GLA_K_DIM = 64
GLA_V_DIM = 128
GLA_GATE_RANK = 16
GLA_GATE_NORM = 16.0
GLA_CHUNK = 64
N_BRANCHES = 4
BRANCH_WIDTH = 512
D_FF = 4 * D_MODEL
ROPE_THETA = 10000.0
RMS_EPS = 1e-6
MAX_POS_OFFSET = 4096
IN_WIDTH = (SSD_INNER + SSD_XBC + SSD_HEADS
            + RET_HEADS * (2 * RET_QK_DIM + 2 * RET_V_DIM)
            + MLA_Q_LORA + MLA_KV_LORA + MLA_ROPE
            + GLA_HEADS * (2 * GLA_K_DIM + 2 * GLA_V_DIM) + GLA_GATE_RANK
            + N_BRANCHES * D_MODEL)

kernel_name = "hybrid_ssd_ret_mla_gla_block"

def rms_norm(x, g, eps=RMS_EPS):
    xf = x.astype(jnp.float32)
    y = xf * lax.rsqrt(jnp.mean(xf * xf, axis=-1, keepdims=True) + eps)
    return (y * g.astype(jnp.float32)).astype(x.dtype)

def rope(x, positions):
    half = x.shape[-1] // 2
    inv_freq = ROPE_THETA ** (-jnp.arange(half, dtype=jnp.float32) / half)
    ang = positions.astype(jnp.float32)[:, :, None, None] * inv_freq
    cos, sin = jnp.cos(ang), jnp.sin(ang)
    xf = x.astype(jnp.float32)
    x1, x2 = xf[..., :half], xf[..., half:]
    return jnp.concatenate([x1 * cos - x2 * sin, x2 * cos + x1 * sin], axis=-1).astype(x.dtype)

def causal_depthwise_conv(x, w, b):
    k = w.shape[0]
    y = lax.conv_general_dilated(x, w[:, None, :], window_strides=(1,), padding=[(k - 1, 0)],
                                 dimension_numbers=('NWC', 'WIO', 'NWC'),
                                 feature_group_count=x.shape[-1])
    return y + b

def scalar_decay_chunked(q, k, v, log_g, chunk):
    b, l, h, n = q.shape
    p = v.shape[-1]
    nc = l // chunk
    qc = q.reshape(b, nc, chunk, h, n)
    kc = k.reshape(b, nc, chunk, h, n)
    vc = v.reshape(b, nc, chunk, h, p)
    a = log_g.astype(jnp.float32).reshape(b, nc, chunk, h).transpose(0, 3, 1, 2)
    cum = jnp.cumsum(a, axis=-1)
    seg = cum[..., :, None] - cum[..., None, :]
    mask = jnp.tril(jnp.ones((chunk, chunk), dtype=bool))
    decay = jnp.exp(jnp.where(mask, seg, -jnp.inf))
    scores = jnp.einsum('bcihn,bcjhn->bhcij', qc, kc) * decay
    y_diag = jnp.einsum('bhcij,bcjhp->bcihp', scores, vc)
    decay_to_end = jnp.exp(cum[..., -1:] - cum)
    states = jnp.einsum('bcjhn,bhcj,bcjhp->bchpn', kc, decay_to_end, vc)
    chunk_decay = jnp.exp(cum[..., -1])

    def step(carry, inp):
        dec, st = inp
        return dec[:, :, None, None] * carry + st, carry

    init = jnp.zeros((b, h, p, n), states.dtype)
    _, prev = lax.scan(step, init, (jnp.moveaxis(chunk_decay, 2, 0), jnp.moveaxis(states, 1, 0)))
    prev = jnp.moveaxis(prev, 0, 1)
    y_off = jnp.einsum('bcihn,bchpn,bhci->bcihp', qc, prev, jnp.exp(cum))
    return (y_diag + y_off).reshape(b, l, h, p).astype(v.dtype)

def gla_chunked(q, k, v, log_g, chunk):
    b, l, h, dk = q.shape
    dv = v.shape[-1]
    nc = l // chunk
    qc = q.reshape(b, nc, chunk, h, dk)
    kc = k.reshape(b, nc, chunk, h, dk)
    vc = v.reshape(b, nc, chunk, h, dv)
    cum = jnp.cumsum(log_g.astype(jnp.float32).reshape(b, nc, chunk, h, dk), axis=2)
    total = cum[:, :, -1:]
    q_in = qc * jnp.exp(cum)
    k_in = kc * jnp.exp(-cum)
    mask = jnp.tril(jnp.ones((chunk, chunk), dtype=bool))
    scores = jnp.where(mask, jnp.einsum('bcihd,bcjhd->bchij', q_in, k_in), 0.0)
    o_intra = jnp.einsum('bchij,bcjhv->bcihv', scores, vc)
    k_st = kc * jnp.exp(total - cum)
    states = jnp.einsum('bcjhd,bcjhv->bchdv', k_st, vc)
    chunk_decay = jnp.exp(total[:, :, 0])

    def step(carry, inp):
        dec, st = inp
        return dec[..., None] * carry + st, carry

    init = jnp.zeros((b, h, dk, dv), states.dtype)
    _, prev = lax.scan(step, init, (jnp.moveaxis(chunk_decay, 1, 0), jnp.moveaxis(states, 1, 0)))
    prev = jnp.moveaxis(prev, 0, 1)
    o_inter = jnp.einsum('bcihd,bchdv->bcihv', q_in, prev)
    return (o_intra + o_inter).reshape(b, l, h, dv).astype(v.dtype)

def causal_attention_blocked(q, k, v, scale):
    b, l, h, d = q.shape
    dv = v.shape[-1]
    nb = l // ATTN_BLOCK
    qb = q.reshape(b, nb, ATTN_BLOCK, h, d).transpose(1, 0, 2, 3, 4)
    starts = jnp.arange(nb, dtype=jnp.int32) * ATTN_BLOCK
    kpos = jnp.arange(l, dtype=jnp.int32)

    def one_block(args):
        qi, s0 = args
        s = jnp.einsum('bqhd,bkhd->bhqk', qi, k, preferred_element_type=jnp.float32) * scale
        qpos = s0 + jnp.arange(ATTN_BLOCK, dtype=jnp.int32)
        s = jnp.where(kpos[None, :] <= qpos[:, None], s, -jnp.inf)
        pr = jax.nn.softmax(s, axis=-1).astype(v.dtype)
        return jnp.einsum('bhqk,bkhd->bqhd', pr, v)

    o = lax.map(one_block, (qb, starts))
    return o.transpose(1, 0, 2, 3, 4).reshape(b, l, h, dv)

def ssd_mixer(z, xbc, dt_raw, conv_w, conv_b, dt_bias, a_log, d_skip, norm_g):
    b, l, _ = z.shape
    xbc = jax.nn.silu(causal_depthwise_conv(xbc, conv_w, conv_b))
    xs, bm, cm = jnp.split(xbc, [SSD_INNER, SSD_INNER + SSD_GROUPS * SSD_STATE], axis=-1)
    xs = xs.reshape(b, l, SSD_HEADS, SSD_HEAD_DIM)
    rep = SSD_HEADS // SSD_GROUPS
    bm = jnp.repeat(bm.reshape(b, l, SSD_GROUPS, SSD_STATE), rep, axis=2)
    cm = jnp.repeat(cm.reshape(b, l, SSD_GROUPS, SSD_STATE), rep, axis=2)
    dt = jax.nn.softplus(dt_raw.astype(jnp.float32) + dt_bias.astype(jnp.float32))
    a = -jnp.exp(a_log.astype(jnp.float32))
    y = scalar_decay_chunked(cm, bm, xs * dt[..., None].astype(xs.dtype), dt * a, SSD_CHUNK)
    y = y + d_skip[:, None] * xs
    y = y.reshape(b, l, SSD_INNER) * jax.nn.silu(z)
    y = rms_norm(y.reshape(b, l, SSD_GROUPS, SSD_INNER // SSD_GROUPS),
                 norm_g.reshape(SSD_GROUPS, SSD_INNER // SSD_GROUPS))
    return y.reshape(b, l, SSD_INNER)

def retention_mixer(q, k, v, g, positions, norm_g):
    b, l, _ = q.shape
    q = rope(q.reshape(b, l, RET_HEADS, RET_QK_DIM), positions)
    k = rope(k.reshape(b, l, RET_HEADS, RET_QK_DIM), positions) * (RET_QK_DIM ** -0.5)
    v = v.reshape(b, l, RET_HEADS, RET_V_DIM)
    log_gamma = jnp.log1p(-jnp.exp2(-5.0 - jnp.arange(RET_HEADS, dtype=jnp.float32)))
    log_g = jnp.broadcast_to(log_gamma, (b, l, RET_HEADS))
    y = scalar_decay_chunked(q, k, v, log_g, RET_CHUNK)
    y = rms_norm(y, norm_g.reshape(RET_HEADS, RET_V_DIM)).reshape(b, l, RET_HEADS * RET_V_DIM)
    return y * jax.nn.silu(g)

def mla_mixer(c_q, c_kv, k_rope, positions, q_norm, w_uq, kv_norm, w_ukv):
    b, l, _ = c_q.shape
    q = (rms_norm(c_q, q_norm) @ w_uq).reshape(b, l, MLA_HEADS, MLA_NOPE + MLA_ROPE)
    q_nope, q_pe = q[..., :MLA_NOPE], rope(q[..., MLA_NOPE:], positions)
    kv = (rms_norm(c_kv, kv_norm) @ w_ukv).reshape(b, l, MLA_HEADS, MLA_NOPE + MLA_V)
    k_nope, v = kv[..., :MLA_NOPE], kv[..., MLA_NOPE:]
    k_pe = rope(k_rope[:, :, None, :], positions)
    q = jnp.concatenate([q_nope, q_pe], axis=-1)
    k = jnp.concatenate([k_nope, jnp.broadcast_to(k_pe, (b, l, MLA_HEADS, MLA_ROPE))], axis=-1)
    o = causal_attention_blocked(q, k, v, (MLA_NOPE + MLA_ROPE) ** -0.5)
    return o.reshape(b, l, MLA_HEADS * MLA_V)

def gla_mixer(q, k, v, gk_low, g, w_gk2, b_gk, norm_g):
    b, l, _ = q.shape
    q = q.reshape(b, l, GLA_HEADS, GLA_K_DIM) * (GLA_K_DIM ** -0.5)
    k = k.reshape(b, l, GLA_HEADS, GLA_K_DIM)
    v = v.reshape(b, l, GLA_HEADS, GLA_V_DIM)
    log_g = jax.nn.log_sigmoid((gk_low @ w_gk2 + b_gk).astype(jnp.float32)) / GLA_GATE_NORM
    o = gla_chunked(q, k, v, log_g.reshape(b, l, GLA_HEADS, GLA_K_DIM), GLA_CHUNK)
    o = rms_norm(o, norm_g.reshape(GLA_HEADS, GLA_V_DIM)).reshape(b, l, GLA_HEADS * GLA_V_DIM)
    return o * jax.nn.silu(g)

def hybrid_layer(x, positions, w_in, b_gate, ssd_conv_w, ssd_conv_b, ssd_dt_bias, ssd_a_log, ssd_d,
                 ssd_norm, ret_norm, mla_q_norm, mla_w_uq, mla_kv_norm, mla_w_ukv, gla_w_gk2, gla_b_gk,
                 gla_norm, w_branch, w_out, norm_pre_mix, norm_post_mix, norm_pre_mlp, norm_post_mlp,
                 w_mlp_in, w_mlp_out):
    b, l, _ = x.shape
    h = rms_norm(x, norm_pre_mix)
    sizes = (SSD_INNER, SSD_XBC, SSD_HEADS,
             RET_HEADS * RET_QK_DIM, RET_HEADS * RET_QK_DIM, RET_HEADS * RET_V_DIM, RET_HEADS * RET_V_DIM,
             MLA_Q_LORA, MLA_KV_LORA, MLA_ROPE,
             GLA_HEADS * GLA_K_DIM, GLA_HEADS * GLA_K_DIM, GLA_HEADS * GLA_V_DIM, GLA_GATE_RANK,
             GLA_HEADS * GLA_V_DIM, N_BRANCHES * D_MODEL)
    idx = [int(s) for s in np.cumsum(sizes)[:-1]]
    (z, xbc, dt_raw, rq, rk, rv, rg, cq, ckv, kr,
     gq, gk, gv, ggk, gg, gate_logits) = jnp.split(h @ w_in, idx, axis=-1)

    y_ssd = ssd_mixer(z, xbc, dt_raw, ssd_conv_w, ssd_conv_b, ssd_dt_bias, ssd_a_log, ssd_d, ssd_norm)
    y_ret = retention_mixer(rq, rk, rv, rg, positions, ret_norm)
    y_mla = mla_mixer(cq, ckv, kr, positions, mla_q_norm, mla_w_uq, mla_kv_norm, mla_w_ukv)
    y_gla = gla_mixer(gq, gk, gv, ggk, gg, gla_w_gk2, gla_b_gk, gla_norm)

    ys = jnp.stack([y_ssd, y_ret, y_mla, y_gla], axis=2)
    branches = jnp.einsum('blnw,nwd->blnd', ys, w_branch)
    gates = jax.nn.sigmoid((gate_logits + b_gate).astype(jnp.float32)).astype(x.dtype)
    merged = jnp.sum(gates.reshape(b, l, N_BRANCHES, D_MODEL) * branches, axis=2)
    x = x + rms_norm(merged @ w_out, norm_post_mix)

    u = jnp.square(jax.nn.relu(rms_norm(x, norm_pre_mlp) @ w_mlp_in))
    return x + rms_norm(u @ w_mlp_out, norm_post_mlp)

def setup_inputs(seed: int = 0) -> dict:
    key = jax.random.key(seed)
    ks = jax.random.split(key, 32)
    f32 = jnp.float32
    L = DEPTH

    def nrm(k, shape, scale):
        return jax.random.normal(k, shape, f32) * scale

    def gain(k, shape):
        return 1.0 + 0.02 * jax.random.normal(k, shape, f32)

    x = nrm(ks[0], (BATCH, SEQ, D_MODEL), 1.0)
    offsets = jax.random.randint(ks[1], (BATCH, 1), 0, MAX_POS_OFFSET, dtype=jnp.int32)
    positions = offsets + jnp.arange(SEQ, dtype=jnp.int32)[None, :]
    dt = jnp.exp(jax.random.uniform(ks[2], (L, SSD_HEADS), f32) * (np.log(0.1) - np.log(0.001))
                 + np.log(0.001))
    ssd_dt_bias = dt + jnp.log(-jnp.expm1(-dt))
    ssd_a_log = jnp.log(jax.random.uniform(ks[3], (L, SSD_HEADS), f32, minval=1.0, maxval=16.0))
    return {
        "x": x,
        "positions": positions,
        "w_in": nrm(ks[4], (L, D_MODEL, IN_WIDTH), D_MODEL ** -0.5),
        "b_gate": nrm(ks[5], (L, N_BRANCHES * D_MODEL), 0.01),
        "ssd_conv_w": nrm(ks[6], (L, SSD_CONV, SSD_XBC), SSD_CONV ** -0.5),
        "ssd_conv_b": nrm(ks[7], (L, SSD_XBC), 0.01),
        "ssd_dt_bias": ssd_dt_bias,
        "ssd_a_log": ssd_a_log,
        "ssd_d": 1.0 + 0.1 * jax.random.normal(ks[8], (L, SSD_HEADS), f32),
        "ssd_norm": gain(ks[9], (L, SSD_INNER)),
        "ret_norm": gain(ks[10], (L, RET_HEADS * RET_V_DIM)),
        "mla_q_norm": gain(ks[11], (L, MLA_Q_LORA)),
        "mla_w_uq": nrm(ks[12], (L, MLA_Q_LORA, MLA_HEADS * (MLA_NOPE + MLA_ROPE)), MLA_Q_LORA ** -0.5),
        "mla_kv_norm": gain(ks[13], (L, MLA_KV_LORA)),
        "mla_w_ukv": nrm(ks[14], (L, MLA_KV_LORA, MLA_HEADS * (MLA_NOPE + MLA_V)), MLA_KV_LORA ** -0.5),
        "gla_w_gk2": nrm(ks[15], (L, GLA_GATE_RANK, GLA_HEADS * GLA_K_DIM), GLA_GATE_RANK ** -0.5),
        "gla_b_gk": nrm(ks[16], (L, GLA_HEADS * GLA_K_DIM), 0.01),
        "gla_norm": gain(ks[17], (L, GLA_HEADS * GLA_V_DIM)),
        "w_branch": nrm(ks[18], (L, N_BRANCHES, BRANCH_WIDTH, D_MODEL), BRANCH_WIDTH ** -0.5),
        "w_out": nrm(ks[19], (L, D_MODEL, D_MODEL), D_MODEL ** -0.5),
        "norm_pre_mix": gain(ks[20], (L, D_MODEL)),
        "norm_post_mix": gain(ks[21], (L, D_MODEL)),
        "norm_pre_mlp": gain(ks[22], (L, D_MODEL)),
        "norm_post_mlp": gain(ks[23], (L, D_MODEL)),
        "w_mlp_in": nrm(ks[24], (L, D_MODEL, D_FF), D_MODEL ** -0.5),
        "w_mlp_out": nrm(ks[25], (L, D_FF, D_MODEL), D_FF ** -0.5),
    }

def reference(x, positions, w_in, b_gate, ssd_conv_w, ssd_conv_b, ssd_dt_bias, ssd_a_log, ssd_d,
              ssd_norm, ret_norm, mla_q_norm, mla_w_uq, mla_kv_norm, mla_w_ukv, gla_w_gk2, gla_b_gk,
              gla_norm, w_branch, w_out, norm_pre_mix, norm_post_mix, norm_pre_mlp, norm_post_mlp,
              w_mlp_in, w_mlp_out):
    for i in range(DEPTH):
        x = hybrid_layer(x, positions, w_in[i], b_gate[i], ssd_conv_w[i], ssd_conv_b[i], ssd_dt_bias[i],
                         ssd_a_log[i], ssd_d[i], ssd_norm[i], ret_norm[i], mla_q_norm[i], mla_w_uq[i],
                         mla_kv_norm[i], mla_w_ukv[i], gla_w_gk2[i], gla_b_gk[i], gla_norm[i], w_branch[i],
                         w_out[i], norm_pre_mix[i], norm_post_mix[i], norm_pre_mlp[i], norm_post_mlp[i],
                         w_mlp_in[i], w_mlp_out[i])
    return x


_drawn_inputs = setup_inputs


def setup_inputs(seed=0):
    import zlib

    import numpy as np

    out = dict(_drawn_inputs(seed))
    spreads = {}
    factors = {'b_gate': 8.0,
     'ssd_conv_b': 4.624,
     'ssd_norm': 3.572,
     'ret_norm': 6.071,
     'mla_q_norm': 8.0,
     'mla_kv_norm': 8.0,
     'gla_b_gk': 8.0,
     'gla_norm': 5.97,
     'norm_pre_mlp': 2.873,
     'norm_post_mlp': 3.223}
    for name, (base, spread) in spreads.items():
        noise = np.random.default_rng([zlib.crc32(name.encode()), seed]).standard_normal(out[name].shape)
        drawn = base * np.exp(spread * noise) if base else spread * noise
        out[name] = __import__('jax').numpy.asarray(drawn.astype(out[name].dtype))
    for name, factor in factors.items():
        out[name] = (out[name] * factor).astype(out[name].dtype)
    return out
```

```python
from contextlib import ExitStack

import numpy as np
import concourse.bass as bass
from concourse import mybir

F32 = mybir.dt.float32
F32R = mybir.dt.float32r
I32 = mybir.dt.int32
ALU = mybir.AluOpType
ACT = mybir.ActivationFunctionType
X_AXIS = mybir.AxisListType.X

P = 128
DEPTH, SEQ, D = 2, 256, 1024
T = SEQ // P
KT = D // P
EPS = 1e-6
PI = 3.1415925

WIDTHS = dict(z=512, xbc=1024, dt=8, rqk=512, rv=512, rg=512, cq=256, ckv=128, kr=32,
              gqk=512, gv=512, ggk=16, gg=512, gates=4 * D)
COL = {}
for _name, _w in WIDTHS.items():
    COL[_name] = sum(WIDTHS[k] for k in list(WIDTHS)[:list(WIDTHS).index(_name)])
IN_WIDTH = sum(WIDTHS.values())
BRANCHES = ("ssd", "ret", "mla", "gla")
FF = 4 * D
ROPE = 32
LN_EXP = "natural_log_exp_and_others"

C_PARTS = ("cq", "ckv", "kr", "dt", "ggk")
C_AT = {n: sum(WIDTHS[k] for k in C_PARTS[:i]) for i, n in enumerate(C_PARTS)}
C_WIDTH = sum(WIDTHS[k] for k in C_PARTS)


def units():
    def rows(name):
        return [("token", name, i) for i in range(2)]

    def cols(name, n):
        return [("channel", name, i) for i in range(n)]

    def gates(b):
        return [("gate", b, i) for i in range(4)]

    def branch(b):
        return [("branch", b, i) for i in range(2)]

    u = rows("c") + cols("xbc", 4) + rows("z") + rows("rqk") + gates("mla") + rows("rv") + rows("rg")
    u += branch("mla") + gates("ssd") + cols("gqk", 2) + rows("gv") + rows("gg") + branch("ssd")
    u += gates("ret") + branch("ret") + gates("gla") + branch("gla")
    u += [("out", "out", i) for i in range(4)]
    for j in range(17):
        u += [("up", "up", j)] if j < 16 else []
        u += [("down", "down", j - 1)] if j >= 1 else []
    return u


UNITS = units()
NU = len(UNITS)
AT = {(k, n, i): p for p, (k, n, i) in enumerate(UNITS)}
RAW = 4
HL = 4
AHEAD = 2
IN_TWO = (("token", "z", 0), ("branch", "ssd", 0))
assert NU % RAW == 0 and 2 * NU % HL == 0

FILLS, FILL_ENDS = [], []
for _u, (_kind, _name, _i) in enumerate(UNITS):
    if _kind == "token" and _i == 1 or _kind in ("channel", "gate"):
        FILLS.append((_kind, _name, _i))
        FILL_ENDS.append(2 * _u + 1)
    if _kind == "branch":
        FILLS += [(_kind, _name, 2 * _i), (_kind, _name, 2 * _i + 1)]
        FILL_ENDS += [2 * _u, 2 * _u + 1]
NF = len(FILLS)
READ_BY_ACT = [f[0] != "branch" for f in FILLS]

SOFT = [(0, 0, 4), (0, 4, 4), (1, 0, 2), (1, 2, 2), (1, 4, 2), (1, 6, 2)]
NS = len(SOFT)

STEPS = {
    1: ["mla_norm"], 2: ["mla_turn"], 3: ["mla_q"], 4: ["mla_kv"], 5: ["mla_pe"],
    6: ["mla_a0"], 7: ["mla_a1"], 8: ["mla_a2", "conv0"], 9: ["mla_a3", "conv1"],
    10: ["mla_a4", "conv2"], 11: ["mla_a5", "conv3"], 12: ["mla_a6", "conv4"],
    13: ["mla_a7", "conv5"], 14: ["mla_y", "conv6", "ssd_dt"], 15: ["conv7", "ssd_cum"],
    16: ["ssd_gate"], 17: ["ret_rope"],
    18: ["ssd_turn"], 19: ["ssd_decay0"], 20: ["ssd_decay1", "ssd_state"],
    21: ["ssd_y0"], 22: ["ssd_decay2"], 23: ["ssd_decay3"], 24: ["ssd_y1", "ret_gate"],
    25: ["ssd_norm", "gla_low", "ret_turn"], 26: ["gla_decay", "ret_s0"], 27: ["ssd_y", "ret_s1"],
    28: ["ret_y0", "gla_scale"], 29: ["ret_y1", "gla_turn"], 30: ["ret_norm", "gla_s0"],
    31: ["gla_s1"], 32: ["ret_y", "gla_state"],
    33: ["gla_o0"], 34: ["gla_o1"], 35: ["gla_gate"], 36: ["gla_norm"], 38: ["gla_y"],
    41: ["last_gate"],
}
JOBS_OF = {
    "mla_turn": ["cq", "ckv"], "mla_q": ["qpe", "qn0", "qn1", "qn2", "qn3"],
    "mla_kv": ["kn0", "kn1", "kn2", "kn3", "v0", "v1"], "mla_pe": ["qpeT"],
    "mla_y": ["mla_y0", "mla_y1"],
    "ssd_cum": ["cum"], "ssd_turn": ["G", "xs0", "xs1", "B"],
    "ssd_decay0": ["R0"], "ssd_decay1": ["R1"], "ssd_decay2": ["R2"], "ssd_decay3": ["R3"],
    "ssd_state": ["S"], "ssd_y0": ["Y0"], "ssd_y1": ["off", "Y1"], "ssd_y": ["ssd_y0", "ssd_y1"],
    "ret_turn": ["rq", "rk"], "ret_s0": ["rs0", "rS"], "ret_s1": ["rs1"], "ret_y0": ["rY0"],
    "ret_y1": ["rY1"], "ret_y": ["ret_y0", "ret_y1"],
    "gla_low": ["low"], "gla_decay": ["gate"], "gla_turn": ["kst"], "gla_s0": ["gs0"],
    "gla_s1": ["gs1"], "gla_state": ["gS0", "gS1", "gS2"], "gla_o0": ["gY0"], "gla_o1": ["gY1"],
    "gla_y": ["gla_y0", "gla_y1"],
}
for _i in range(NS + 2):
    JOBS_OF[f"mla_a{_i}"] = ([f"score{_i}"] if _i < NS else []) \
        + ([f"turn{_i - 1}"] if 1 <= _i <= NS else []) + ([f"pv{_i - 2}"] if _i >= 2 else [])
JOBS = [f"h{i}" for i in range(4)]
for _u in range(NU):
    for _s in STEPS.get(_u, []):
        JOBS += JOBS_OF.get(_s, [])
JOBS += [f"u{i}" for i in range(4)]
NJ = len(JOBS)
JOB = {n: i for i, n in enumerate(JOBS)}
TURNED = [j for j in JOBS if j[0] == "h" and len(j) == 2 or j[0] == "u" and len(j) == 2
          or j[:5] in ("ssd_y", "ret_y", "mla_y", "gla_y")]

CHAN = {}
_at = 0
for _n, _w in (("pre_mix", 8), ("pre_mlp", 8), ("conv_w", 32), ("conv_b", 8), ("b_gate", 32),
               ("gla_b", 2), ("q_norm", 2), ("kv_norm", 1), ("ssd", 4), ("ret", 4), ("gla", 4)):
    CHAN[_n] = _at
    _at += _w
N_CHAN = _at
CONST = {}
_at = 0
for _n, _w in (("ident", P), ("causal", P), ("block", P), ("neg", 2 * P), ("restart", SEQ),
               ("freq", ROPE), ("ret_scale", 8), ("ret_total", 2), ("eps", 1), ("one", 1)):
    CONST[_n] = _at
    _at += _w
N_CONST = _at


def constants():
    c = np.zeros((P, N_CONST), np.float64)

    def put(name, a):
        c[:, CONST[name]:CONST[name] + a.shape[1]] = a

    i = np.arange(P)
    put("ident", np.eye(P))
    put("causal", (i[:, None] <= i[None, :]) * 1.0)
    put("block", ((i[:, None] <= i[None, :]) & (i[:, None] // 64 == i[None, :] // 64)) * 1.0)
    put("neg", np.concatenate([np.zeros((P, P)), (i[None, :] > i[:, None]) * -1e30], 1))
    put("restart", np.tile((np.arange(SEQ) % 64 != 0) * 1.0, (P, 1)))
    put("freq", np.tile(10000.0 ** (-np.arange(ROPE) / ROPE), (P, 1)))
    log_gamma = np.log1p(-np.exp2(-5.0 - np.arange(4)))
    cum = (i[:, None] + 1) * log_gamma[None, :]
    put("ret_scale", np.concatenate([np.exp(cum), np.exp(-cum) * 64 ** -0.5], 1))
    put("ret_total", np.exp(P * log_gamma)[2 * np.arange(2)[None, :] + (i[:, None] // 64)])
    put("eps", np.full((P, 1), EPS))
    put("one", np.ones((P, 1)))
    return c.astype(np.float32)


class Signal:

    def __init__(self, semaphore, events, start=0):
        self.sem, self.start, self.per = semaphore, start, len(events)
        self.order = list(events)
        self.number = {e: i + 1 for i, e in enumerate(events)}
        self.marked = 0

    def inc(self, event):
        assert self.order[self.marked] == event, (self.order[self.marked], event)
        self.marked += 1
        return 1

    def at(self, layer, event):
        return layer * self.per + (self.start + self.number[event])

    def at_number(self, layer, number):
        return layer * self.per + (self.start + number)


class Chain:

    def __init__(self, semaphore, per):
        self.sem, self.per, self.n = semaphore, per, 0

    def bind(self, layer):
        self.layer = layer

    def next(self):
        self.n += 1
        return self.layer * self.per + self.n


ACT_LINKS = 18
DVE_LINKS = 82
PE_LINKS = 7
V_EVENTS = """
h_normed pad c_scaled k_rot q_rot shifted0 shifted1 shifted2 conv0 shifted3 conv1 shifted4 conv2
shifted5 conv3 conv4 conv5 conv6 dt_x conv7 dt_w log_decay cum r_scaled xdt x_end mla_merged seg0
weights0 seg1 weights1 seg2 weights2 seg3 weights3 ssd_summed ssd_squared ssd_out gate_n g_cum k_end
qk_in gS_zero ret_squared ret_out ssd_merged gla_squared gla_out ret_merged x_mixed u_normed
""".split()
A_EVENTS = """
h_r mla_r exp0 exp1 exp2 tap0 exp3 tap1 exp4 tap2 exp5 tap3 tap4 tap5 tap6 dt_u tap7 dt_ln
conv_sigmoid z_sigmoid mla_gates ends decay0 decay1 decay2 decay3 rg_sigmoid ssd_gates ssd_r gate_ln
g_exps ret_r gg_sigmoid ret_gates gla_r gla_gates mix_r u_r mlp_r
""".split()
G_EVENTS = """
conv_silu z_silu rg_silu ssd_gated gg_silu
""".split()


def hybrid_trunk(nc, x, positions, w_in, w_branch, w_out, w_up, w_down, w_uq, w_ukv, w_gk2,
                 chan_in, rows_in, const_in, out):
    with ExitStack() as ctx:
        def sb(name, shape, dt=F32):
            return ctx.enter_context(nc.sbuf_tensor(name, shape, dt))

        def sem(name):
            return ctx.enter_context(nc.semaphore(name))

        raw = sb("raw", [P, RAW, 2048])
        w_hi = sb("w_hi", [P, HL, 1024], F32R)
        w_lo = sb("w_lo", [P, HL, 1024], F32R)
        xs_res = sb("x_res", [P, T, D])
        a_hi = sb("a_hi", [P, KT, SEQ], F32R)
        a_lo = sb("a_lo", [P, KT, SEQ], F32R)
        merged = sb("merged", [P, KT, SEQ])
        gates = sb("gates", [P, 8, SEQ])
        y_hi = sb("y_hi", [P, 4, SEQ], F32R)
        y_lo = sb("y_lo", [P, 4, SEQ], F32R)
        post_gain = sb("post_gain", [P, D])
        head_rows = sb("head_rows", [P, 24])
        chan = sb("chan", [P, N_CHAN])
        ukv = sb("ukv", [P, D])
        gk2 = sb("gk2", [16, 256])
        const = sb("const", [P, N_CONST])
        trig = sb("trig", [P, 2, T, ROPE])
        c = sb("c", [P, T, C_WIDTH])
        rqk = sb("rqk", [P, T, 512])
        stat = sb("stat", [P, 64])
        pos_i = sb("pos_i", [P, T], I32)
        R1 = sb("region_1", [P, 8256])
        R2 = sb("region_2", [P, 10300])
        uq = gates[:, 0:6, :].rearrange("p a b -> p (a b)").rearrange("p (k n) -> p k n", k=2)

        def part(region, at, *dims):
            n = int(np.prod(dims))
            v = region[:, at:at + n]
            if len(dims) == 2:
                v = v.rearrange("p (a b) -> p a b", a=dims[0])
            if len(dims) == 3:
                v = v.rearrange("p (a b c) -> p a b c", a=dims[0], b=dims[1])
            return v

        normed = part(R1, 0, T, D)
        update = part(R1, 0, T, D)
        square_out = part(R2, 0, T, D)
        c_square_out = part(R2, 2072, T, 512)
        qT = part(R1, 0, 8, SEQ)
        kT = part(R1, 2048, 8, SEQ)
        v_mla = part(R1, 4096, T, 512)
        o_mla = part(R1, 5120, T, 512)
        soft = part(R1, 6144, 2, 512)
        q_pe = part(R1, 6144, T, 256)
        q_rot = part(R1, 6656, T, 256)
        probT = part(R1, 7168, 2, 512)
        cT = part(R1, 7168, 3, SEQ)
        k_rot = part(R1, 7936, T, 32)
        rot_a = part(R1, 4096, 512)
        rot_b = part(R1, 4608, 512)
        rv = part(R1, 0, T, 512)
        rg = part(R1, 1024, T, 512)
        rg_s = part(R1, 2048, T, 512)
        rr = part(R1, 3072, T, 512)
        rT = part(R1, 4096, 4, SEQ)
        rS = part(R1, 5120, T, 512)
        r_rot_a = part(R1, 5120, 512)
        r_rot_b = part(R1, 5632, 512)
        ry = part(R1, 6144, T, 512)
        r_state = part(R1, 7168, 2, P)
        xbc = part(R2, 0, 8, SEQ + 3)
        xbc_s = part(R2, 0, 8, SEQ)
        xs = part(R2, 0, T, 512)
        xdt = part(R2, 1024, T, 512)
        conv = part(R2, 2072, 8, SEQ)
        z = part(R2, 4120, T, 512)
        B_tok = part(R2, 5144, 2, P)
        x_end = part(R2, 5400, 512)
        L = part(R2, 5912, 8, P)
        z_s = part(R2, 5912, T, 512)
        s_state = part(R2, 6936, 512)
        sy = part(R2, 7448, T, 512)
        G = part(R2, 8472, 4, P)
        s_tmp = part(R2, 8984, 512)
        cum_keep = part(R2, 9496, 16)
        log_decay = part(R2, 9512, 16)
        w1 = part(R2, 9528, 16)
        gqk = part(R2, 0, 4, SEQ)
        gv = part(R2, 1024, T, 512)
        gg = part(R2, 2072, T, 512)
        gg_s = part(R2, 3096, T, 512)
        k_tok = part(R2, 4120, T, 256)
        g_cum = part(R2, 5144, 2, SEQ)
        g_e = part(R2, 5656, 2, SEQ)
        g_ei = part(R2, 6168, 2, SEQ)
        g_end = part(R2, 6680, 2, SEQ)
        gS = part(R2, 7448, T, 512)
        gy = part(R2, 8472, T, 512)
        g_state = part(R2, 9496, 3, 2, P)
        g_low = R2[0:16, 9496:9752]
        relu = part(R2, 0, 2, 512)
        relu2 = part(R2, 1024, 2, 512)

        def cst(name, n):
            return const[:, CONST[name]:CONST[name] + n]

        ident, causal = cst("ident", P), cst("causal", P)

        proj = ctx.enter_context(nc.psum_tensor("proj", [P, 4, 512], F32))
        mix = ctx.enter_context(nc.psum_tensor("mix", [P, 4, 512], F32))

        def bank(job):
            return mix[:, JOB[job] % 4, :]

        def chan_col(name, i, n=1):
            return chan[:, CHAN[name] + i:CHAN[name] + i + n]

        landed = [sem(f"weights_landed_{i}") for i in range(RAW)]
        s_input = sem("inputs_landed")
        s_param = sem("parameters_landed")
        s_gain2 = sem("mlp_gain_landed")
        s_stored = sem("output_stored")
        halves = [f"half{i}" for i in range(2 * NU)]
        hi_made = Signal(sem("hi_made"), halves)
        lo_even = Signal(sem("lo_even_made"), [f"unit{i}" for i in range(NU)], start=RAW)
        lo_odd = Signal(sem("lo_odd_made"), [f"unit{i}" for i in range(NU)], start=RAW)
        half_done = Signal(sem("half_done"), halves, start=HL)
        read_act = Signal(sem("projection_read_by_act"), [f"fill{i}" for i in range(NF) if READ_BY_ACT[i]])
        read_dve = Signal(sem("projection_read_by_dve"), [f"fill{i}" for i in range(NF) if not READ_BY_ACT[i]])
        job_full = Signal(sem("mix_job_full"), JOBS)
        job_read = Signal(sem("mix_job_read"), JOBS)
        turned_hi = Signal(sem("turned_hi"), TURNED)
        x_done = Signal(sem("x_done"), ["x"], start=1)
        up_read = Signal(sem("up_read"), [f"up{i}" for i in range(16)])
        up_hi = Signal(sem("up_hi"), [f"up{i}" for i in range(16)])
        up_lo = Signal(sem("up_lo"), [f"up{i}" for i in range(16)])
        merge_hi = Signal(sem("merge_hi"), [f"m{i}" for i in range(4)])
        merge_lo = Signal(sem("merge_lo"), [f"m{i}" for i in range(4)])
        merge_sum = Signal(sem("merge_summed"), [f"m{i}" for i in range(4)])
        dve_ready = Signal(sem("dve_ready"), V_EVENTS)
        act_ready = Signal(sem("act_ready"), A_EVENTS)
        pool_ready = Signal(sem("pool_ready"), G_EVENTS)
        act_link = Chain(sem("act_link"), ACT_LINKS)
        dve_link = Chain(sem("dve_link"), DVE_LINKS)
        pe_link = Chain(sem("pe_link"), PE_LINKS)
        s_rope = sem("rope_tables")
        s_rope_act = sem("rope_sines")
        s_pre = sem("rope_steps")
        n_params = 6

        block = ctx.enter_context(nc.Block())

        def unit_parts(u, layer):
            kind, name, i = UNITS[u]
            slot = raw[:, u % RAW, :]
            lay = bass.ds(layer, 1)
            if kind == "token" and name == "c":
                dst = slot[:, 0:4 * C_WIDTH].rearrange("p (k n) -> p k n", k=4)
                got = []
                for first, last in (("cq", "kr"), ("dt", "dt"), ("ggk", "ggk")):
                    a, w = C_AT[first], C_AT[last] + WIDTHS[last] - C_AT[first]
                    src = w_in[lay, 512 * i:512 * i + 512, COL[first]:COL[first] + w]
                    got.append((dst[:, :, a:a + w], src.rearrange("o (k p) n -> p (o k) n", p=P)))
                return got
            if kind == "token":
                src = w_in[lay, 512 * i:512 * i + 512, COL[name]:COL[name] + 512]
                k, n = 4, 512
            elif kind in ("channel", "gate"):
                at = COL[name] if kind == "channel" else COL["gates"] + BRANCHES.index(name) * D
                src = w_in[lay, :, at + 256 * i:at + 256 * i + 256]
                k, n = 8, 256
            elif kind == "branch":
                at = 512 * BRANCHES.index(name)
                src = w_branch[lay, at:at + 512, 512 * i:512 * i + 512]
                k, n = 4, 512
            elif kind == "up":
                src = w_up[lay, :, 256 * i:256 * i + 256]
                k, n = 8, 256
            else:
                src = (w_out if kind == "out" else w_down)[lay, 256 * i:256 * i + 256, :]
                k, n = 2, D
            dst = slot[:, 0:k * n].rearrange("p (k n) -> p k n", k=k)
            src = src.rearrange("o (k p) n -> p (o k) n", p=P)
            if (kind, name, i) in IN_TWO:
                return [(dst[:, 1:k], src[:, 1:k]), (dst[:, 0:1], src[:, 0:1])]
            return [(dst, src)]

        def n_dmas(u):
            return 3 if UNITS[u][:2] == ("token", "c") else 2 if UNITS[u] in IN_TWO else 1

        def landed_count(u):
            return 16 * sum(n_dmas(v) for v in range(u % RAW, u + 1, RAW))

        def half_views(u, half):
            kind, name, i = UNITS[u]
            if kind == "token":
                k, n = 4, C_WIDTH if name == "c" else 512
            elif kind == "branch":
                k, n = 4, 512
            elif kind in ("out", "down"):
                k, n = 2, D
            else:
                k, n = 8, 256
            src = raw[:, u % RAW, 0:k * n].rearrange("p (k n) -> p k n", k=k)
            if kind == "branch":
                src, n = src[:, :, 256 * half:256 * half + 256], 256
            else:
                k //= 2
                src = src[:, k * half:k * half + k, :]
            s = (2 * u + half) % HL
            hi, lo = (w[:, s, 0:k * n].rearrange("p (k n) -> p k n", k=k) for w in (w_hi, w_lo))
            return src, hi, lo

        def wait_for_products(engine, layer, kind, name, i, half=1):
            engine.wait_ge(half_done.sem, half_done.at(layer, f"half{2 * AT[(kind, name, i)] + half}"))

        def wait_for_read(engine, layer, f):
            if READ_BY_ACT[f]:
                engine.wait_ge(read_act.sem, read_act.at(layer, f"fill{f}"))
            else:
                engine.wait_ge(read_dve.sem, read_dve.at(layer, f"fill{f}"))

        fills_of = {}
        for f, (kind, name, i) in enumerate(FILLS):
            u = AT[(kind, name, i // 2 if kind == "branch" else i)]
            fills_of.setdefault(u, []).append(f)

        @block.sync
        def _(sp):
            sp.dma_start(xs_res[:], x.rearrange("o (t p) d -> p (o t) d", p=P)).then_inc(s_input, 16)
            sp.dma_start(const[:], const_in).then_inc(s_input, 16)
            sp.dma_start(pos_i[:], positions).then_inc(s_input, 16)
            with sp.Fori(0, DEPTH) as layer:
                for u in range(NU):
                    sp.wait_ge(lo_odd.sem, lo_odd.at_number(layer, u + 1 - RAW))
                    for dst, src in unit_parts(u, layer):
                        sp.dma_start(dst, src).then_inc(landed[u % RAW], 16)
            sp.wait_ge(x_done.sem, x_done.at(DEPTH - 1, "x"))
            sp.dma_start(out.rearrange("o (t p) d -> p (o t) d", p=P), xs_res[:]).then_inc(s_stored, 16)
            sp.wait_ge(s_stored, 16)

        @block.gpsimd
        def _(pool):
            def lo_half(layer, u):
                src, hi, lo = half_views(u, 1)
                pool.wait_ge(hi_made.sem, hi_made.at(layer, f"half{2 * u + 1}"))
                pool.wait_ge(lo_even.sem, lo_even.at(layer, f"unit{u}"))
                nc.gpsimd.tensor_tensor(lo, src, hi.bitcast(F32), ALU.subtract).then_inc(lo_odd.sem, lo_odd.inc(f"unit{u}"))

            def step(name, layer):
                if name == "ssd_gate":
                    pool.wait_ge(act_ready.sem, act_ready.at(layer, "conv_sigmoid"))
                    pool.wait_ge(dve_ready.sem, dve_ready.at(layer, "conv7"))
                    nc.gpsimd.tensor_tensor(conv, conv, xbc_s, ALU.mult).then_inc(pool_ready.sem, pool_ready.inc("conv_silu"))
                    pool.wait_ge(act_ready.sem, act_ready.at(layer, "z_sigmoid"))
                    nc.gpsimd.tensor_tensor(z, z, z_s, ALU.mult).then_inc(pool_ready.sem, pool_ready.inc("z_silu"))
                if name == "ssd_norm":
                    pool.wait_ge(dve_ready.sem, dve_ready.at(layer, "ssd_summed"))
                    pool.wait_ge(pool_ready.sem, pool_ready.at(layer, "z_silu"))
                    nc.gpsimd.tensor_tensor(sy, sy, z, ALU.mult).then_inc(pool_ready.sem, pool_ready.inc("ssd_gated"))
                if name == "ret_gate":
                    pool.wait_ge(act_ready.sem, act_ready.at(layer, "rg_sigmoid"))
                    nc.gpsimd.tensor_tensor(rg, rg, rg_s, ALU.mult).then_inc(pool_ready.sem, pool_ready.inc("rg_silu"))
                if name == "gla_gate":
                    pool.wait_ge(act_ready.sem, act_ready.at(layer, "gg_sigmoid"))
                    nc.gpsimd.tensor_tensor(gg, gg, gg_s, ALU.mult).then_inc(pool_ready.sem, pool_ready.inc("gg_silu"))

            with pool.Fori(0, DEPTH) as layer:
                pool.wait_ge(x_done.sem, x_done.at_number(layer, 0))
                lay = bass.ds(layer, 1)
                pool.dma_start(chan[:], chan_in[lay].rearrange("o p n -> p (o n)")).then_inc(s_param, 16)
                pool.dma_start(uq, w_uq[lay].rearrange("o (k p) n -> p (o k) n", p=P)).then_inc(s_param, 16)
                pool.dma_start(ukv[:], w_ukv[lay].rearrange("o p n -> p (o n)")).then_inc(s_param, 16)
                pool.dma_start(gk2[:], w_gk2[lay].rearrange("o p n -> p (o n)")).then_inc(s_param, 16)
                pool.dma_start(post_gain[:], rows_in[lay, 0:D].partition_broadcast(P)
                               .rearrange("p o n -> p (o n)")).then_inc(s_param, 16)
                pool.dma_start(head_rows[:], rows_in[lay, 2 * D:2 * D + 24].partition_broadcast(P)
                               .rearrange("p o n -> p (o n)")).then_inc(s_param, 16)
                lo_half(layer, 0)
                for u in range(NU):
                    if u + 1 < NU:
                        lo_half(layer, u + 1)
                    for name in STEPS.get(u, []):
                        step(name, layer)
                    if u == AT[("up", "up", 2)]:
                        pool.wait_ge(dve_ready.sem, dve_ready.at(layer, "x_mixed"))
                        pool.dma_start(post_gain[:], rows_in[lay, D:2 * D].partition_broadcast(P)
                                       .rearrange("p o n -> p (o n)")).then_inc(s_gain2, 16)

        @block.scalar
        def _(act):
            def run(out_, in_, func=ACT.Copy, **kw):
                return nc.scalar.activation(out_, in_, func, **kw)

            def hi_half(layer, h):
                u, half = h // 2, h % 2
                src, hi, _ = half_views(u, half)
                total = landed_count(NU - RAW + u % RAW)
                if half == 0:
                    act.wait_ge(landed[u % RAW], layer * total + landed_count(u))
                act.wait_ge(half_done.sem, half_done.at_number(layer, h + 1 - HL))
                run(hi, src).then_inc(hi_made.sem, hi_made.inc(f"half{h}"))

            def turn_hi(layer, name, dst, gain):
                act.wait_ge(job_full.sem, job_full.at(layer, name))
                for i in range(2):
                    src = bank(name)[:, SEQ * i:SEQ * i + SEQ]
                    ins = run(dst[:, i, :], src, scale=gain[i]) if gain else run(dst[:, i, :], src)
                ins.then_inc(turned_hi.sem, turned_hi.inc(name))

            def rsqrt(dst, src, width):
                run(dst, src, ACT.Ln, scale=1.0 / width, bias=cst("eps", 1)).then_inc(act_link.sem, 1)
                act.wait_ge(act_link.sem, act_link.next())
                return run(dst, dst, ACT.Exp, scale=-0.5)

            def read(layer, f):
                kind, name, i = FILLS[f]
                act.wait_ge(half_done.sem, half_done.at(layer, f"half{FILL_ENDS[f]}"))
                pair = proj[:, 2 * (f % 2):2 * (f % 2) + 2, :]
                if kind == "token":
                    width = C_WIDTH if name == "c" else 512
                    dst = {"c": c[:], "z": z, "rqk": rqk[:], "rv": rv, "rg": rg, "gv": gv, "gg": gg}[name]
                    if name == "rv":
                        act.wait_ge(job_read.sem, job_read.at(layer, "mla_y1"))
                    if name == "gv":
                        act.wait_ge(dve_ready.sem, dve_ready.at(layer, "ssd_summed"))
                    run(dst, pair[:, :, 0:width]).then_inc(read_act.sem, read_act.inc(f"fill{f}"))
                elif kind == "channel":
                    dst = xbc[:, 2 * i:2 * i + 2, 3:SEQ + 3] if name == "xbc" else gqk[:, 2 * i:2 * i + 2, :]
                    if name == "gqk" and i == 0:
                        act.wait_ge(dve_ready.sem, dve_ready.at(layer, "ssd_summed"))
                    run(dst, pair[:, :, 0:SEQ]).then_inc(read_act.sem, read_act.inc(f"fill{f}"))
                else:
                    if name == "mla" and i == 0:
                        act.wait_ge(job_read.sem, job_read.at(layer, "qn3"))
                    elif i == 0:
                        before = {"ssd": "mla", "ret": "ssd", "gla": "ret"}[name]
                        act.wait_ge(dve_ready.sem, dve_ready.at(layer, f"{before}_merged"))
                    for m in range(2):
                        col = 8 * BRANCHES.index(name) + 2 * i + m
                        ins = run(gates[:, 2 * i + m, :], pair[:, m, 0:SEQ], ACT.Identity,
                                  bias=chan_col("b_gate", col))
                    ins.then_inc(read_act.sem, read_act.inc(f"fill{f}"))

            def gate_sigmoid(layer, b):
                act.wait_ge(read_act.sem, read_act.at(layer, f"fill{FILLS.index(('gate', b, 3))}"))
                run(gates[:], gates[:], ACT.Sigmoid).then_inc(act_ready.sem, act_ready.inc(f"{b}_gates"))

            def step(name, layer):
                if name == "mla_norm":
                    act.wait_ge(read_act.sem, read_act.at(layer, "fill0"))
                    for t in range(T):
                        run(c_square_out[:, t, 0:256], c[:, t, 0:256], ACT.Square, accum_out=stat[:, 4 + t:5 + t])
                        ins = run(c_square_out[:, t, 256:384], c[:, t, 256:384], ACT.Square,
                                  accum_out=stat[:, 6 + t:7 + t])
                    ins.then_inc(act_link.sem, 1)
                    act.wait_ge(act_link.sem, act_link.next())
                    run(stat[:, 4:6], stat[:, 4:6], ACT.Ln, scale=1.0 / 256, bias=cst("eps", 1)).then_inc(act_link.sem, 1)
                    act.wait_ge(act_link.sem, act_link.next())
                    run(stat[:, 6:8], stat[:, 6:8], ACT.Ln, scale=1.0 / 128, bias=cst("eps", 1)).then_inc(act_link.sem, 1)
                    act.wait_ge(act_link.sem, act_link.next())
                    run(stat[:, 4:8], stat[:, 4:8], ACT.Exp, scale=-0.5).then_inc(act_ready.sem, act_ready.inc("mla_r"))
                if name.startswith("mla_a") and int(name[5:]) < NS:
                    i = int(name[5:])
                    act.wait_ge(dve_ready.sem, dve_ready.at(layer, f"shifted{i}"))
                    run(soft[:, i % 2, :], soft[:, i % 2, :], ACT.Exp).then_inc(act_ready.sem, act_ready.inc(f"exp{i}"))
                if name == "mla_y":
                    for j in range(2):
                        turn_hi(layer, f"mla_y{j}", y_hi[:, 2 * j:2 * j + 2, :], None)
                if name.startswith("conv"):
                    m = int(name[4:])
                    act.wait_ge(dve_ready.sem, dve_ready.at(layer, "pad"))
                    act.wait_ge(read_act.sem, read_act.at(layer, f"fill{FILLS.index(('channel', 'xbc', m // 2))}"))
                    run(conv[:, m, :], xbc[:, m, 0:SEQ], ACT.Identity,
                               scale=chan_col("conv_w", m), bias=chan_col("conv_b", m)).then_inc(act_ready.sem, act_ready.inc(f"tap{m}"))
                if name == "ssd_dt":
                    act.wait_ge(dve_ready.sem, dve_ready.at(layer, "dt_x"))
                    run(stat[:, 24:40], stat[:, 24:40], ACT.Exp).then_inc(act_link.sem, 1)
                    act.wait_ge(act_link.sem, act_link.next())
                    run(stat[:, 0:8], head_rows[:, 8:16], ACT.Exp).then_inc(act_ready.sem, act_ready.inc("dt_u"))
                if name == "ssd_cum":
                    act.wait_ge(dve_ready.sem, dve_ready.at(layer, "dt_w"))
                    run(stat[:, 40:56], stat[:, 40:56], ACT.Ln).then_inc(act_ready.sem, act_ready.inc("dt_ln"))
                if name == "ssd_gate":
                    act.wait_ge(dve_ready.sem, dve_ready.at(layer, "conv7"))
                    run(xbc_s, conv, ACT.Sigmoid).then_inc(act_ready.sem, act_ready.inc("conv_sigmoid"))
                    act.wait_ge(read_act.sem, read_act.at(layer, f"fill{FILLS.index(('token', 'z', 1))}"))
                    run(z_s, z, ACT.Sigmoid).then_inc(act_ready.sem, act_ready.inc("z_sigmoid"))
                    gate_sigmoid(layer, "mla")
                if name == "ssd_turn":
                    act.wait_ge(dve_ready.sem, dve_ready.at(layer, "cum"))
                    run(stat[:, 40:56], stat[:, 40:56], ACT.Exp).then_inc(act_ready.sem, act_ready.inc("ends"))
                if name.startswith("ssd_decay"):
                    i = int(name[9:])
                    act.wait_ge(dve_ready.sem, dve_ready.at(layer, f"seg{i}"))
                    run(L[:, 4 * (i % 2):4 * (i % 2) + 4, :], L[:, 4 * (i % 2):4 * (i % 2) + 4, :],
                               ACT.Exp).then_inc(act_ready.sem, act_ready.inc(f"decay{i}"))
                if name == "ret_gate":
                    act.wait_ge(read_act.sem, read_act.at(layer, f"fill{FILLS.index(('token', 'rg', 1))}"))
                    run(rg_s, rg, ACT.Sigmoid).then_inc(act_ready.sem, act_ready.inc("rg_sigmoid"))
                    gate_sigmoid(layer, "ssd")
                if name == "gla_decay":
                    act.wait_ge(dve_ready.sem, dve_ready.at(layer, "gate_n"))
                    run(g_ei, g_ei, ACT.Exp).then_inc(act_link.sem, 1)
                    act.wait_ge(act_link.sem, act_link.next())
                    run(g_ei, g_ei, ACT.Ln, bias=cst("one", 1)).then_inc(act_ready.sem, act_ready.inc("gate_ln"))
                    act.wait_ge(dve_ready.sem, dve_ready.at(layer, "g_cum"))
                    run(g_e, g_cum, ACT.Exp, scale=1.0 / 16).then_inc(act_link.sem, 1)
                    act.wait_ge(act_link.sem, act_link.next())
                    run(g_ei, g_cum, ACT.Exp, scale=-1.0 / 16).then_inc(act_link.sem, 1)
                    act.wait_ge(act_link.sem, act_link.next())
                    run(g_end, g_end, ACT.Exp, scale=1.0 / 16).then_inc(act_ready.sem, act_ready.inc("g_exps"))
                if name in ("ssd_y", "ret_y", "gla_y"):
                    b = name[:3]
                    before = {"ssd": "mla", "ret": "ssd", "gla": "ret"}[b]
                    wait_for_products(act, layer, "branch", before, 1)
                    for j in range(2):
                        turn_hi(layer, f"{name}{j}", y_hi[:, 2 * j:2 * j + 2, :],
                                [chan_col(b, 2 * j + i) for i in range(2)])
                if name == "gla_gate":
                    act.wait_ge(read_act.sem, read_act.at(layer, f"fill{FILLS.index(('token', 'gg', 1))}"))
                    run(gg_s, gg, ACT.Sigmoid).then_inc(act_ready.sem, act_ready.inc("gg_sigmoid"))
                    gate_sigmoid(layer, "ret")
                if name == "last_gate":
                    gate_sigmoid(layer, "gla")

            def group_rsqrt(layer, b, n, width):
                act.wait_ge(dve_ready.sem, dve_ready.at(layer, f"{b}_squared"))
                rsqrt(stat[:, 8:8 + n], stat[:, 8:8 + n], width).then_inc(act_ready.sem, act_ready.inc(f"{b}_r"))

            act.wait_ge(s_rope, 1)
            run(trig[:, 0], trig[:, 0], ACT.Sin).then_inc(s_rope_act, 1)
            run(trig[:, 1], trig[:, 1], ACT.Sin).then_inc(s_rope_act, 1)

            with act.Fori(0, DEPTH) as layer:
                act_link.bind(layer)
                nc.scalar.preload_act_table_set(LN_EXP)
                act.wait_ge(x_done.sem, x_done.at_number(layer, 0))
                for t in range(T):
                    ins = run(square_out[:, t, :], xs_res[:, t, :], ACT.Square, accum_out=stat[:, t:t + 1])
                ins.then_inc(act_link.sem, 1)
                act.wait_ge(act_link.sem, act_link.next())
                rsqrt(stat[:, 0:2], stat[:, 0:2], D).then_inc(act_ready.sem, act_ready.inc("h_r"))
                for h in range(AHEAD):
                    hi_half(layer, h)
                act.wait_ge(s_param, layer * (16 * n_params) + 16 * n_params)
                for j in range(4):
                    turn_hi(layer, f"h{j}", a_hi[:, 2 * j:2 * j + 2, :],
                            [chan_col("pre_mix", 2 * j + i) for i in range(2)])
                for u in range(NU):
                    kind, name, i = UNITS[u]
                    for h in range(2 * u + AHEAD, min(2 * u + AHEAD + 2, 2 * NU)):
                        hi_half(layer, h)
                    for f in fills_of.get(u, []):
                        if READ_BY_ACT[f]:
                            read(layer, f)
                    for s in STEPS.get(u, []):
                        if s in ("ssd_gate", "ret_gate", "gla_gate", "last_gate"):
                            step(s, layer)
                            nc.scalar.preload_act_table_set(LN_EXP)
                        elif s == "ssd_norm":
                            group_rsqrt(layer, "ssd", 4, 256)
                        elif s == "ret_norm":
                            group_rsqrt(layer, "ret", 8, 128)
                        elif s == "gla_norm":
                            group_rsqrt(layer, "gla", 8, 128)
                        else:
                            step(s, layer)
                    if kind == "branch" and name == "gla":
                        for m in (2 * i, 2 * i + 1):
                            act.wait_ge(merge_sum.sem, merge_sum.at(layer, f"m{m}"))
                            run(a_hi[:, 2 * m:2 * m + 2, :], merged[:, 2 * m:2 * m + 2, :]).then_inc(merge_hi.sem, merge_hi.inc(f"m{m}"))
                    if kind == "out" and i == 3:
                        wait_for_products(act, layer, "out", "out", 3)
                        for t in range(T):
                            ins = run(square_out[:, t, :].rearrange("p (a b) -> p a b", a=2),
                                      proj[:, 2 * t:2 * t + 2, :], ACT.Square, accum_out=stat[:, t:t + 1])
                        ins.then_inc(act_link.sem, 1)
                        act.wait_ge(act_link.sem, act_link.next())
                        rsqrt(stat[:, 0:2], stat[:, 0:2], D).then_inc(act_ready.sem, act_ready.inc("mix_r"))
                        act.wait_ge(dve_ready.sem, dve_ready.at(layer, "x_mixed"))
                        for t in range(T):
                            ins = run(square_out[:, t, :], xs_res[:, t, :], ACT.Square,
                                      accum_out=stat[:, t:t + 1])
                        ins.then_inc(act_link.sem, 1)
                        act.wait_ge(act_link.sem, act_link.next())
                        rsqrt(stat[:, 0:2], stat[:, 0:2], D).then_inc(act_ready.sem, act_ready.inc("u_r"))
                        for j in range(4):
                            turn_hi(layer, f"u{j}", a_hi[:, 2 * j:2 * j + 2, :],
                                    [chan_col("pre_mlp", 2 * j + k) for k in range(2)])
                    if kind == "up":
                        wait_for_products(act, layer, "up", "up", i)
                        pair = mix[:, 2 * (i % 2):2 * (i % 2) + 2, 0:SEQ]
                        if i >= 2:
                            act.wait_ge(up_lo.sem, up_lo.at(layer, f"up{i - 2}"))
                        run(part(R2, 512 * (i % 2), 2, SEQ), pair, ACT.Relu).then_inc(up_read.sem, up_read.inc(f"up{i}"))
                        act.wait_ge(up_read.sem, up_read.at(layer, f"up{i}"))
                        if i >= 2:
                            wait_for_products(act, layer, "down", "down", i - 2)
                        else:
                            wait_for_products(act, layer, "branch", "gla", 1)
                        run(y_hi[:, 2 * (i % 2):2 * (i % 2) + 2, :], part(R2, 512 * (i % 2), 2, SEQ),
                                       ACT.Square).then_inc(up_hi.sem, up_hi.inc(f"up{i}"))
                wait_for_products(act, layer, "down", "down", 15)
                for t in range(T):
                    ins = run(square_out[:, t, :].rearrange("p (a b) -> p a b", a=2),
                              proj[:, 2 * t:2 * t + 2, :], ACT.Square, accum_out=stat[:, t:t + 1])
                ins.then_inc(act_link.sem, 1)
                act.wait_ge(act_link.sem, act_link.next())
                rsqrt(stat[:, 0:2], stat[:, 0:2], D).then_inc(act_ready.sem, act_ready.inc("mlp_r"))
            assert act_link.n == ACT_LINKS, act_link.n

        @block.vector
        def _(dve):
            v = nc.vector

            def lo_half(layer, u):
                src, hi, lo = half_views(u, 0)
                dve.wait_ge(hi_made.sem, hi_made.at(layer, f"half{2 * u}"))
                v.tensor_tensor(lo, src, hi.bitcast(F32), ALU.subtract).then_inc(lo_even.sem, lo_even.inc(f"unit{u}"))

            def turn_lo(layer, name, hi, lo, gain):
                dve.wait_ge(turned_hi.sem, turned_hi.at(layer, name))
                for i in range(2):
                    ins = v.scalar_tensor_tensor(out=lo[:, i, :], in0=bank(name)[:, SEQ * i:SEQ * i + SEQ],
                                                 scalar=gain[i] if gain else 1.0, in1=hi[:, i, :].bitcast(F32),
                                                 op0=ALU.mult, op1=ALU.subtract)
                ins.then_inc(job_read.sem, job_read.inc(name))

            def full(layer, job):
                dve.wait_ge(job_full.sem, job_full.at(layer, job))
                return bank(job)

            def rope(x1, x2, cos, sin, o1, o2, a, b):
                v.tensor_tensor(a, x1, cos, ALU.mult)
                v.tensor_tensor(b, x2, sin, ALU.mult).then_inc(dve_link.sem, 1)
                dve.wait_ge(dve_link.sem, dve_link.next())
                v.tensor_tensor(o1, a, b, ALU.subtract).then_inc(dve_link.sem, 1)
                dve.wait_ge(dve_link.sem, dve_link.next())
                v.tensor_tensor(a, x2, cos, ALU.mult)
                v.tensor_tensor(b, x1, sin, ALU.mult).then_inc(dve_link.sem, 1)
                dve.wait_ge(dve_link.sem, dve_link.next())
                return v.tensor_tensor(o2, a, b, ALU.add)

            def heads(ap, n, d):
                return ap.unsqueeze(2).broadcast_to((P, n, d))

            def split_heads(ap, n):
                return ap.rearrange("p t (h d) -> p (t h) d", h=n)

            def squares(y, n, tmp, event, at=8):
                v.tensor_tensor(tmp, y, y, ALU.mult).then_inc(dve_link.sem, 1)
                dve.wait_ge(dve_link.sem, dve_link.next())
                v.tensor_reduce(stat[:, at:at + T * n], split_heads(tmp, n), X_AXIS, ALU.add).then_inc(dve_ready.sem, dve_ready.inc(event))

            def step(name, layer):
                if name == "mla_norm":
                    dve.wait_ge(act_ready.sem, act_ready.at(layer, "mla_r"))
                    for t in range(T):
                        v.tensor_scalar(c[:, t, 0:256], c[:, t, 0:256], stat[:, 4 + t:5 + t], None, ALU.mult)
                        ins = v.tensor_scalar(c[:, t, 256:384], c[:, t, 256:384], stat[:, 6 + t:7 + t], None,
                                              ALU.mult)
                    ins.then_inc(dve_ready.sem, dve_ready.inc("c_scaled"))
                    cos, sin = trig[:, 0, :, 0::2], trig[:, 1, :, 0::2]
                    kr = c[:, :, 384:416]
                    ra, rb = (part(R1, 4096 + 512 * i, T, 16) for i in range(2))
                    rope(kr[:, :, 0:16], kr[:, :, 16:32], cos, sin, k_rot[:, :, 0:16],
                                k_rot[:, :, 16:32], ra, rb).then_inc(dve_ready.sem, dve_ready.inc("k_rot"))
                if name == "mla_turn":
                    b = full(layer, "cq")
                    for m in range(2):
                        ins = v.tensor_scalar(cT[:, m, :], b[:, SEQ * m:SEQ * m + SEQ], chan_col("q_norm", m),
                                              None, ALU.mult)
                    ins.then_inc(job_read.sem, job_read.inc("cq"))
                    b = full(layer, "ckv")
                    v.tensor_scalar(cT[:, 2, :], b[:, 0:SEQ], chan_col("kv_norm", 0), None, ALU.mult)
                    v.tensor_copy(kT[64:96, :, :], b[0:32, SEQ:2 * SEQ].unsqueeze(1)
                                                .broadcast_to((32, 8, SEQ))).then_inc(job_read.sem, job_read.inc("ckv"))
                if name == "mla_q":
                    v.tensor_copy(q_pe.rearrange("p a b -> p (a b)"), full(layer, "qpe")).then_inc(job_read.sem, job_read.inc("qpe"))
                    for j in range(4):
                        b = full(layer, f"qn{j}")[0:64].rearrange("p (h n) -> p h n", h=2)
                        v.tensor_copy(qT[0:64, 2 * j:2 * j + 2, :], b).then_inc(job_read.sem, job_read.inc(f"qn{j}"))
                    q = q_pe.rearrange("p t (h d) -> p t h d", h=8)
                    o = q_rot.rearrange("p t (h d) -> p t h d", h=8)
                    cos, sin = (trig[:, i, :, 0::2].unsqueeze(2).broadcast_to((P, T, 8, 16)) for i in range(2))
                    ra, rb = (part(R1, 4096 + 512 * i, T, 8, 16) for i in range(2))
                    dve.wait_ge(job_read.sem, job_read.at(layer, "qn3"))
                    rope(q[:, :, :, 0:16], q[:, :, :, 16:32], cos, sin, o[:, :, :, 0:16],
                                o[:, :, :, 16:32], ra, rb).then_inc(dve_ready.sem, dve_ready.inc("q_rot"))
                if name == "mla_kv":
                    for j in range(4):
                        b = full(layer, f"kn{j}")[0:64].rearrange("p (h n) -> p h n", h=2)
                        v.tensor_copy(kT[0:64, 2 * j:2 * j + 2, :], b).then_inc(job_read.sem, job_read.inc(f"kn{j}"))
                    dve.wait_ge(dve_ready.sem, dve_ready.at(layer, "q_rot"))
                    for t in range(T):
                        v.tensor_copy(v_mla[:, t, :], full(layer, f"v{t}")).then_inc(job_read.sem, job_read.inc(f"v{t}"))
                if name == "mla_pe":
                    b = full(layer, "qpeT").rearrange("p (g n) -> p g n", g=2)
                    for q in range(4):
                        ins = v.tensor_copy(qT[64:96, q:8:4, :], b[32 * q:32 * q + 32])
                    ins.then_inc(job_read.sem, job_read.inc("qpeT"))
                if name.startswith("mla_a"):
                    i = int(name[5:])
                    if i < NS:
                        t, _, n = SOFT[i]
                        w = P * (t + 1)
                        s = soft[:, i % 2, :].rearrange("p (h n) -> p h n", h=n)
                        neg = cst("neg", 2 * P)[:, 2 * P - w:2 * P].unsqueeze(1).broadcast_to((P, n, w))
                        b = full(layer, f"score{i}").rearrange("p (h n) -> p h n", h=n)
                        if i >= 2:
                            dve.wait_ge(job_full.sem, job_full.at(layer, f"turn{i - 2}"))
                        elif i == 0:
                            dve.wait_ge(job_full.sem, job_full.at(layer, "qpeT"))
                        v.scalar_tensor_tensor(out=s, in0=b, scalar=96 ** -0.5, in1=neg,
                                                             op0=ALU.mult, op1=ALU.add).then_inc(job_read.sem, job_read.inc(f"score{i}"))
                        dve.wait_ge(job_read.sem, job_read.at(layer, f"score{i}"))
                        v.tensor_reduce(stat[:, 8:8 + n], s, X_AXIS, ALU.max).then_inc(dve_link.sem, 1)
                        dve.wait_ge(dve_link.sem, dve_link.next())
                        v.tensor_tensor(s, s, heads(stat[:, 8:8 + n], n, w), ALU.subtract).then_inc(dve_ready.sem, dve_ready.inc(f"shifted{i}"))
                    if 1 <= i <= NS:
                        j = i - 1
                        t, _, n = SOFT[j]
                        dve.wait_ge(act_ready.sem, act_ready.at(layer, f"exp{j}"))
                        s = soft[:, j % 2, :].rearrange("p (h n) -> p h n", h=n)
                        sums = stat[:, 16 + 4 * (j % 2):16 + 4 * (j % 2) + n]
                        v.tensor_reduce(sums, s, X_AXIS, ALU.add).then_inc(dve_link.sem, 1)
                        dve.wait_ge(dve_link.sem, dve_link.next())
                        v.reciprocal(sums, sums).then_inc(dve_link.sem, 1)
                        dve.wait_ge(dve_link.sem, dve_link.next())
                        if i == 1:
                            dve.wait_ge(job_read.sem, job_read.at(layer, "v1"))
                        v.tensor_copy(probT[:, j % 2, :], full(layer, f"turn{j}")).then_inc(job_read.sem, job_read.inc(f"turn{j}"))
                    if i >= 2:
                        j = i - 2
                        t, h, n = SOFT[j]
                        b = full(layer, f"pv{j}")[:, 0:64 * n].rearrange("p (h n) -> p h n", h=n)
                        o = o_mla[:, t, 64 * h:64 * (h + n)].rearrange("p (h n) -> p h n", h=n)
                        sums = stat[:, 16 + 4 * (j % 2):16 + 4 * (j % 2) + n]
                        v.tensor_tensor(o, b, heads(sums, n, 64), ALU.mult).then_inc(job_read.sem, job_read.inc(f"pv{j}"))
                if name == "mla_y":
                    for j in range(2):
                        s = slice(2 * j, 2 * j + 2)
                        turn_lo(layer, f"mla_y{j}", y_hi[:, s, :], y_lo[:, s, :], None)
                if name.startswith("conv"):
                    m = int(name[4:])
                    dve.wait_ge(act_ready.sem, act_ready.at(layer, f"tap{m}"))
                    for k in range(1, 4):
                        ins = v.scalar_tensor_tensor(out=conv[:, m, :], in0=xbc[:, m, k:k + SEQ],
                                                     scalar=chan_col("conv_w", 8 * k + m), in1=conv[:, m, :],
                                                     op0=ALU.mult, op1=ALU.add)
                        if k < 3:
                            ins.then_inc(dve_link.sem, 1)
                            dve.wait_ge(dve_link.sem, dve_link.next())
                    ins.then_inc(dve_ready.sem, dve_ready.inc(f"conv{m}"))
                if name == "ssd_dt":
                    x_ = stat[:, 8:24]
                    dve.wait_ge(read_act.sem, read_act.at(layer, "fill0"))
                    v.tensor_tensor(x_.rearrange("p (t h) -> p t h", t=T), c[:, :, 416:424],
                                             head_rows[:, 0:8].unsqueeze(1).broadcast_to((P, T, 8)), ALU.add).then_inc(dve_link.sem, 1)
                    dve.wait_ge(dve_link.sem, dve_link.next())
                    v.scalar_tensor_tensor(out=stat[:, 24:40], in0=x_, scalar=-1.0, in1=x_,
                                                  op0=ALU.mult, op1=ALU.min).then_inc(dve_ready.sem, dve_ready.inc("dt_x"))
                if name == "ssd_cum":
                    x_, u, w = stat[:, 8:24], stat[:, 24:40], stat[:, 40:56]
                    dve.wait_ge(act_ready.sem, act_ready.at(layer, "dt_u"))
                    v.tensor_scalar(w1, u, 1.0, None, ALU.add).then_inc(dve_link.sem, 1)
                    dve.wait_ge(dve_link.sem, dve_link.next())
                    v.tensor_copy(w, w1).then_inc(dve_ready.sem, dve_ready.inc("dt_w"))
                    v.scalar_tensor_tensor(out=u, in0=w1, scalar=-1.0, in1=u, op0=ALU.add,
                                                    op1=ALU.subtract).then_inc(dve_link.sem, 1)
                    dve.wait_ge(dve_link.sem, dve_link.next())
                    v.reciprocal(w1, w1).then_inc(dve_link.sem, 1)
                    dve.wait_ge(dve_link.sem, dve_link.next())
                    v.tensor_tensor(u, u, w1, ALU.mult).then_inc(dve_link.sem, 1)
                    dve.wait_ge(dve_link.sem, dve_link.next())
                    v.scalar_tensor_tensor(out=x_, in0=x_, scalar=0.0, in1=u, op0=ALU.max,
                                                    op1=ALU.subtract).then_inc(dve_link.sem, 1)
                    dve.wait_ge(dve_link.sem, dve_link.next())
                    dve.wait_ge(act_ready.sem, act_ready.at(layer, "dt_ln"))
                    v.tensor_tensor(x_, x_, w, ALU.add).then_inc(dve_link.sem, 1)
                    dve.wait_ge(dve_link.sem, dve_link.next())
                    v.scalar_tensor_tensor(
                        out=log_decay.rearrange("p (t h) -> p t h", t=T), in0=x_.rearrange("p (t h) -> p t h", t=T),
                        scalar=-1.0, in1=stat[:, 0:8].unsqueeze(1).broadcast_to((P, T, 8)),
                        op0=ALU.mult, op1=ALU.mult).then_inc(dve_ready.sem, dve_ready.inc("log_decay"))
                if name == "ssd_turn":
                    b = full(layer, "G").rearrange("p (g n) -> p g n", g=4)
                    v.tensor_tensor(G, b, causal.unsqueeze(1).broadcast_to((P, 4, P)), ALU.mult).then_inc(job_read.sem, job_read.inc("G"))
                    for t in range(T):
                        b = full(layer, f"xs{t}")
                        v.tensor_copy(xs[:, t, :], b).then_inc(job_read.sem, job_read.inc(f"xs{t}"))
                    dve.wait_ge(job_read.sem, job_read.at(layer, "xs1"))
                    v.tensor_tensor(split_heads(xdt, 8), split_heads(xs, 8),
                                           heads(stat[:, 8:24], 16, 64), ALU.mult).then_inc(dve_ready.sem, dve_ready.inc("xdt"))
                    v.tensor_copy(B_tok.rearrange("p a b -> p (a b)"), full(layer, "B")[:, 0:256]).then_inc(job_read.sem, job_read.inc("B"))
                    dve.wait_ge(act_ready.sem, act_ready.at(layer, "ends"))
                    dve.wait_ge(dve_ready.sem, dve_ready.at(layer, "xdt"))
                    v.tensor_tensor(x_end.rearrange("p (h d) -> p h d", h=8),
                                           xdt[:, 0, :].rearrange("p (h d) -> p h d", h=8),
                                           heads(stat[:, 40:48], 8, 64), ALU.mult).then_inc(dve_ready.sem, dve_ready.inc("x_end"))
                    v.tensor_tensor(split_heads(sy, 8)[:, 0:8], split_heads(xs, 8)[:, 0:8],
                                    heads(head_rows[:, 16:24], 8, 64), ALU.mult)
                    v.tensor_tensor(split_heads(sy, 8)[:, 8:16], split_heads(xs, 8)[:, 8:16],
                                             heads(head_rows[:, 16:24], 8, 64), ALU.mult).then_inc(dve_link.sem, 1)
                    dve.wait_ge(dve_link.sem, dve_link.next())
                if name.startswith("ssd_decay"):
                    i = int(name[9:])
                    t, g = i // 2, i % 2
                    s = L[:, 4 * g:4 * g + 4, :]
                    b = full(layer, f"R{i}").rearrange("p (h n) -> p h n", h=4)
                    if i == 0:
                        dve.wait_ge(pool_ready.sem, pool_ready.at(layer, "z_silu"))
                    if i >= 2:
                        dve.wait_ge(job_full.sem, job_full.at(layer, "Y0"))
                    v.tensor_tensor(s, b, heads(c_cum(t, g), 4, P), ALU.subtract).then_inc(job_read.sem, job_read.inc(f"R{i}"))
                    dve.wait_ge(job_read.sem, job_read.at(layer, f"R{i}"))
                    v.tensor_scalar(s, s, 0.0, None, ALU.min).then_inc(dve_ready.sem, dve_ready.inc(f"seg{i}"))
                    dve.wait_ge(act_ready.sem, act_ready.at(layer, f"decay{i}"))
                    v.tensor_tensor(s, s, G[:, 2 * t + g, :].unsqueeze(1).broadcast_to((P, 4, P)),
                                           ALU.mult).then_inc(dve_ready.sem, dve_ready.inc(f"weights{i}"))
                    if i == 1:
                        v.tensor_copy(s_state, full(layer, "S")).then_inc(job_read.sem, job_read.inc("S"))
                if name == "ssd_y0":
                    v.tensor_tensor(sy[:, 0, :], sy[:, 0, :], full(layer, "Y0"), ALU.add).then_inc(job_read.sem, job_read.inc("Y0"))
                if name == "ssd_y1":
                    b = full(layer, "off").rearrange("p (h d) -> p h d", h=8)
                    s = s_tmp.rearrange("p (h d) -> p h d", h=8)
                    v.tensor_tensor(s, b, heads(stat[:, 48:56], 8, 64), ALU.mult).then_inc(job_read.sem, job_read.inc("off"))
                    dve.wait_ge(job_read.sem, job_read.at(layer, "off"))
                    v.tensor_tensor(sy[:, 1, :], sy[:, 1, :], s_tmp, ALU.add).then_inc(dve_link.sem, 1)
                    dve.wait_ge(dve_link.sem, dve_link.next())
                    v.tensor_tensor(sy[:, 1, :], sy[:, 1, :], full(layer, "Y1"), ALU.add).then_inc(job_read.sem, job_read.inc("Y1"))
                    dve.wait_ge(job_read.sem, job_read.at(layer, "Y1"))
                    v.memset(stat[:, 63:64], 0.0).then_inc(dve_ready.sem, dve_ready.inc("ssd_summed"))
                if name == "ssd_norm":
                    dve.wait_ge(pool_ready.sem, pool_ready.at(layer, "ssd_gated"))
                    squares(sy, 2, z_s, "ssd_squared")
                    dve.wait_ge(act_ready.sem, act_ready.at(layer, "ssd_r"))
                    v.tensor_tensor(split_heads(sy, 2), split_heads(sy, 2), heads(stat[:, 8:12], 4, 256),
                                           ALU.mult).then_inc(dve_ready.sem, dve_ready.inc("ssd_out"))
                if name in ("ssd_y", "ret_y", "gla_y"):
                    for j in range(2):
                        s = slice(2 * j, 2 * j + 2)
                        turn_lo(layer, f"{name}{j}", y_hi[:, s, :], y_lo[:, s, :],
                                [chan_col(name[:3], 2 * j + i) for i in range(2)])
                if name == "ret_rope":
                    dve.wait_ge(read_act.sem, read_act.at(layer, f"fill{FILLS.index(('token', 'rqk', 1))}"))
                    dve.wait_ge(job_read.sem, job_read.at(layer, "mla_y1"))
                    for t in range(T):
                        q = rqk[:, t, :].rearrange("p (h d) -> p h d", h=8)
                        o = rr[:, t, :].rearrange("p (h d) -> p h d", h=8)
                        cos, sin = (trig[:, i, t, :].unsqueeze(1).broadcast_to((P, 8, 32)) for i in range(2))
                        ra, rb = (part(R1, 5120 + 512 * i + 256 * t, 8, 32) for i in range(2))
                        rope(q[:, :, 0:32], q[:, :, 32:64], cos, sin, o[:, :, 0:32], o[:, :, 32:64],
                                      ra, rb).then_inc(dve_link.sem, 1)
                        dve.wait_ge(dve_link.sem, dve_link.next())
                    for t in range(T):
                        o = rr[:, t, :].rearrange("p (h d) -> p h d", h=8)
                        ins = v.tensor_tensor(o, o, heads(cst("ret_scale", 8), 8, 64), ALU.mult)
                    ins.then_inc(dve_ready.sem, dve_ready.inc("r_scaled"))
                if name == "ret_turn":
                    for j, n in enumerate(("rq", "rk")):
                        v.tensor_copy(rT[:, 2 * j:2 * j + 2, :].rearrange("p a b -> p (a b)"),
                                                    full(layer, n)).then_inc(job_read.sem, job_read.inc(n))
                if name in ("ret_s0", "ret_s1"):
                    t = int(name[5])
                    b = full(layer, f"rs{t}").rearrange("p (h n) -> p h n", h=4)
                    s = rS[:, t, :].rearrange("p (h n) -> p h n", h=4)
                    v.tensor_tensor(s, b, causal.unsqueeze(1).broadcast_to((P, 4, P)), ALU.mult).then_inc(job_read.sem, job_read.inc(f"rs{t}"))
                    if t == 0:
                        b = full(layer, "rS")[:, 0:256].rearrange("p (h n) -> p h n", h=2)
                        v.tensor_tensor(r_state, b, heads(cst("ret_total", 2), 2, P), ALU.mult).then_inc(job_read.sem, job_read.inc("rS"))
                if name in ("ret_y0", "ret_y1"):
                    t = int(name[5])
                    v.tensor_copy(ry[:, t, :], full(layer, f"rY{t}")).then_inc(job_read.sem, job_read.inc(f"rY{t}"))
                if name == "ret_norm":
                    dve.wait_ge(job_read.sem, job_read.at(layer, "rY1"))
                    squares(ry, 4, rg_s, "ret_squared")
                    dve.wait_ge(pool_ready.sem, pool_ready.at(layer, "rg_silu"))
                    v.tensor_tensor(ry, ry, rg, ALU.mult).then_inc(dve_link.sem, 1)
                    dve.wait_ge(dve_link.sem, dve_link.next())
                    dve.wait_ge(act_ready.sem, act_ready.at(layer, "ret_r"))
                    v.tensor_tensor(split_heads(ry, 4), split_heads(ry, 4), heads(stat[:, 8:16], 8, P),
                                           ALU.mult).then_inc(dve_ready.sem, dve_ready.inc("ret_out"))
                if name == "gla_low":
                    v.tensor_copy(g_low, full(layer, "low")[0:16, 0:SEQ]).then_inc(job_read.sem, job_read.inc("low"))
                if name == "gla_decay":
                    b = full(layer, "gate").rearrange("p (m n) -> p m n", m=2)
                    for m in range(2):
                        ins = v.tensor_scalar(g_cum[:, m, :], b[:, m, :], chan_col("gla_b", m), None, ALU.add)
                    ins.then_inc(job_read.sem, job_read.inc("gate"))
                    dve.wait_ge(job_read.sem, job_read.at(layer, "gate"))
                    v.scalar_tensor_tensor(out=g_ei, in0=g_cum, scalar=-1.0, in1=g_cum,
                                                  op0=ALU.mult, op1=ALU.min).then_inc(dve_ready.sem, dve_ready.inc("gate_n"))
                    dve.wait_ge(act_ready.sem, act_ready.at(layer, "gate_ln"))
                    v.scalar_tensor_tensor(out=g_end, in0=g_cum, scalar=0.0, in1=g_ei,
                                                    op0=ALU.min, op1=ALU.subtract).then_inc(dve_link.sem, 1)
                    dve.wait_ge(dve_link.sem, dve_link.next())
                    for m in range(2):
                        ins = v.tensor_tensor_scan(g_cum[:, m, :], cst("restart", SEQ), g_end[:, m, :], 0.0,
                                                   ALU.mult, ALU.add)
                    ins.then_inc(dve_link.sem, 1)
                    dve.wait_ge(dve_link.sem, dve_link.next())
                    cum = g_cum.rearrange("p m (c n) -> p (m c) n", n=64)
                    v.tensor_tensor(g_end.rearrange("p m (c n) -> p (m c) n", n=64),
                                           cum[:, :, 63:64].broadcast_to((P, 8, 64)), cum, ALU.subtract).then_inc(dve_ready.sem, dve_ready.inc("g_cum"))
                if name == "gla_scale":
                    dve.wait_ge(act_ready.sem, act_ready.at(layer, "g_exps"))
                    dve.wait_ge(read_act.sem, read_act.at(layer, f"fill{FILLS.index(('channel', 'gqk', 1))}"))
                    v.tensor_tensor(g_end, g_end, gqk[:, 2:4, :], ALU.mult).then_inc(dve_ready.sem, dve_ready.inc("k_end"))
                    v.scalar_tensor_tensor(out=gqk[:, 0:2, :], in0=gqk[:, 0:2, :], scalar=64 ** -0.5, in1=g_e,
                                           op0=ALU.mult, op1=ALU.mult)
                    v.tensor_tensor(gqk[:, 2:4, :], gqk[:, 2:4, :], g_ei, ALU.mult).then_inc(dve_ready.sem, dve_ready.inc("qk_in"))
                if name == "gla_turn":
                    dve.wait_ge(job_read.sem, job_read.at(layer, "ssd_y1"))
                    v.memset(gS, 0.0).then_inc(dve_ready.sem, dve_ready.inc("gS_zero"))
                    v.tensor_copy(k_tok.rearrange("p a b -> p (a b)"), full(layer, "kst")).then_inc(job_read.sem, job_read.inc("kst"))
                if name in ("gla_s0", "gla_s1"):
                    t = int(name[5])
                    b = full(layer, f"gs{t}").rearrange("p (h n) -> p h n", h=4)
                    s = gS[:, t, :].rearrange("p (h n) -> p h n", h=4)
                    dve.wait_ge(dve_ready.sem, dve_ready.at(layer, "gS_zero"))
                    mask = cst("block", P).bitcast(I32).unsqueeze(1).broadcast_to((P, 4, P))
                    v.memset(stat[:, 63:64], 0.0)
                    v.copy_predicated(s, mask, b).then_inc(job_read.sem, job_read.inc(f"gs{t}"))
                if name == "gla_state":
                    b = full(layer, "gS0")[:, 0:256]
                    v.tensor_copy(g_state[:, 0].rearrange("p a b -> p (a b)"), b).then_inc(job_read.sem, job_read.inc("gS0"))
                    for ch in (1, 2):
                        dve.wait_ge(job_read.sem, job_read.at(layer, f"gS{ch - 1}"))
                        b = full(layer, f"gS{ch}")[:, 0:256].rearrange("p (a b) -> p a b", a=2)
                        for m in range(2):
                            ins = v.scalar_tensor_tensor(out=g_state[:, ch, m, :], in0=g_state[:, ch - 1, m, :],
                                                         scalar=g_e[:, m, 64 * ch + 63:64 * ch + 64],
                                                         in1=b[:, m, :], op0=ALU.mult, op1=ALU.add)
                        ins.then_inc(job_read.sem, job_read.inc(f"gS{ch}"))
                if name in ("gla_o0", "gla_o1"):
                    t = int(name[5])
                    v.tensor_copy(gy[:, t, :], full(layer, f"gY{t}")).then_inc(job_read.sem, job_read.inc(f"gY{t}"))
                if name == "gla_norm":
                    dve.wait_ge(job_read.sem, job_read.at(layer, "gY1"))
                    dve.wait_ge(pool_ready.sem, pool_ready.at(layer, "gg_silu"))
                    squares(gy, 4, gg_s, "gla_squared")
                    v.tensor_tensor(gy, gy, gg, ALU.mult).then_inc(dve_link.sem, 1)
                    dve.wait_ge(dve_link.sem, dve_link.next())
                    dve.wait_ge(act_ready.sem, act_ready.at(layer, "gla_r"))
                    v.tensor_tensor(split_heads(gy, 4), split_heads(gy, 4), heads(stat[:, 8:16], 8, P),
                                           ALU.mult).then_inc(dve_ready.sem, dve_ready.inc("gla_out"))


            def c_cum(t, g):
                return cum_keep[:, 8 * t + 4 * g:8 * t + 4 * g + 4]

            def cum_read(layer):
                b = full(layer, "cum")
                v.tensor_copy(cum_keep, b[:, 0:16])
                v.tensor_copy(stat[:, 40:56], b[:, 0:16])
                v.tensor_copy(stat[:, 24:32], b[:, 16:24]).then_inc(job_read.sem, job_read.inc("cum"))
                dve.wait_ge(job_read.sem, job_read.at(layer, "cum"))
                v.tensor_tensor(stat[:, 40:48], stat[:, 24:32], stat[:, 40:48], ALU.subtract).then_inc(dve_ready.sem, dve_ready.inc("cum"))

            def branch_read(layer, f):
                _, name, m = FILLS[f]
                dve.wait_ge(half_done.sem, half_done.at(layer, f"half{FILL_ENDS[f]}"))
                if m == 0:
                    dve.wait_ge(act_ready.sem, act_ready.at(layer, f"{name}_gates"))
                pair = proj[:, 2 * (f % 2):2 * (f % 2) + 2, 0:SEQ]
                s = slice(2 * m, 2 * m + 2)
                if name == "mla":
                    v.tensor_tensor(merged[:, s, :], pair, gates[:, s, :], ALU.mult).then_inc(read_dve.sem, read_dve.inc(f"fill{f}"))
                    if m == 3:
                        v.memset(stat[:, 63:64], 0.0).then_inc(dve_ready.sem, dve_ready.inc("mla_merged"))
                    return
                v.tensor_tensor(gates[:, s, :], pair, gates[:, s, :], ALU.mult).then_inc(read_dve.sem, read_dve.inc(f"fill{f}"))
                dve.wait_ge(read_dve.sem, read_dve.at(layer, f"fill{f}"))
                ins = v.tensor_tensor(merged[:, s, :], merged[:, s, :], gates[:, s, :], ALU.add)
                if name == "gla":
                    ins.then_inc(merge_sum.sem, merge_sum.inc(f"m{m}"))
                    dve.wait_ge(merge_hi.sem, merge_hi.at(layer, f"m{m}"))
                    v.tensor_tensor(a_lo[:, s, :], merged[:, s, :], a_hi[:, s, :].bitcast(F32),
                                                  ALU.subtract).then_inc(merge_lo.sem, merge_lo.inc(f"m{m}"))
                elif m == 3:
                    ins.then_inc(dve_ready.sem, dve_ready.inc(f"{name}_merged"))

            def add_normed(layer, event):
                dve.wait_ge(act_ready.sem, act_ready.at(layer, event))
                for t in range(T):
                    ins = v.scalar_tensor_tensor(
                        out=update[:, t, :].rearrange("p (a b) -> p a b", a=2), in0=proj[:, 2 * t:2 * t + 2, :],
                        scalar=stat[:, t:t + 1], in1=post_gain[:].rearrange("p (a b) -> p a b", a=2),
                        op0=ALU.mult, op1=ALU.mult)
                ins.then_inc(dve_link.sem, 1)
                dve.wait_ge(dve_link.sem, dve_link.next())
                return v.tensor_tensor(xs_res[:], xs_res[:], update, ALU.add)

            def normalise(layer, event_in, event_out):
                dve.wait_ge(act_ready.sem, act_ready.at(layer, event_in))
                for t in range(T):
                    ins = v.tensor_scalar(normed[:, t, :], xs_res[:, t, :], stat[:, t:t + 1], None, ALU.mult)
                ins.then_inc(dve_ready.sem, dve_ready.inc(event_out))

            v.memset(stat[:, 56:57], 0.0).then_inc(lo_even.sem, RAW)
            v.memset(stat[:, 62:63], 0.0).then_inc(lo_odd.sem, RAW)
            v.memset(stat[:, 57:58], 0.0).then_inc(half_done.sem, HL)
            dve.wait_ge(s_input, 48)
            v.memset(stat[:, 58:59], 0.0).then_inc(x_done.sem, 1)

            n = [0]

            def pre(ins):
                n[0] += 1
                ins.then_inc(s_pre, 1)
                dve.wait_ge(s_pre, n[0])

            ang, turns = part(R1, 0, T, ROPE), part(R1, 128, T, ROPE)
            pre(v.tensor_copy(stat[:, 60:62], pos_i[:]))
            for t in range(T):
                pre(v.tensor_scalar(ang[:, t, :], cst("freq", ROPE), stat[:, 60 + t:61 + t], None, ALU.mult))
            magic = 12582912.0
            for i, quarter in ((0, 0.25), (1, 0.0)):
                pre(v.tensor_scalar(turns, ang, 1 / (2 * np.pi), quarter, ALU.mult, ALU.add))
                pre(v.tensor_scalar(turns, turns, magic, -magic, ALU.add, ALU.add))
                at = trig[:, i]
                rest = 2 * np.pi
                for k in range(4):
                    bits = np.float64(rest) if k == 3 else np.float64(
                        np.floor(rest * 2.0 ** (6 + 9 * k)) / 2.0 ** (6 + 9 * k))
                    rest -= bits
                    pre(v.scalar_tensor_tensor(out=at, in0=turns, scalar=-float(bits), in1=ang if k == 0 else at,
                                               op0=ALU.mult, op1=ALU.add))
                if i == 0:
                    pre(v.tensor_scalar(at, at, float(np.pi / 2), None, ALU.add))
                pre(v.tensor_scalar(at, at, PI, -PI, ALU.min, ALU.max))
            v.memset(stat[:, 59:60], 0.0).then_inc(s_rope, 1)
            dve.wait_ge(s_rope_act, 2)

            with dve.Fori(0, DEPTH) as layer:
                dve_link.bind(layer)
                normalise(layer, "h_r", "h_normed")
                dve.wait_ge(s_param, layer * (16 * n_params) + 16 * n_params)
                lo_half(layer, 0)
                for j in range(4):
                    s = slice(2 * j, 2 * j + 2)
                    turn_lo(layer, f"h{j}", a_hi[:, s, :], a_lo[:, s, :],
                            [chan_col("pre_mix", 2 * j + i) for i in range(2)])
                v.memset(xbc[:, :, 0:3], 0.0).then_inc(dve_ready.sem, dve_ready.inc("pad"))
                for u in range(NU):
                    kind, name, i = UNITS[u]
                    if u + 1 < NU:
                        lo_half(layer, u + 1)
                    for f in fills_of.get(u, []):
                        if not READ_BY_ACT[f]:
                            branch_read(layer, f)
                    for s in STEPS.get(u, []):
                        if s == "ssd_gate":
                            cum_read(layer)
                        else:
                            step(s, layer)
                    if kind == "out" and i == 3:
                        add_normed(layer, "mix_r").then_inc(dve_ready.sem, dve_ready.inc("x_mixed"))
                        normalise(layer, "u_r", "u_normed")
                        for j in range(4):
                            s = slice(2 * j, 2 * j + 2)
                            turn_lo(layer, f"u{j}", a_hi[:, s, :], a_lo[:, s, :],
                                    [chan_col("pre_mlp", 2 * j + k) for k in range(2)])
                    if kind == "up":
                        r, r2 = part(R2, 512 * (i % 2), 2, SEQ), part(R2, 1024 + 512 * (i % 2), 2, SEQ)
                        dve.wait_ge(up_read.sem, up_read.at(layer, f"up{i}"))
                        v.tensor_tensor(r2, r, r, ALU.mult).then_inc(dve_link.sem, 1)
                        dve.wait_ge(dve_link.sem, dve_link.next())
                        dve.wait_ge(up_hi.sem, up_hi.at(layer, f"up{i}"))
                        s = slice(2 * (i % 2), 2 * (i % 2) + 2)
                        v.tensor_tensor(y_lo[:, s, :], r2, y_hi[:, s, :].bitcast(F32), ALU.subtract).then_inc(up_lo.sem, up_lo.inc(f"up{i}"))
                dve.wait_ge(s_gain2, layer * 16 + 16)
                add_normed(layer, "mlp_r").then_inc(x_done.sem, x_done.inc("x"))
            assert dve_link.n == DVE_LINKS, dve_link.n

        @block.tensor
        def _(pe):
            mm = nc.tensor.matmul

            def open_bank(layer, job):
                if JOB[job] >= 4:
                    pe.wait_ge(job_read.sem, job_read.at(layer, JOBS[JOB[job] - 4]))
                return bank(job)

            def rows_changed(last):
                last.then_inc(pe_link.sem, 1)
                pe.wait_ge(pe_link.sem, pe_link.next())

            def turn(layer, job, blocks):
                b = open_bank(layer, job)
                for src, at in blocks:
                    n = src.shape[1]
                    ins = nc.tensor.transpose(b[0:n, at:at + P], src, ident)
                ins.then_inc(job_full.sem, job_full.inc(job))

            def turn_tokens(layer, prefix, src, n):
                for j in range(n):
                    turn(layer, f"{prefix}{j}", [(src[:, t, P * (2 * j + i):P * (2 * j + i) + P], SEQ * i + P * t)
                                                 for i in range(2) for t in range(T)])

            def split_product(dst, lhs, rhs, start, stop):
                mm(dst, lhs[1], rhs[0], start=start, stop=False)
                mm(dst, lhs[0], rhs[1], start=False, stop=False)
                return mm(dst, lhs[0], rhs[0], start=False, stop=stop)

            def pairs(hi, lo, *index):
                return hi[index], lo[index]

            def step(name, layer):
                if name == "mla_turn":
                    pe.wait_ge(dve_ready.sem, dve_ready.at(layer, "c_scaled"))
                    turn(layer, "cq", [(c[:, t, P * m:P * m + P], SEQ * m + P * t) for m in range(2) for t in range(T)])
                    pe.wait_ge(dve_ready.sem, dve_ready.at(layer, "k_rot"))
                    turn(layer, "ckv", [(c[:, t, 256:384], P * t) for t in range(T)]
                         + [(k_rot[:, t, :], SEQ + P * t) for t in range(T)])
                if name == "mla_q":
                    pe.wait_ge(job_read.sem, job_read.at(layer, "cq"))
                    pe.wait_ge(s_param, layer * (16 * n_params) + 16 * n_params)
                    b = open_bank(layer, "qpe")
                    heads_ = uq.rearrange("p k (h n) -> p k h n", h=8)
                    for t in range(T):
                        for k in range(2):
                            ins = mm(b[:, 256 * t:256 * t + 256], cT[:, k, P * t:P * t + P], heads_[:, k, :, 64:96],
                                     start=k == 0, stop=k == 1)
                    ins.then_inc(job_full.sem, job_full.inc("qpe"))
                    for j in range(4):
                        b = open_bank(layer, f"qn{j}")
                        for i in range(2):
                            for k in range(2):
                                ins = mm(b[0:64, SEQ * i:SEQ * i + SEQ], heads_[:, k, 2 * j + i, 0:64], cT[:, k, :],
                                         start=k == 0, stop=k == 1)
                        ins.then_inc(job_full.sem, job_full.inc(f"qn{j}"))
                if name == "mla_kv":
                    pe.wait_ge(job_read.sem, job_read.at(layer, "ckv"))
                    heads_ = ukv[:].rearrange("p (h n) -> p h n", h=8)
                    for j in range(4):
                        b = open_bank(layer, f"kn{j}")
                        for i in range(2):
                            ins = mm(b[0:64, SEQ * i:SEQ * i + SEQ], heads_[:, 2 * j + i, 0:64], cT[:, 2, :],
                                     start=True, stop=True)
                        ins.then_inc(job_full.sem, job_full.inc(f"kn{j}"))
                    for t in range(T):
                        b = open_bank(layer, f"v{t}")
                        mm(b, cT[:, 2, P * t:P * t + P], heads_[:, :, 64:128], start=True, stop=True).then_inc(job_full.sem, job_full.inc(f"v{t}"))
                if name == "mla_pe":
                    pe.wait_ge(dve_ready.sem, dve_ready.at(layer, "q_rot"))
                    turn(layer, "qpeT", [(q_rot[:, t, P * g:P * g + P], SEQ * g + P * t)
                                         for g in range(2) for t in range(T)])
                if name.startswith("mla_a"):
                    i = int(name[5:])
                    if i < NS:
                        t, h, n = SOFT[i]
                        w = P * (t + 1)
                        b = open_bank(layer, f"score{i}")
                        if i == 0:
                            pe.wait_ge(job_read.sem, job_read.at(layer, "qpeT"))
                        for k in range(n):
                            ins = mm(b[:, w * k:w * k + w], qT[0:96, h + k, P * t:P * t + P], kT[0:96, h + k, 0:w],
                                     start=True, stop=True)
                        ins.then_inc(job_full.sem, job_full.inc(f"score{i}"))
                    if 1 <= i <= NS:
                        pe.wait_ge(act_ready.sem, act_ready.at(layer, f"exp{i - 1}"))
                        turn(layer, f"turn{i - 1}", [(soft[:, (i - 1) % 2, P * k:P * k + P], P * k) for k in range(4)])
                    if i >= 2:
                        j = i - 2
                        t, h, n = SOFT[j]
                        b = open_bank(layer, f"pv{j}")
                        pe.wait_ge(job_read.sem, job_read.at(layer, f"turn{j}"))
                        for k in range(n):
                            for jt in range(t + 1):
                                at = P * (k * (t + 1) + jt)
                                ins = mm(b[:, 64 * k:64 * k + 64], probT[:, j % 2, at:at + P],
                                         v_mla[:, jt, 64 * (h + k):64 * (h + k) + 64], start=jt == 0, stop=jt == t)
                        ins.then_inc(job_full.sem, job_full.inc(f"pv{j}"))
                if name == "mla_y":
                    pe.wait_ge(job_read.sem, job_read.at(layer, f"pv{NS - 1}"))
                    turn_tokens(layer, "mla_y", o_mla, 2)
                if name == "ssd_cum":
                    pe.wait_ge(dve_ready.sem, dve_ready.at(layer, "log_decay"))
                    b = open_bank(layer, "cum")
                    for t in range(T):
                        mm(b[:, 8 * t:8 * t + 8], causal, log_decay[:, 8 * t:8 * t + 8], start=True, stop=True)
                    ins = mm(b[:, 16:24], causal[:, P - 1:P].broadcast_to((P, P)), log_decay[:, 0:8],
                             start=True, stop=True)
                    ins.then_inc(job_full.sem, job_full.inc("cum"))
                if name == "ssd_turn":
                    pe.wait_ge(pool_ready.sem, pool_ready.at(layer, "conv_silu"))
                    b = open_bank(layer, "G")
                    for t in range(T):
                        for g in range(2):
                            at = P * (2 * t + g)
                            ins = mm(b[:, at:at + P], conv[:, 4 + g, P * t:P * t + P], conv[:, 6 + g, P * t:P * t + P],
                                     start=True, stop=True)
                    ins.then_inc(job_full.sem, job_full.inc("G"))
                    for t in range(T):
                        turn(layer, f"xs{t}", [(conv[:, m, P * t:P * t + P], P * m) for m in range(4)])
                    turn(layer, "B", [(conv[:, 4 + g, 0:P], P * g) for g in range(2)])
                if name.startswith("ssd_decay"):
                    i = int(name[9:])
                    t, g = i // 2, i % 2
                    b = open_bank(layer, f"R{i}")
                    for k in range(4):
                        col = 8 * t + 4 * g + k
                        ins = mm(b[:, P * k:P * k + P], log_decay[:, col:col + 1].broadcast_to((P, P)), causal,
                                 start=True, stop=True)
                    ins.then_inc(job_full.sem, job_full.inc(f"R{i}"))
                if name == "ssd_state":
                    b = open_bank(layer, "S")
                    pe.wait_ge(dve_ready.sem, dve_ready.at(layer, "x_end"))
                    for g in range(2):
                        ins = mm(b[:, 256 * g:256 * g + 256], B_tok[:, g, :], x_end[:, 256 * g:256 * g + 256],
                                 start=True, stop=True)
                    ins.then_inc(job_full.sem, job_full.inc("S"))
                if name in ("ssd_y0", "ssd_y1"):
                    t = int(name[5])
                    if t == 1:
                        b = open_bank(layer, "off")
                        pe.wait_ge(job_read.sem, job_read.at(layer, "S"))
                        for g in range(2):
                            ins = mm(b[:, 256 * g:256 * g + 256], conv[:, 6 + g, P:2 * P],
                                     s_state[:, 256 * g:256 * g + 256], start=True, stop=True)
                        ins.then_inc(job_full.sem, job_full.inc("off"))
                    b = open_bank(layer, f"Y{t}")
                    pe.wait_ge(dve_ready.sem, dve_ready.at(layer, f"weights{2 * t + 1}"))
                    for h in range(8):
                        ins = mm(b[:, 64 * h:64 * h + 64], L[:, h, :], xdt[:, t, 64 * h:64 * h + 64],
                                 start=True, stop=True)
                    ins.then_inc(job_full.sem, job_full.inc(f"Y{t}"))
                if name in ("ssd_y", "ret_y", "gla_y"):
                    pe.wait_ge(dve_ready.sem, dve_ready.at(layer, f"{name[:3]}_out"))
                    turn_tokens(layer, name, {"ssd_y": sy, "ret_y": ry, "gla_y": gy}[name], 2)
                if name == "ret_turn":
                    pe.wait_ge(dve_ready.sem, dve_ready.at(layer, "r_scaled"))
                    for j, n in enumerate(("rq", "rk")):
                        turn(layer, n, [(rr[:, t, P * (2 * j + m):P * (2 * j + m) + P], SEQ * m + P * t)
                                        for m in range(2) for t in range(T)])
                if name in ("ret_s0", "ret_s1"):
                    t = int(name[5])
                    pe.wait_ge(job_read.sem, job_read.at(layer, "rk"))
                    b = open_bank(layer, f"rs{t}")
                    for h in (0, 2, 1, 3):
                        if h == 1:
                            rows_changed(ins)
                        r = slice(64 * (h % 2), 64 * (h % 2) + 64)
                        ins = mm(b[:, P * h:P * h + P], rT[r, 2 + h // 2, P * t:P * t + P],
                                 rT[r, h // 2, P * t:P * t + P], start=True, stop=True)
                    ins.then_inc(job_full.sem, job_full.inc(f"rs{t}"))
                    if t == 0:
                        pe.wait_ge(read_act.sem, read_act.at(layer, f"fill{FILLS.index(('token', 'rv', 1))}"))
                        b = open_bank(layer, "rS")
                        for h in range(4):
                            ins = mm(b[64 * (h % 2):64 * (h % 2) + 64, P * (h // 2):P * (h // 2) + P],
                                     rr[:, 0, 256 + 64 * h:320 + 64 * h], rv[:, 0, P * h:P * h + P],
                                     start=True, stop=True)
                        ins.then_inc(job_full.sem, job_full.inc("rS"))
                if name in ("ret_y0", "ret_y1"):
                    t = int(name[5])
                    b = open_bank(layer, f"rY{t}")
                    pe.wait_ge(job_read.sem, job_read.at(layer, f"rs{t}"))
                    for h in range(4):
                        o = slice(P * h, P * h + P)
                        ins = mm(b[:, o], rS[:, t, o], rv[:, t, o], start=h == 0, stop=t == 0, skip_group_check=True)
                    for h in (0, 2, 1, 3) if t == 1 else ():
                        if h == 1:
                            rows_changed(ins)
                        r = slice(64 * (h % 2), 64 * (h % 2) + 64)
                        ins = mm(b[:, P * h:P * h + P], rT[r, h // 2, P:2 * P], r_state[r, h // 2, :],
                                 start=False, stop=True, skip_group_check=True)
                    ins.then_inc(job_full.sem, job_full.inc(f"rY{t}"))
                if name == "gla_low":
                    turn(layer, "low", [(c[:, t, 424:440], P * t) for t in range(T)])
                if name == "gla_decay":
                    b = open_bank(layer, "gate")
                    pe.wait_ge(job_read.sem, job_read.at(layer, "low"))
                    for m in range(2):
                        ins = mm(b[:, SEQ * m:SEQ * m + SEQ], gk2[:, P * m:P * m + P], g_low, start=True, stop=True)
                    ins.then_inc(job_full.sem, job_full.inc("gate"))
                if name == "gla_turn":
                    pe.wait_ge(dve_ready.sem, dve_ready.at(layer, "k_end"))
                    turn(layer, "kst", [(g_end[:, m, P * t:P * t + P], 256 * t + P * m) for t in range(T) for m in range(2)])
                if name in ("gla_s0", "gla_s1"):
                    t = int(name[5])
                    b = open_bank(layer, f"gs{t}")
                    pe.wait_ge(dve_ready.sem, dve_ready.at(layer, "qk_in"))
                    for h in (0, 2, 1, 3):
                        if h == 1:
                            rows_changed(ins)
                        r = slice(64 * (h % 2), 64 * (h % 2) + 64)
                        ins = mm(b[:, P * h:P * h + P], gqk[r, 2 + h // 2, P * t:P * t + P],
                                 gqk[r, h // 2, P * t:P * t + P], start=True, stop=True)
                    ins.then_inc(job_full.sem, job_full.inc(f"gs{t}"))
                if name == "gla_state":
                    pe.wait_ge(job_read.sem, job_read.at(layer, "kst"))
                    pe.wait_ge(read_act.sem, read_act.at(layer, f"fill{FILLS.index(('token', 'gv', 1))}"))
                    for ch in range(3):
                        r, t = slice(64 * (ch % 2), 64 * (ch % 2) + 64), ch // 2
                        b = open_bank(layer, f"gS{ch}")
                        mm(b[:, 256:258], causal, causal[:, 0:2], start=True, stop=True)
                        for h in range(4):
                            ins = mm(b[64 * (h % 2):64 * (h % 2) + 64, P * (h // 2):P * (h // 2) + P],
                                     k_tok[r, t, 64 * h:64 * h + 64], gv[r, t, P * h:P * h + P],
                                     start=True, stop=True)
                        ins.then_inc(job_full.sem, job_full.inc(f"gS{ch}"))
                if name in ("gla_o0", "gla_o1"):
                    t = int(name[5])
                    b = open_bank(layer, f"gY{t}")
                    pe.wait_ge(job_read.sem, job_read.at(layer, "gS2"))
                    for h in (0, 2, 1, 3):
                        if h == 1:
                            rows_changed(ins)
                        for d in {0: (0, ), 2: (), 1: (1, 2, 3), 3: ()}[h]:
                            o = slice(P * d, P * d + P)
                            mm(b[:, o], gS[:, t, o], gv[:, t, o], start=d == 0, stop=False, skip_group_check=True)
                        r = slice(64 * (h % 2), 64 * (h % 2) + 64)
                        o = slice(P * h, P * h + P)
                        for ch in (2 * t, 2 * t + 1):
                            if ch:
                                ins = mm(b[64 * (ch % 2):64 * (ch % 2) + 64, o], gqk[r, h // 2, 64 * ch:64 * ch + 64],
                                         g_state[r, ch - 1, h // 2, :], start=False, stop=True, skip_group_check=True)
                    ins.then_inc(job_full.sem, job_full.inc(f"gY{t}"))

            with pe.Fori(0, DEPTH) as layer:
                pe_link.bind(layer)
                pe.wait_ge(dve_ready.sem, dve_ready.at(layer, "h_normed"))
                turn_tokens(layer, "h", normed, 4)
                pe.wait_ge(job_read.sem, job_read.at(layer, "h3"))
                f = 0
                for u in range(NU):
                    kind, name, i = UNITS[u]
                    if kind == "branch" and i == 0:
                        pe.wait_ge(job_read.sem, job_read.at(layer, f"{name}_y1"))
                    for half in range(2):
                        h = 2 * u + half
                        _, hi, lo = half_views(u, half)
                        w = (hi, lo)
                        if half:
                            pe.wait_ge(lo_odd.sem, lo_odd.at(layer, f"unit{u}"))
                        else:
                            pe.wait_ge(lo_even.sem, lo_even.at(layer, f"unit{u}"))
                        if kind in ("token", "channel", "gate", "branch"):
                            begins = half == 0 and i == 0 if kind == "token" else half == 0 or kind == "branch"
                            ends = half == 1 and i == 1 if kind == "token" else half == 1 or kind == "branch"
                            if begins and f >= 2:
                                wait_for_read(pe, layer, f - 2)
                            for b in range(2):
                                o = proj[:, 2 * (f % 2) + b, :]
                                for k in range(4 if kind in ("channel", "gate", "branch") else 2):
                                    if kind == "token":
                                        kk = 4 * i + 2 * half + k
                                        n = w[0].shape[2]
                                        ins = split_product(o[:, 0:n], (a_hi[:, kk, P * b:P * b + P], a_lo[:, kk, P * b:P * b + P]),
                                                            (hi[:, k, :], lo[:, k, :]), begins and k == 0, ends and k == 1)
                                    elif kind == "branch":
                                        ins = split_product(o[:, 0:SEQ], (hi[:, k, P * b:P * b + P], lo[:, k, P * b:P * b + P]),
                                                            (y_hi[:, k, :], y_lo[:, k, :]), k == 0, k == 3)
                                    else:
                                        kk = 4 * half + k
                                        ins = split_product(o[:, 0:SEQ], (hi[:, k, P * b:P * b + P], lo[:, k, P * b:P * b + P]),
                                                            (a_hi[:, kk, :], a_lo[:, kk, :]), begins and k == 0, ends and k == 3)
                            if ends:
                                f += 1
                        elif kind == "out":
                            if i == 0 and half == 0:
                                wait_for_read(pe, layer, NF - 2)
                                wait_for_read(pe, layer, NF - 1)
                            pe.wait_ge(merge_lo.sem, merge_lo.at(layer, f"m{i}"))
                            k = 2 * i + half
                            for t in range(T):
                                for n in range(2):
                                    ins = split_product(proj[:, 2 * t + n, :],
                                                        (a_hi[:, k, P * t:P * t + P], a_lo[:, k, P * t:P * t + P]),
                                                        (hi[:, 0, 512 * n:512 * n + 512], lo[:, 0, 512 * n:512 * n + 512]),
                                                        k == 0, k == 7)
                        elif kind == "up":
                            if i >= 2 and half == 0:
                                pe.wait_ge(up_read.sem, up_read.at(layer, f"up{i - 2}"))
                            for b in range(2):
                                for k in range(4):
                                    kk = 4 * half + k
                                    ins = split_product(mix[:, 2 * (i % 2) + b, 0:SEQ],
                                                        (hi[:, k, P * b:P * b + P], lo[:, k, P * b:P * b + P]),
                                                        (a_hi[:, kk, :], a_lo[:, kk, :]), kk == 0, kk == 7)
                        else:
                            if half == 0:
                                pe.wait_ge(up_lo.sem, up_lo.at(layer, f"up{i}"))
                            k = 2 * (i % 2) + half
                            for t in range(T):
                                for n in range(2):
                                    ins = split_product(proj[:, 2 * t + n, :],
                                                        (y_hi[:, k, P * t:P * t + P], y_lo[:, k, P * t:P * t + P]),
                                                        (hi[:, 0, 512 * n:512 * n + 512], lo[:, 0, 512 * n:512 * n + 512]),
                                                        h == 2 * AT[("down", "down", 0)], h == 2 * NU - 1)
                        ins.then_inc(half_done.sem, half_done.inc(f"half{h}"))
                    for s in STEPS.get(u, []):
                        step(s, layer)
                    if kind == "out" and i == 3:
                        pe.wait_ge(dve_ready.sem, dve_ready.at(layer, "u_normed"))
                        turn_tokens(layer, "u", normed, 4)
                        pe.wait_ge(job_read.sem, job_read.at(layer, "u3"))
            assert pe_link.n == PE_LINKS, pe_link.n


def kernel(**inputs):
    import concourse.bacc as bacc
    from concourse.bass_utils import run_bass_kernel_spmd

    def by_channel(name):
        a = np.asarray(inputs[name])
        return a.reshape(DEPTH, -1, P).transpose(0, 2, 1)

    arrays = {
        "x": inputs["x"], "positions": np.asarray(inputs["positions"]).reshape(T, P).T, "w_in": inputs["w_in"],
        "w_branch": np.asarray(inputs["w_branch"]).reshape(DEPTH, 4 * 512, D),
        "w_out": inputs["w_out"], "w_up": inputs["w_mlp_in"], "w_down": inputs["w_mlp_out"],
        "w_uq": inputs["mla_w_uq"], "w_ukv": inputs["mla_w_ukv"], "w_gk2": inputs["gla_w_gk2"],
        "chan_in": np.concatenate([by_channel(n) for n in (
            "norm_pre_mix", "norm_pre_mlp", "ssd_conv_w", "ssd_conv_b", "b_gate", "gla_b_gk",
            "mla_q_norm", "mla_kv_norm", "ssd_norm", "ret_norm", "gla_norm")], 2),
        "rows_in": np.concatenate([np.asarray(inputs[n]) for n in (
            "norm_post_mix", "norm_post_mlp", "ssd_dt_bias", "ssd_a_log", "ssd_d")], 1),
        "const_in": constants(),
    }
    nc = bacc.Bacc("TRN2", target_bir_lowering=False, num_devices=1)
    arrays = {f"in_{n}": np.ascontiguousarray(a) for n, a in arrays.items()}
    args = [nc.dram_tensor(n, a.shape, mybir.dt.from_np(a.dtype), kind="ExternalInput").ap()
            for n, a in arrays.items()]
    out = nc.dram_tensor("out", (1, SEQ, D), F32, kind="ExternalOutput").ap()
    hybrid_trunk(nc, *args, out)
    got = run_bass_kernel_spmd(nc, [arrays], core_ids=[0])
    return got.results[0]["out"]
```

```python
from contextlib import ExitStack

import numpy as np
import concourse.bass as bass
from concourse import mybir

F32 = mybir.dt.float32
F32R = mybir.dt.float32r
I32 = mybir.dt.int32
ALU = mybir.AluOpType
ACT = mybir.ActivationFunctionType
X_AXIS = mybir.AxisListType.X

P = 128
DEPTH, SEQ, D = 2, 256, 1024
T = SEQ // P
KT = D // P
EPS = 1e-6
PI = 3.1415925

WIDTHS = dict(z=512, xbc=1024, dt=8, rqk=512, rv=512, rg=512, cq=256, ckv=128, kr=32,
              gqk=512, gv=512, ggk=16, gg=512, gates=4 * D)
COL = {}
for _name, _w in WIDTHS.items():
    COL[_name] = sum(WIDTHS[k] for k in list(WIDTHS)[:list(WIDTHS).index(_name)])
IN_WIDTH = sum(WIDTHS.values())
BRANCHES = ("ssd", "ret", "mla", "gla")
FF = 4 * D
ROPE = 32
LN_EXP = "natural_log_exp_and_others"

C_PARTS = ("cq", "ckv", "kr", "dt", "ggk")
C_AT = {n: sum(WIDTHS[k] for k in C_PARTS[:i]) for i, n in enumerate(C_PARTS)}
C_WIDTH = sum(WIDTHS[k] for k in C_PARTS)


def units():
    def rows(name):
        return [("token", name, i) for i in range(2)]

    def cols(name, n):
        return [("channel", name, i) for i in range(n)]

    def gates(b):
        return [("gate", b, i) for i in range(4)]

    def branch(b):
        return [("branch", b, i) for i in range(2)]

    u = rows("c") + cols("xbc", 4) + rows("z") + rows("rqk") + gates("mla") + rows("rv") + rows("rg")
    u += branch("mla") + gates("ssd") + cols("gqk", 2) + rows("gv") + rows("gg") + branch("ssd")
    u += gates("ret") + branch("ret") + gates("gla") + branch("gla")
    u += [("out", "out", i) for i in range(4)]
    for j in range(17):
        u += [("up", "up", j)] if j < 16 else []
        u += [("down", "down", j - 1)] if j >= 1 else []
    return u


UNITS = units()
NU = len(UNITS)
AT = {(k, n, i): p for p, (k, n, i) in enumerate(UNITS)}
RAW = 4
HL = 4
AHEAD = 2
IN_TWO = (("token", "z", 0), ("branch", "ssd", 0))
assert NU % RAW == 0 and 2 * NU % HL == 0

BY_HALVES = ((0, 0), (0, 1), (1, 0), (1, 1))
BY_TILES = ((0, 0), (1, 0), (0, 1), (1, 1))
ORDER = {AT[("token", "c", 0)]: BY_TILES, AT[("out", "out", 0)]: ((0, 1), (1, 1), (0, 0), (1, 0)),
         AT[("out", "out", 3)]: BY_TILES, AT[("down", "down", 15)]: BY_TILES}

FILLS, FILL_ENDS = [], []
for _u, (_kind, _name, _i) in enumerate(UNITS):
    if _kind == "token" and _i == 1 or _kind in ("channel", "gate"):
        FILLS.append((_kind, _name, _i))
        FILL_ENDS.append(2 * _u + 1)
    if _kind == "branch":
        FILLS += [(_kind, _name, 2 * _i), (_kind, _name, 2 * _i + 1)]
        FILL_ENDS += [2 * _u, 2 * _u + 1]
NF = len(FILLS)
LATE = ("ret", "gla")
assert NF % 2 == 1
READ_BY_ACT = [f[0] != "branch" for f in FILLS]

SOFT = [(0, 0, 4), (0, 4, 4), (1, 0, 2), (1, 2, 2), (1, 4, 2), (1, 6, 2)]
NS = len(SOFT)

STEPS = {
    1: ["mla_norm"], 2: ["mla_turn"], 3: ["mla_q"], 4: ["mla_kv"], 5: ["mla_pe"],
    6: ["mla_a0"], 7: ["mla_a1"], 8: ["mla_a2", "conv0"], 9: ["mla_a3", "ssd_dt", "conv1"],
    10: ["mla_a4", "ssd_log", "conv2"], 11: ["mla_a5", "ssd_cum", "conv3"], 12: ["mla_a6", "conv4"],
    13: ["mla_a7", "conv5"], 14: ["conv6", "mla_y"], 15: ["conv7"],
    16: ["ssd_gate"], 17: ["z_gate", "mla_gate", "ret_rope"],
    18: ["ret_gate", "ssd_turn"], 19: ["ssd_decay0"], 20: ["ssd_decay1", "ssd_state"],
    21: ["ssd_y0"], 22: ["ssd_decay2"], 23: ["ssd_decay3", "gla_low"], 24: ["ssd_y1", "ssd_gated", "ret_turn"],
    25: ["gla_decay", "ssd_norm"], 26: ["ssd_scale", "gla_sum", "ret_s0"], 27: ["ssd_y", "ret_s1"],
    28: ["ret_y0", "gla_scale"], 29: ["ret_y1", "gla_turn", "ssd_gates"], 30: ["ret_norm", "gla_s0"],
    31: ["ret_scale", "gla_s1"], 32: ["gla_state"],
    33: ["ret_y", "gla_o0"], 34: ["gla_o1"], 35: ["gla_gate"], 36: ["gla_norm"], 37: ["gla_scaled"], 38: ["gla_y"],
}
JOBS_OF = {
    "mla_turn": ["cq", "ckv"], "mla_q": ["qpe", "qn0", "qn1"],
    "mla_kv": ["kn0", "kn1", "v0", "v1"], "mla_pe": ["qpeT"],
    "mla_y": ["mla_y0", "mla_y1"],
    "ssd_cum": ["cum"], "ssd_turn": ["G", "xs0", "xs1", "B"],
    "ssd_decay0": ["R0"], "ssd_decay1": ["R1"], "ssd_decay2": ["R2"], "ssd_decay3": ["R3"],
    "ssd_state": ["S"], "ssd_y0": ["Y0"], "ssd_y1": ["off", "Y1"], "ssd_y": ["ssd_y0", "ssd_y1"],
    "ret_turn": ["rq", "rk"], "ret_s0": ["rs0", "rS"], "ret_s1": ["rs1"], "ret_y0": ["rY0"],
    "ret_y1": ["rY1"], "ret_y": ["ret_y0", "ret_y1"],
    "gla_low": ["low"], "gla_decay": ["gate"], "gla_turn": ["kst"], "gla_s0": ["gs0"],
    "gla_s1": ["gs1"], "gla_state": ["gS0", "gS1", "gS2"], "gla_o0": ["gY0"], "gla_o1": ["gY1"],
    "gla_y": ["gla_y0", "gla_y1"],
}
for _i in range(NS + 2):
    JOBS_OF[f"mla_a{_i}"] = ([f"score{_i}"] if _i < NS else []) \
        + ([f"turn{_i - 1}"] if 1 <= _i <= NS else []) + ([f"pv{_i - 2}"] if _i >= 2 else [])
JOBS = ["h00", "h01", "h10", "h11"]
for _u in range(NU):
    for _s in STEPS.get(_u, []):
        JOBS += JOBS_OF.get(_s, [])
JOBS += ["u00", "u01", "u10", "u11"]
NJ = len(JOBS)
JOB = {n: i for i, n in enumerate(JOBS)}
TURNED = [j for j in JOBS if j[0] in "hu" and len(j) == 3 or j[:5] in ("ssd_y", "ret_y", "mla_y", "gla_y")]

CHAN = {}
_at = 0
for _n, _w in (("pre_mix", 8), ("pre_mlp", 8), ("conv_w", 32), ("conv_b", 8), ("b_gate", 32),
               ("gla_b", 2), ("q_norm", 2), ("kv_norm", 1), ("ssd", 4), ("ret", 4), ("gla", 4)):
    CHAN[_n] = _at
    _at += _w
N_CHAN = _at
CONST = {}
_at = 0
for _n, _w in (("ident", P), ("causal", P), ("block", P), ("neg", 2 * P), ("restart", SEQ),
               ("freq", ROPE), ("ret_scale", 8), ("ret_total", 2), ("eps", 1), ("one", 1), ("ln_1/D", 1)):
    CONST[_n] = _at
    _at += _w
N_CONST = _at


def constants():
    c = np.zeros((P, N_CONST), np.float64)

    def put(name, a):
        c[:, CONST[name]:CONST[name] + a.shape[1]] = a

    i = np.arange(P)
    put("ident", np.eye(P))
    put("causal", (i[:, None] <= i[None, :]) * 1.0)
    put("block", ((i[:, None] <= i[None, :]) & (i[:, None] // 64 == i[None, :] // 64)) * 1.0)
    put("neg", np.concatenate([np.zeros((P, P)), (i[None, :] > i[:, None]) * -1e30], 1))
    put("restart", np.tile((np.arange(SEQ) % 64 != 0) * 1.0, (P, 1)))
    put("freq", np.tile(10000.0 ** (-np.arange(ROPE) / ROPE), (P, 1)))
    log_gamma = np.log1p(-np.exp2(-5.0 - np.arange(4)))
    cum = (i[:, None] + 1) * log_gamma[None, :]
    put("ret_scale", np.concatenate([np.exp(cum), np.exp(-cum) * 64 ** -0.5], 1))
    put("ret_total", np.exp(P * log_gamma)[2 * np.arange(2)[None, :] + (i[:, None] // 64)])
    put("eps", np.full((P, 1), EPS))
    put("one", np.ones((P, 1)))
    put("ln_1/D", np.full((P, 1), -np.log(D)))
    return c.astype(np.float32)


class Signal:

    def __init__(self, semaphore, events, start=0):
        self.sem, self.start, self.per = semaphore, start, len(events)
        self.order = list(events)
        self.number = {e: i + 1 for i, e in enumerate(events)}
        self.marked = 0

    def inc(self, event):
        assert self.order[self.marked] == event, (self.order[self.marked], event)
        self.marked += 1
        return 1

    def at(self, layer, event):
        return layer * self.per + (self.start + self.number[event])

    def at_number(self, layer, number):
        return layer * self.per + (self.start + number)


class Chain:

    def __init__(self, semaphore, per):
        self.sem, self.per, self.n = semaphore, per, 0

    def bind(self, layer):
        self.layer = layer

    def next(self):
        self.n += 1
        return self.layer * self.per + self.n


ACT_LINKS = 27
DVE_LINKS = 84
PE_LINKS = 7
V_EVENTS = """
h_normed0 h_normed1 pad c_scaled k_rot q_rot shifted0 shifted1 shifted2 conv0 shifted3 dt_x conv1
shifted4 dt_w log_decay conv2 shifted5 cum conv3 conv4 conv5 conv6 conv7 r_scaled xdt x_end
mla_merged seg0 weights0 seg1 weights1 seg2 weights2 seg3 weights3 ssd_summed gate_n ssd_squared
ssd_out g_cum k_end qk_in gS_zero ret_squared ret_gated ssd_merged ret_out gla_squared gla_gated
ret_merged gla_out x_mixed00 x_mixed01 x_mixed10 x_mixed11
""".split()
A_EVENTS = """
h_r0 h_r1 mla_r exp0 exp1 exp2 tap0 exp3 dt_u tap1 exp4 dt_ln tap2 exp5 tap3 tap4 tap5 tap6 tap7
conv_sigmoid z_sigmoid mla_gates rg_sigmoid ends decay0 decay1 decay2 decay3 gate_ln ssd_r g_exps
ssd_gates ret_r gg_sigmoid gla_r mix_r0 mix_r1 mlp_r0 mlp_r1
""".split()
G_EVENTS = """
conv_silu z_silu rg_silu ssd_gated gg_silu
""".split()


def hybrid_trunk(nc, x, positions, w_in, w_branch, w_out, w_up, w_down, w_uq, w_ukv, w_gk2,
                 chan_in, rows_in, const_in, out):
    with ExitStack() as ctx:
        def sb(name, shape, dt=F32):
            return ctx.enter_context(nc.sbuf_tensor(name, shape, dt))

        def sem(name):
            return ctx.enter_context(nc.semaphore(name))

        raw = sb("raw", [P, RAW, 2048])
        w_hi = sb("w_hi", [P, HL, 1024], F32R)
        w_lo = sb("w_lo", [P, HL, 1024], F32R)
        xs_res = sb("x_res", [P, T, D])
        a_hi = sb("a_hi", [P, KT, SEQ], F32R)
        a_lo = sb("a_lo", [P, KT, SEQ], F32R)
        merged = sb("merged", [P, KT, SEQ])
        gates = sb("gates", [P, 8, SEQ])
        y_hi = sb("y_hi", [P, 4, SEQ], F32R)
        y_lo = sb("y_lo", [P, 4, SEQ], F32R)
        post_gain = sb("post_gain", [P, D])
        head_rows = sb("head_rows", [P, 24])
        chan = sb("chan", [P, N_CHAN])
        ukv = sb("ukv", [P, D])
        gk2 = sb("gk2", [16, 256])
        const = sb("const", [P, N_CONST])
        trig = sb("trig", [P, 2, T, ROPE])
        c = sb("c", [P, T, C_WIDTH])
        rqk = sb("rqk", [P, T, 512])
        stat = sb("stat", [P, 128])
        pos_i = sb("pos_i", [P, T], I32)
        R1 = sb("region_1", [P, 8256])
        R2 = sb("region_2", [P, 10300])
        uq = gates[:, 0:6, :].rearrange("p a b -> p (a b)").rearrange("p (k n) -> p k n", k=2)

        def part(region, at, *dims):
            n = int(np.prod(dims))
            v = region[:, at:at + n]
            if len(dims) == 2:
                v = v.rearrange("p (a b) -> p a b", a=dims[0])
            if len(dims) == 3:
                v = v.rearrange("p (a b c) -> p a b c", a=dims[0], b=dims[1])
            return v

        normed = part(R1, 0, T, D)
        update = part(R1, 0, T, D)
        square_out = part(R2, 0, T, D)
        c_square_out = part(R2, 2072, T, 512)
        qT = part(R1, 0, 8, SEQ)
        kT = part(R1, 2048, 8, SEQ)
        v_mla = part(R1, 4096, T, 512)
        o_mla = part(R1, 5120, T, 512)
        soft = part(R1, 6144, 2, 512)
        q_pe = part(R1, 6144, T, 256)
        q_rot = part(R1, 6656, T, 256)
        probT = part(R1, 7168, 2, 512)
        cT = part(R1, 7168, 3, SEQ)
        k_rot = part(R1, 7936, T, 32)
        rot_a = part(R1, 4096, 512)
        rot_b = part(R1, 4608, 512)
        rv = part(R1, 0, T, 512)
        rg = part(R1, 1024, T, 512)
        rg_s = part(R1, 2048, T, 512)
        rr = part(R1, 3072, T, 512)
        rT = part(R1, 4096, 4, SEQ)
        rS = part(R1, 5120, T, 512)
        r_rot_a = part(R1, 5120, 512)
        r_rot_b = part(R1, 5632, 512)
        ry = part(R1, 6144, T, 512)
        r_state = part(R1, 7168, 2, P)
        xbc = part(R2, 0, 8, SEQ + 3)
        xbc_s = part(R2, 0, 8, SEQ)
        xs = part(R2, 0, T, 512)
        xdt = part(R2, 1024, T, 512)
        conv = part(R2, 2072, 8, SEQ)
        z = part(R2, 4120, T, 512)
        B_tok = part(R2, 5144, 2, P)
        x_end = part(R2, 5400, 512)
        L = part(R2, 5912, 8, P)
        z_s = part(R2, 5912, T, 512)
        s_state = part(R2, 6936, 512)
        sy = part(R2, 7448, T, 512)
        G = part(R2, 8472, 4, P)
        s_tmp = part(R2, 8984, 512)
        cum_keep = part(R2, 9496, 16)
        log_decay = part(R2, 9512, 16)
        w1 = part(R2, 9528, 16)
        gqk = rqk[:].rearrange("p t (a n) -> p (t a) n", n=SEQ)
        gv = part(R2, 1024, T, 512)
        gg = part(R2, 2072, T, 512)
        gg_s = part(R2, 3096, T, 512)
        k_tok = part(R2, 4120, T, 256)
        g_cum = part(R2, 5144, 2, SEQ)
        g_e = part(R2, 5656, 2, SEQ)
        g_ei = part(R2, 6168, 2, SEQ)
        g_end = part(R2, 6680, 2, SEQ)
        gS = part(R2, 7448, T, 512)
        gy = part(R2, 8472, T, 512)
        g_state = part(R2, 9496, 3, 2, P)
        g_low = R2[0:16, 9496:9752]
        relu = part(R2, 0, 2, 512)
        relu2 = part(R2, 1024, 2, 512)

        def cst(name, n):
            return const[:, CONST[name]:CONST[name] + n]

        ident, causal = cst("ident", P), cst("causal", P)

        proj = ctx.enter_context(nc.psum_tensor("proj", [P, 4, 512], F32))
        mix = ctx.enter_context(nc.psum_tensor("mix", [P, 4, 512], F32))

        def bank(job):
            return mix[:, JOB[job] % 4, :]

        def chan_col(name, i, n=1):
            return chan[:, CHAN[name] + i:CHAN[name] + i + n]

        landed = [sem(f"weights_landed_{i}") for i in range(RAW)]
        s_input = sem("inputs_landed")
        s_x = [sem(f"x_landed_{t}") for t in range(T)]
        s_param = sem("parameters_landed")
        s_chan = sem("channel_parameters_landed")
        params_used = Signal(sem("parameters_used"), ["all"], start=1)
        s_gain2 = sem("mlp_gain_landed")
        s_stored = sem("output_stored")
        halves = [f"half{i}" for i in range(2 * NU)]
        hi_made = Signal(sem("hi_made"), halves)
        lo_even = Signal(sem("lo_even_made"), [f"unit{i}" for i in range(NU)], start=RAW)
        lo_odd = Signal(sem("lo_odd_made"), [f"unit{i}" for i in range(NU)], start=RAW)
        half_done = Signal(sem("half_done"), halves, start=HL)
        read_act = Signal(sem("projection_read_by_act"), [f"fill{i}" for i in range(NF) if READ_BY_ACT[i]])
        read_dve = Signal(sem("projection_read_by_dve"), [f"fill{i}" for i in range(NF) if not READ_BY_ACT[i]])
        job_full = Signal(sem("mix_job_full"), JOBS)
        job_read = Signal(sem("mix_job_read"), JOBS)
        turned_hi = Signal(sem("turned_hi"), TURNED)
        x_done = Signal(sem("x_done"), ["x0", "x1"], start=2)
        tile_done = Signal(sem("first_tile_done"), ["out", "down"])
        up_read = Signal(sem("up_read"), [f"up{i}" for i in range(16)])
        up_hi = Signal(sem("up_hi"), [f"up{i}" for i in range(16)])
        up_lo = Signal(sem("up_lo"), [f"up{i}" for i in range(16)])
        merge_hi = Signal(sem("merge_hi"), [f"m{i}" for i in range(4)])
        merge_lo = Signal(sem("merge_lo"), [f"m{i}" for i in range(4)])
        merge_sum = Signal(sem("merge_summed"), [f"m{i}" for i in range(4)])
        dve_ready = Signal(sem("dve_ready"), V_EVENTS)
        act_ready = Signal(sem("act_ready"), A_EVENTS)
        pool_ready = Signal(sem("pool_ready"), G_EVENTS)
        act_link = Chain(sem("act_link"), ACT_LINKS)
        dve_link = Chain(sem("dve_link"), DVE_LINKS)
        pe_link = Chain(sem("pe_link"), PE_LINKS)
        s_rope = sem("rope_tables")
        s_rope_act = sem("rope_sines")
        s_pre = sem("rope_steps")
        n_params = 5

        block = ctx.enter_context(nc.Block())

        def unit_parts(u, layer):
            kind, name, i = UNITS[u]
            slot = raw[:, u % RAW, :]
            lay = bass.ds(layer, 1)
            if kind == "token" and name == "c":
                dst = slot[:, 0:4 * C_WIDTH].rearrange("p (k n) -> p k n", k=4)
                got = []
                for first, last in (("cq", "kr"), ("dt", "dt"), ("ggk", "ggk")):
                    a, w = C_AT[first], C_AT[last] + WIDTHS[last] - C_AT[first]
                    src = w_in[lay, 512 * i:512 * i + 512, COL[first]:COL[first] + w]
                    got.append((dst[:, :, a:a + w], src.rearrange("o (k p) n -> p (o k) n", p=P)))
                return got
            if kind == "token":
                src = w_in[lay, 512 * i:512 * i + 512, COL[name]:COL[name] + 512]
                k, n = 4, 512
            elif kind in ("channel", "gate"):
                at = COL[name] if kind == "channel" else COL["gates"] + BRANCHES.index(name) * D
                src = w_in[lay, :, at + 256 * i:at + 256 * i + 256]
                k, n = 8, 256
            elif kind == "branch":
                at = 512 * BRANCHES.index(name)
                src = w_branch[lay, at:at + 512, 512 * i:512 * i + 512]
                k, n = 4, 512
            elif kind == "up":
                src = w_up[lay, :, 256 * i:256 * i + 256]
                k, n = 8, 256
            else:
                src = (w_out if kind == "out" else w_down)[lay, 256 * i:256 * i + 256, :]
                k, n = 2, D
            dst = slot[:, 0:k * n].rearrange("p (k n) -> p k n", k=k)
            src = src.rearrange("o (k p) n -> p (o k) n", p=P)
            if (kind, name, i) in IN_TWO:
                return [(dst[:, 1:k], src[:, 1:k]), (dst[:, 0:1], src[:, 0:1])]
            return [(dst, src)]

        def n_dmas(u):
            return 3 if UNITS[u][:2] == ("token", "c") else 2 if UNITS[u] in IN_TWO else 1

        def landed_count(u):
            return 16 * sum(n_dmas(v) for v in range(u % RAW, u + 1, RAW))

        def half_views(u, half):
            kind, name, i = UNITS[u]
            if kind == "token":
                k, n = 4, C_WIDTH if name == "c" else 512
            elif kind == "branch":
                k, n = 4, 512
            elif kind in ("out", "down"):
                k, n = 2, D
            else:
                k, n = 8, 256
            src = raw[:, u % RAW, 0:k * n].rearrange("p (k n) -> p k n", k=k)
            if kind == "branch":
                src, n = src[:, :, 256 * half:256 * half + 256], 256
            else:
                k //= 2
                src = src[:, k * half:k * half + k, :]
            s = (2 * u + half) % HL
            hi, lo = (w[:, s, 0:k * n].rearrange("p (k n) -> p k n", k=k) for w in (w_hi, w_lo))
            return src, hi, lo

        def wait_for_products(engine, layer, kind, name, i, half=1):
            engine.wait_ge(half_done.sem, half_done.at(layer, f"half{2 * AT[(kind, name, i)] + half}"))

        def wait_for_read(engine, layer, f):
            if READ_BY_ACT[f]:
                engine.wait_ge(read_act.sem, read_act.at(layer, f"fill{f}"))
            else:
                engine.wait_ge(read_dve.sem, read_dve.at(layer, f"fill{f}"))

        fills_of = {}
        for f, (kind, name, i) in enumerate(FILLS):
            u = AT[(kind, name, i // 2 if kind == "branch" else i)]
            fills_of.setdefault(u, []).append(f)

        @block.sync
        def _(sp):
            sp.dma_start(pos_i[:], positions).then_inc(s_input, 16)
            sp.dma_start(const[:], const_in).then_inc(s_input, 16)
            for t in range(T):
                sp.dma_start(xs_res[:, t, :], x[0, P * t:P * t + P, :]).then_inc(s_x[t], 16)
            with sp.Fori(0, DEPTH) as layer:
                for u in range(NU):
                    sp.wait_ge(lo_odd.sem, lo_odd.at_number(layer, u + 1 - RAW))
                    for dst, src in unit_parts(u, layer):
                        sp.dma_start(dst, src).then_inc(landed[u % RAW], 16)
            for t in range(T):
                sp.wait_ge(x_done.sem, x_done.at(DEPTH - 1, f"x{t}"))
                sp.dma_start(out[0, P * t:P * t + P, :], xs_res[:, t, :]).then_inc(s_stored, 16)
            sp.wait_ge(s_stored, 16 * T)

        @block.gpsimd
        def _(pool):
            def lo_half(layer, u):
                src, hi, lo = half_views(u, 1)
                pool.wait_ge(hi_made.sem, hi_made.at(layer, f"half{2 * u + 1}"))
                pool.wait_ge(lo_even.sem, lo_even.at(layer, f"unit{u}"))
                nc.gpsimd.tensor_tensor(lo, src, hi.bitcast(F32), ALU.subtract).then_inc(lo_odd.sem, lo_odd.inc(f"unit{u}"))

            def step(name, layer):
                if name == "ssd_gate":
                    pool.wait_ge(act_ready.sem, act_ready.at(layer, "conv_sigmoid"))
                    pool.wait_ge(dve_ready.sem, dve_ready.at(layer, "conv7"))
                    nc.gpsimd.tensor_tensor(conv, conv, xbc_s, ALU.mult).then_inc(pool_ready.sem, pool_ready.inc("conv_silu"))
                if name == "z_gate":
                    pool.wait_ge(act_ready.sem, act_ready.at(layer, "z_sigmoid"))
                    nc.gpsimd.tensor_tensor(z, z, z_s, ALU.mult).then_inc(pool_ready.sem, pool_ready.inc("z_silu"))
                if name == "ssd_gated":
                    pool.wait_ge(dve_ready.sem, dve_ready.at(layer, "ssd_summed"))
                    pool.wait_ge(pool_ready.sem, pool_ready.at(layer, "z_silu"))
                    nc.gpsimd.tensor_tensor(sy, sy, z, ALU.mult).then_inc(pool_ready.sem, pool_ready.inc("ssd_gated"))
                if name == "ret_gate":
                    pool.wait_ge(act_ready.sem, act_ready.at(layer, "rg_sigmoid"))
                    nc.gpsimd.tensor_tensor(rg, rg, rg_s, ALU.mult).then_inc(pool_ready.sem, pool_ready.inc("rg_silu"))
                if name == "gla_gate":
                    pool.wait_ge(act_ready.sem, act_ready.at(layer, "gg_sigmoid"))
                    nc.gpsimd.tensor_tensor(gg, gg, gg_s, ALU.mult).then_inc(pool_ready.sem, pool_ready.inc("gg_silu"))

            pool.dma_start(chan[:], chan_in[0]).then_inc(s_chan, 16)
            with pool.Fori(0, DEPTH) as layer:
                pool.wait_ge(params_used.sem, params_used.at_number(layer, 0))
                lay = bass.ds(layer, 1)
                pool.dma_start(uq, w_uq[lay].rearrange("o (k p) n -> p (o k) n", p=P)).then_inc(s_param, 16)
                pool.dma_start(ukv[:], w_ukv[lay].rearrange("o p n -> p (o n)")).then_inc(s_param, 16)
                pool.dma_start(gk2[:], w_gk2[lay].rearrange("o p n -> p (o n)")).then_inc(s_param, 16)
                pool.dma_start(post_gain[:], rows_in[lay, 0:D].partition_broadcast(P)
                               .rearrange("p o n -> p (o n)")).then_inc(s_param, 16)
                pool.dma_start(head_rows[:], rows_in[lay, 2 * D:2 * D + 24].partition_broadcast(P)
                               .rearrange("p o n -> p (o n)")).then_inc(s_param, 16)
                lo_half(layer, 0)
                for u in range(NU):
                    if u + 1 < NU:
                        lo_half(layer, u + 1)
                    for name in STEPS.get(u, []):
                        step(name, layer)
                    if u == AT[("up", "up", 2)]:
                        pool.wait_ge(dve_ready.sem, dve_ready.at(layer, "x_mixed11"))
                        pool.dma_start(post_gain[:], rows_in[lay, D:2 * D].partition_broadcast(P)
                                       .rearrange("p o n -> p (o n)")).then_inc(s_gain2, 16)
                        pool.wait_ge(job_read.sem, job_read.at(layer, "u11"))
                        pool.dma_start(chan[:], chan_in[bass.ds(layer + 1, 1)].rearrange("o p n -> p (o n)")).then_inc(
                            s_chan, 16)

        @block.scalar
        def _(act):
            def run(out_, in_, func=ACT.Copy, **kw):
                return nc.scalar.activation(out_, in_, func, **kw)

            def hi_half(layer, h):
                u, half = h // 2, h % 2
                src, hi, _ = half_views(u, half)
                total = landed_count(NU - RAW + u % RAW)
                if half == 0:
                    act.wait_ge(landed[u % RAW], layer * total + landed_count(u))
                act.wait_ge(half_done.sem, half_done.at_number(layer, h + 1 - HL))
                run(hi, src).then_inc(hi_made.sem, hi_made.inc(f"half{h}"))

            def turn_hi_tile(layer, name, t, gain):
                for q in range(2):
                    act.wait_ge(job_full.sem, job_full.at(layer, f"{name}{t}{q}"))
                    for i in range(4):
                        ins = run(a_hi[:, 4 * q + i, P * t:P * t + P], bank(f"{name}{t}{q}")[:, P * i:P * i + P],
                                  scale=chan_col(gain, 4 * q + i))
                    ins.then_inc(turned_hi.sem, turned_hi.inc(f"{name}{t}{q}"))

            def squares(src, col, junk=square_out):
                run(junk[:, col % 2, :] if len(src.shape) == 2 else
                    junk[:, col % 2, :].rearrange("p (a b) -> p a b", a=2), src, ACT.Square,
                    accum_out=stat[:, col:col + 1]).then_inc(act_link.sem, 1)
                act.wait_ge(act_link.sem, act_link.next())

            def turn_hi(layer, name, dst, gain):
                act.wait_ge(job_full.sem, job_full.at(layer, name))
                for i in range(2):
                    src = bank(name)[:, SEQ * i:SEQ * i + SEQ]
                    ins = run(dst[:, i, :], src, scale=gain[i]) if gain else run(dst[:, i, :], src)
                ins.then_inc(turned_hi.sem, turned_hi.inc(name))

            def rsqrt(dst, src, width):
                run(dst, src, ACT.Ln, scale=1.0 / width, bias=cst("eps", 1)).then_inc(act_link.sem, 1)
                act.wait_ge(act_link.sem, act_link.next())
                return run(dst, dst, ACT.Exp, scale=-0.5)

            def read(layer, f):
                kind, name, i = FILLS[f]
                act.wait_ge(half_done.sem, half_done.at(layer, f"half{FILL_ENDS[f]}"))
                pair = proj[:, 2 * (f % 2):2 * (f % 2) + 2, :]
                if kind == "token":
                    width = C_WIDTH if name == "c" else 512
                    dst = {"c": c[:], "z": z, "rqk": rqk[:], "rv": rv, "rg": rg, "gv": gv, "gg": gg}[name]
                    if name == "rv":
                        act.wait_ge(job_read.sem, job_read.at(layer, "mla_y1"))
                    if name == "gv":
                        act.wait_ge(dve_ready.sem, dve_ready.at(layer, "ssd_summed"))
                    run(dst, pair[:, :, 0:width]).then_inc(read_act.sem, read_act.inc(f"fill{f}"))
                elif kind == "channel":
                    dst = xbc[:, 2 * i:2 * i + 2, 3:SEQ + 3] if name == "xbc" else gqk[:, 2 * i:2 * i + 2, :]
                    if name == "gqk" and i == 0:
                        act.wait_ge(dve_ready.sem, dve_ready.at(layer, "r_scaled"))
                    run(dst, pair[:, :, 0:SEQ]).then_inc(read_act.sem, read_act.inc(f"fill{f}"))
                else:
                    if name == "mla" and i == 0:
                        act.wait_ge(job_read.sem, job_read.at(layer, "qn1"))
                    elif i == 0:
                        before = {"ssd": "mla", "ret": "ssd", "gla": "ret"}[name]
                        act.wait_ge(dve_ready.sem, dve_ready.at(layer, f"{before}_merged"))
                    for m in range(2):
                        col = 8 * BRANCHES.index(name) + 2 * i + m
                        ins = run(gates[:, 2 * i + m, :], pair[:, m, 0:SEQ],
                                  ACT.Sigmoid if name in LATE else ACT.Identity, bias=chan_col("b_gate", col))
                    ins.then_inc(read_act.sem, read_act.inc(f"fill{f}"))

            def gate_sigmoid(layer, b):
                act.wait_ge(read_act.sem, read_act.at(layer, f"fill{FILLS.index(('gate', b, 3))}"))
                run(gates[:], gates[:], ACT.Sigmoid).then_inc(act_ready.sem, act_ready.inc(f"{b}_gates"))

            def step(name, layer):
                if name == "mla_norm":
                    act.wait_ge(read_act.sem, read_act.at(layer, "fill0"))
                    for t in range(T):
                        run(c_square_out[:, t, 0:256], c[:, t, 0:256], ACT.Square, accum_out=stat[:, 4 + t:5 + t])
                        ins = run(c_square_out[:, t, 256:384], c[:, t, 256:384], ACT.Square,
                                  accum_out=stat[:, 6 + t:7 + t])
                    ins.then_inc(act_link.sem, 1)
                    act.wait_ge(act_link.sem, act_link.next())
                    run(stat[:, 4:6], stat[:, 4:6], ACT.Ln, scale=1.0 / 256, bias=cst("eps", 1)).then_inc(act_link.sem, 1)
                    act.wait_ge(act_link.sem, act_link.next())
                    run(stat[:, 6:8], stat[:, 6:8], ACT.Ln, scale=1.0 / 128, bias=cst("eps", 1)).then_inc(act_link.sem, 1)
                    act.wait_ge(act_link.sem, act_link.next())
                    run(stat[:, 4:8], stat[:, 4:8], ACT.Exp, scale=-0.5).then_inc(act_ready.sem, act_ready.inc("mla_r"))
                if name.startswith("mla_a") and int(name[5:]) < NS:
                    i = int(name[5:])
                    act.wait_ge(dve_ready.sem, dve_ready.at(layer, f"shifted{i}"))
                    run(soft[:, i % 2, :], soft[:, i % 2, :], ACT.Exp).then_inc(act_ready.sem, act_ready.inc(f"exp{i}"))
                if name == "mla_y":
                    for j in range(2):
                        turn_hi(layer, f"mla_y{j}", y_hi[:, 2 * j:2 * j + 2, :], None)
                if name.startswith("conv"):
                    m = int(name[4:])
                    act.wait_ge(dve_ready.sem, dve_ready.at(layer, "pad"))
                    act.wait_ge(read_act.sem, read_act.at(layer, f"fill{FILLS.index(('channel', 'xbc', m // 2))}"))
                    run(conv[:, m, :], xbc[:, m, 0:SEQ], ACT.Identity,
                               scale=chan_col("conv_w", m), bias=chan_col("conv_b", m)).then_inc(act_ready.sem, act_ready.inc(f"tap{m}"))
                if name == "ssd_dt":
                    act.wait_ge(dve_ready.sem, dve_ready.at(layer, "dt_x"))
                    run(stat[:, 80:96], stat[:, 80:96], ACT.Exp).then_inc(act_link.sem, 1)
                    act.wait_ge(act_link.sem, act_link.next())
                    run(stat[:, 112:120], head_rows[:, 8:16], ACT.Exp).then_inc(act_ready.sem, act_ready.inc("dt_u"))
                if name == "ssd_log":
                    act.wait_ge(dve_ready.sem, dve_ready.at(layer, "dt_w"))
                    run(stat[:, 96:112], stat[:, 96:112], ACT.Ln).then_inc(act_ready.sem, act_ready.inc("dt_ln"))
                if name == "ssd_gate":
                    act.wait_ge(dve_ready.sem, dve_ready.at(layer, "conv7"))
                    run(xbc_s, conv, ACT.Sigmoid).then_inc(act_ready.sem, act_ready.inc("conv_sigmoid"))
                if name == "z_gate":
                    act.wait_ge(read_act.sem, read_act.at(layer, f"fill{FILLS.index(('token', 'z', 1))}"))
                    run(z_s, z, ACT.Sigmoid).then_inc(act_ready.sem, act_ready.inc("z_sigmoid"))
                if name == "mla_gate":
                    gate_sigmoid(layer, "mla")
                if name == "ssd_turn":
                    act.wait_ge(dve_ready.sem, dve_ready.at(layer, "cum"))
                    run(stat[:, 96:112], stat[:, 96:112], ACT.Exp).then_inc(act_ready.sem, act_ready.inc("ends"))
                if name.startswith("ssd_decay"):
                    i = int(name[9:])
                    act.wait_ge(dve_ready.sem, dve_ready.at(layer, f"seg{i}"))
                    run(L[:, 4 * (i % 2):4 * (i % 2) + 4, :], L[:, 4 * (i % 2):4 * (i % 2) + 4, :],
                               ACT.Exp).then_inc(act_ready.sem, act_ready.inc(f"decay{i}"))
                if name == "ret_gate":
                    act.wait_ge(read_act.sem, read_act.at(layer, f"fill{FILLS.index(('token', 'rg', 1))}"))
                    run(rg_s, rg, ACT.Sigmoid).then_inc(act_ready.sem, act_ready.inc("rg_sigmoid"))
                if name == "ssd_gates":
                    gate_sigmoid(layer, "ssd")
                if name == "gla_decay":
                    act.wait_ge(dve_ready.sem, dve_ready.at(layer, "gate_n"))
                    run(g_ei, g_ei, ACT.Exp).then_inc(act_link.sem, 1)
                    act.wait_ge(act_link.sem, act_link.next())
                    run(g_ei, g_ei, ACT.Ln, bias=cst("one", 1)).then_inc(act_ready.sem, act_ready.inc("gate_ln"))
                if name == "gla_scale":
                    act.wait_ge(dve_ready.sem, dve_ready.at(layer, "g_cum"))
                    run(g_e, g_cum, ACT.Exp, scale=1.0 / 16).then_inc(act_link.sem, 1)
                    act.wait_ge(act_link.sem, act_link.next())
                    run(g_ei, g_cum, ACT.Exp, scale=-1.0 / 16).then_inc(act_link.sem, 1)
                    act.wait_ge(act_link.sem, act_link.next())
                    run(g_end, g_end, ACT.Exp, scale=1.0 / 16).then_inc(act_ready.sem, act_ready.inc("g_exps"))
                if name in ("ssd_y", "ret_y", "gla_y"):
                    b = name[:3]
                    before = {"ssd": "mla", "ret": "ssd", "gla": "ret"}[b]
                    wait_for_products(act, layer, "branch", before, 1)
                    for j in range(2):
                        turn_hi(layer, f"{name}{j}", y_hi[:, 2 * j:2 * j + 2, :],
                                [chan_col(b, 2 * j + i) for i in range(2)])
                if name == "gla_gate":
                    act.wait_ge(read_act.sem, read_act.at(layer, f"fill{FILLS.index(('token', 'gg', 1))}"))
                    run(gg_s, gg, ACT.Sigmoid).then_inc(act_ready.sem, act_ready.inc("gg_sigmoid"))

            def group_rsqrt(layer, b, n, width):
                act.wait_ge(dve_ready.sem, dve_ready.at(layer, f"{b}_squared"))
                rsqrt(stat[:, 8:8 + n], stat[:, 8:8 + n], width).then_inc(act_ready.sem, act_ready.inc(f"{b}_r"))

            act.wait_ge(s_rope, 1)
            run(trig[:, 0], trig[:, 0], ACT.Sin).then_inc(s_rope_act, 1)
            run(trig[:, 1], trig[:, 1], ACT.Sin).then_inc(s_rope_act, 1)

            nc.scalar.preload_act_table_set(LN_EXP)
            with act.Fori(0, DEPTH) as layer:
                act_link.bind(layer)
                for t in range(T):
                    act.wait_ge(x_done.sem, x_done.at_number(layer, t - 1))
                    squares(xs_res[:, t, :], t)
                    rsqrt(stat[:, t:t + 1], stat[:, t:t + 1], D).then_inc(act_ready.sem, act_ready.inc(f"h_r{t}"))
                    hi_half(layer, t)
                act.wait_ge(s_chan, layer * 16 + 16)
                for t in range(T):
                    turn_hi_tile(layer, "h", t, "pre_mix")
                for u in range(NU):
                    kind, name, i = UNITS[u]
                    for h in range(2 * u + AHEAD, min(2 * u + AHEAD + 2, 2 * NU)):
                        hi_half(layer, h)
                    for f in fills_of.get(u, []):
                        if READ_BY_ACT[f]:
                            read(layer, f)
                    for s in STEPS.get(u, []):
                        if s in ("ret_gate", "ssd_gates", "gla_gate"):
                            step(s, layer)
                            nc.scalar.preload_act_table_set(LN_EXP)
                        elif s == "ssd_scale":
                            group_rsqrt(layer, "ssd", 4, 256)
                        elif s == "ret_scale":
                            group_rsqrt(layer, "ret", 8, 128)
                        elif s == "gla_scaled":
                            group_rsqrt(layer, "gla", 8, 128)
                        else:
                            step(s, layer)
                    if (kind, name, i) == ("gate", "gla", 3):
                        nc.scalar.preload_act_table_set(LN_EXP)
                    if kind == "branch" and name == "gla":
                        for m in (2 * i, 2 * i + 1):
                            act.wait_ge(merge_sum.sem, merge_sum.at(layer, f"m{m}"))
                            run(a_hi[:, 2 * m:2 * m + 2, :], merged[:, 2 * m:2 * m + 2, :]).then_inc(merge_hi.sem, merge_hi.inc(f"m{m}"))
                    if kind == "out" and i == 3:
                        for t in range(T):
                            if t == 0:
                                act.wait_ge(tile_done.sem, tile_done.at(layer, "out"))
                            else:
                                wait_for_products(act, layer, "out", "out", 3)
                            squares(proj[:, 2 * t:2 * t + 2, :], t)
                            rsqrt(stat[:, t:t + 1], stat[:, t:t + 1], D).then_inc(act_ready.sem, act_ready.inc(f"mix_r{t}"))
                        for t in range(T):
                            turn_hi_tile(layer, "u", t, "pre_mlp")
                    if (kind, i) == ("down", 0):
                        act.wait_ge(dve_ready.sem, dve_ready.at(layer, "x_mixed11"))
                        for t in range(T):
                            squares(xs_res[:, t, :], 2 + t, update)
                        run(stat[:, 2:4], stat[:, 2:4], ACT.Ln, scale=1.0 / D, bias=cst("eps", 1)).then_inc(act_link.sem, 1)
                        act.wait_ge(act_link.sem, act_link.next())
                        run(stat[:, 56:58], stat[:, 2:4], ACT.Exp, scale=-2.0, bias=cst("ln_1/D", 1)).then_inc(act_link.sem, 1)
                        act.wait_ge(act_link.sem, act_link.next())
                        run(stat[:, 2:4], stat[:, 2:4], ACT.Copy, scale=-1.0).then_inc(act_link.sem, 1)
                        act.wait_ge(act_link.sem, act_link.next())
                    if kind == "up":
                        wait_for_products(act, layer, "up", "up", i)
                        pair = mix[:, 2 * (i % 2):2 * (i % 2) + 2, 0:SEQ]
                        if i >= 2:
                            act.wait_ge(up_lo.sem, up_lo.at(layer, f"up{i - 2}"))
                        run(part(R2, 512 * (i % 2), 2, SEQ), pair, ACT.Relu).then_inc(up_read.sem, up_read.inc(f"up{i}"))
                        act.wait_ge(up_read.sem, up_read.at(layer, f"up{i}"))
                        if i >= 2:
                            wait_for_products(act, layer, "down", "down", i - 2)
                        else:
                            wait_for_products(act, layer, "branch", "gla", 1)
                        run(y_hi[:, 2 * (i % 2):2 * (i % 2) + 2, :], part(R2, 512 * (i % 2), 2, SEQ),
                                       ACT.Square).then_inc(up_hi.sem, up_hi.inc(f"up{i}"))
                for t in range(T):
                    if t == 0:
                        act.wait_ge(tile_done.sem, tile_done.at(layer, "down"))
                    else:
                        wait_for_products(act, layer, "down", "down", 15)
                    squares(proj[:, 2 * t:2 * t + 2, :], t)
                    run(stat[:, t:t + 1], stat[:, t:t + 1], ACT.Ln, scale=stat[:, 56 + t:57 + t],
                        bias=cst("eps", 1)).then_inc(act_link.sem, 1)
                    act.wait_ge(act_link.sem, act_link.next())
                    run(stat[:, t:t + 1], stat[:, t:t + 1], ACT.Exp, scale=-0.5,
                        bias=stat[:, 2 + t:3 + t]).then_inc(act_ready.sem, act_ready.inc(f"mlp_r{t}"))
            assert act_link.n == ACT_LINKS, act_link.n

        @block.vector
        def _(dve):
            v = nc.vector

            def lo_half(layer, u):
                src, hi, lo = half_views(u, 0)
                dve.wait_ge(hi_made.sem, hi_made.at(layer, f"half{2 * u}"))
                v.tensor_tensor(lo, src, hi.bitcast(F32), ALU.subtract).then_inc(lo_even.sem, lo_even.inc(f"unit{u}"))

            def turn_lo(layer, name, hi, lo, gain):
                dve.wait_ge(turned_hi.sem, turned_hi.at(layer, name))
                for i in range(2):
                    ins = v.scalar_tensor_tensor(out=lo[:, i, :], in0=bank(name)[:, SEQ * i:SEQ * i + SEQ],
                                                 scalar=gain[i] if gain else 1.0, in1=hi[:, i, :].bitcast(F32),
                                                 op0=ALU.mult, op1=ALU.subtract)
                ins.then_inc(job_read.sem, job_read.inc(name))

            def turn_lo_tile(layer, name, t, gain):
                for q in range(2):
                    dve.wait_ge(turned_hi.sem, turned_hi.at(layer, f"{name}{t}{q}"))
                    for i in range(4):
                        s = slice(P * t, P * t + P)
                        ins = v.scalar_tensor_tensor(
                            out=a_lo[:, 4 * q + i, s], in0=bank(f"{name}{t}{q}")[:, P * i:P * i + P],
                            scalar=chan_col(gain, 4 * q + i), in1=a_hi[:, 4 * q + i, s].bitcast(F32),
                            op0=ALU.mult, op1=ALU.subtract)
                    ins.then_inc(job_read.sem, job_read.inc(f"{name}{t}{q}"))

            def full(layer, job):
                dve.wait_ge(job_full.sem, job_full.at(layer, job))
                return bank(job)

            def rope(x1, x2, cos, sin, o1, o2, a, b):
                v.tensor_tensor(a, x1, cos, ALU.mult)
                v.tensor_tensor(b, x2, sin, ALU.mult).then_inc(dve_link.sem, 1)
                dve.wait_ge(dve_link.sem, dve_link.next())
                v.tensor_tensor(o1, a, b, ALU.subtract).then_inc(dve_link.sem, 1)
                dve.wait_ge(dve_link.sem, dve_link.next())
                v.tensor_tensor(a, x2, cos, ALU.mult)
                v.tensor_tensor(b, x1, sin, ALU.mult).then_inc(dve_link.sem, 1)
                dve.wait_ge(dve_link.sem, dve_link.next())
                return v.tensor_tensor(o2, a, b, ALU.add)

            def heads(ap, n, d):
                return ap.unsqueeze(2).broadcast_to((P, n, d))

            def split_heads(ap, n):
                return ap.rearrange("p t (h d) -> p (t h) d", h=n)

            def squares(y, n, tmp, event, at=8):
                v.tensor_tensor(tmp, y, y, ALU.mult).then_inc(dve_link.sem, 1)
                dve.wait_ge(dve_link.sem, dve_link.next())
                v.tensor_reduce(stat[:, at:at + T * n], split_heads(tmp, n), X_AXIS, ALU.add).then_inc(dve_ready.sem, dve_ready.inc(event))

            def step(name, layer):
                if name == "mla_norm":
                    dve.wait_ge(act_ready.sem, act_ready.at(layer, "mla_r"))
                    for t in range(T):
                        v.tensor_scalar(c[:, t, 0:256], c[:, t, 0:256], stat[:, 4 + t:5 + t], None, ALU.mult)
                        ins = v.tensor_scalar(c[:, t, 256:384], c[:, t, 256:384], stat[:, 6 + t:7 + t], None,
                                              ALU.mult)
                    ins.then_inc(dve_ready.sem, dve_ready.inc("c_scaled"))
                    cos, sin = trig[:, 0, :, 0::2], trig[:, 1, :, 0::2]
                    kr = c[:, :, 384:416]
                    ra, rb = (part(R1, 4096 + 512 * i, T, 16) for i in range(2))
                    rope(kr[:, :, 0:16], kr[:, :, 16:32], cos, sin, k_rot[:, :, 0:16],
                                k_rot[:, :, 16:32], ra, rb).then_inc(dve_ready.sem, dve_ready.inc("k_rot"))
                if name == "mla_turn":
                    b = full(layer, "cq")
                    for m in range(2):
                        ins = v.tensor_scalar(cT[:, m, :], b[:, SEQ * m:SEQ * m + SEQ], chan_col("q_norm", m),
                                              None, ALU.mult)
                    ins.then_inc(job_read.sem, job_read.inc("cq"))
                    b = full(layer, "ckv")
                    v.tensor_scalar(cT[:, 2, :], b[:, 0:SEQ], chan_col("kv_norm", 0), None, ALU.mult)
                    v.tensor_copy(kT[64:96, :, :], b[0:32, SEQ:2 * SEQ].unsqueeze(1)
                                                .broadcast_to((32, 8, SEQ))).then_inc(job_read.sem, job_read.inc("ckv"))
                if name == "mla_q":
                    v.tensor_copy(q_pe.rearrange("p a b -> p (a b)"), full(layer, "qpe")).then_inc(job_read.sem, job_read.inc("qpe"))
                    for j in range(2):
                        b = full(layer, f"qn{j}").rearrange("p (h n) -> p h n", h=2)
                        v.tensor_copy(qT[0:64, 4 * j:4 * j + 4:2, :], b[0:64])
                        v.tensor_copy(qT[0:64, 4 * j + 1:4 * j + 4:2, :], b[64:128]).then_inc(
                            job_read.sem, job_read.inc(f"qn{j}"))
                    q = q_pe.rearrange("p t (h d) -> p t h d", h=8)
                    o = q_rot.rearrange("p t (h d) -> p t h d", h=8)
                    cos, sin = (trig[:, i, :, 0::2].unsqueeze(2).broadcast_to((P, T, 8, 16)) for i in range(2))
                    ra, rb = (part(R1, 4096 + 512 * i, T, 8, 16) for i in range(2))
                    dve.wait_ge(job_read.sem, job_read.at(layer, "qn1"))
                    rope(q[:, :, :, 0:16], q[:, :, :, 16:32], cos, sin, o[:, :, :, 0:16],
                                o[:, :, :, 16:32], ra, rb).then_inc(dve_ready.sem, dve_ready.inc("q_rot"))
                if name == "mla_kv":
                    for j in range(2):
                        b = full(layer, f"kn{j}").rearrange("p (h n) -> p h n", h=2)
                        v.tensor_copy(kT[0:64, 4 * j:4 * j + 4:2, :], b[0:64])
                        v.tensor_copy(kT[0:64, 4 * j + 1:4 * j + 4:2, :], b[64:128]).then_inc(
                            job_read.sem, job_read.inc(f"kn{j}"))
                    dve.wait_ge(dve_ready.sem, dve_ready.at(layer, "q_rot"))
                    for t in range(T):
                        v.tensor_copy(v_mla[:, t, :], full(layer, f"v{t}")).then_inc(job_read.sem, job_read.inc(f"v{t}"))
                if name == "mla_pe":
                    b = full(layer, "qpeT").rearrange("p (g n) -> p g n", g=2)
                    for q in range(4):
                        ins = v.tensor_copy(qT[64:96, q:8:4, :], b[32 * q:32 * q + 32])
                    ins.then_inc(job_read.sem, job_read.inc("qpeT"))
                if name.startswith("mla_a"):
                    i = int(name[5:])
                    if i < NS:
                        t, _, n = SOFT[i]
                        w = P * (t + 1)
                        s = soft[:, i % 2, :].rearrange("p (h n) -> p h n", h=n)
                        neg = cst("neg", 2 * P)[:, 2 * P - w:2 * P].unsqueeze(1).broadcast_to((P, n, w))
                        b = full(layer, f"score{i}").rearrange("p (h n) -> p h n", h=n)
                        if i >= 2:
                            dve.wait_ge(job_full.sem, job_full.at(layer, f"turn{i - 2}"))
                        elif i == 0:
                            dve.wait_ge(job_full.sem, job_full.at(layer, "qpeT"))
                        v.scalar_tensor_tensor(out=s, in0=b, scalar=96 ** -0.5, in1=neg,
                                                             op0=ALU.mult, op1=ALU.add).then_inc(job_read.sem, job_read.inc(f"score{i}"))
                        dve.wait_ge(job_read.sem, job_read.at(layer, f"score{i}"))
                        v.tensor_reduce(stat[:, 8:8 + n], s, X_AXIS, ALU.max).then_inc(dve_link.sem, 1)
                        dve.wait_ge(dve_link.sem, dve_link.next())
                        v.tensor_tensor(s, s, heads(stat[:, 8:8 + n], n, w), ALU.subtract).then_inc(dve_ready.sem, dve_ready.inc(f"shifted{i}"))
                    if 1 <= i <= NS:
                        j = i - 1
                        t, _, n = SOFT[j]
                        dve.wait_ge(act_ready.sem, act_ready.at(layer, f"exp{j}"))
                        s = soft[:, j % 2, :].rearrange("p (h n) -> p h n", h=n)
                        sums = stat[:, 16 + 4 * (j % 2):16 + 4 * (j % 2) + n]
                        v.tensor_reduce(sums, s, X_AXIS, ALU.add).then_inc(dve_link.sem, 1)
                        dve.wait_ge(dve_link.sem, dve_link.next())
                        v.reciprocal(sums, sums).then_inc(dve_link.sem, 1)
                        dve.wait_ge(dve_link.sem, dve_link.next())
                        if i == 1:
                            dve.wait_ge(job_read.sem, job_read.at(layer, "v1"))
                        v.tensor_copy(probT[:, j % 2, :], full(layer, f"turn{j}")).then_inc(job_read.sem, job_read.inc(f"turn{j}"))
                    if i >= 2:
                        j = i - 2
                        t, h, n = SOFT[j]
                        b = full(layer, f"pv{j}")[:, 0:64 * n].rearrange("p (h n) -> p h n", h=n)
                        o = o_mla[:, t, 64 * h:64 * (h + n)].rearrange("p (h n) -> p h n", h=n)
                        sums = stat[:, 16 + 4 * (j % 2):16 + 4 * (j % 2) + n]
                        v.tensor_tensor(o, b, heads(sums, n, 64), ALU.mult).then_inc(job_read.sem, job_read.inc(f"pv{j}"))
                if name == "mla_y":
                    for j in range(2):
                        s = slice(2 * j, 2 * j + 2)
                        turn_lo(layer, f"mla_y{j}", y_hi[:, s, :], y_lo[:, s, :], None)
                if name.startswith("conv"):
                    m = int(name[4:])
                    dve.wait_ge(act_ready.sem, act_ready.at(layer, f"tap{m}"))
                    for k in range(1, 4):
                        ins = v.scalar_tensor_tensor(out=conv[:, m, :], in0=xbc[:, m, k:k + SEQ],
                                                     scalar=chan_col("conv_w", 8 * k + m), in1=conv[:, m, :],
                                                     op0=ALU.mult, op1=ALU.add)
                        if k < 3:
                            ins.then_inc(dve_link.sem, 1)
                            dve.wait_ge(dve_link.sem, dve_link.next())
                    ins.then_inc(dve_ready.sem, dve_ready.inc(f"conv{m}"))
                if name == "ssd_dt":
                    dve.wait_ge(s_param, layer * (16 * n_params) + 16 * n_params)
                    x_ = stat[:, 64:80]
                    dve.wait_ge(read_act.sem, read_act.at(layer, "fill0"))
                    v.tensor_tensor(x_.rearrange("p (t h) -> p t h", t=T), c[:, :, 416:424],
                                             head_rows[:, 0:8].unsqueeze(1).broadcast_to((P, T, 8)), ALU.add).then_inc(dve_link.sem, 1)
                    dve.wait_ge(dve_link.sem, dve_link.next())
                    v.scalar_tensor_tensor(out=stat[:, 80:96], in0=x_, scalar=-1.0, in1=x_,
                                                  op0=ALU.mult, op1=ALU.min).then_inc(dve_ready.sem, dve_ready.inc("dt_x"))
                if name == "ssd_cum":
                    cum_read(layer)
                if name == "ssd_log":
                    x_, u, w = stat[:, 64:80], stat[:, 80:96], stat[:, 96:112]
                    dve.wait_ge(act_ready.sem, act_ready.at(layer, "dt_u"))
                    v.tensor_scalar(w1, u, 1.0, None, ALU.add).then_inc(dve_link.sem, 1)
                    dve.wait_ge(dve_link.sem, dve_link.next())
                    v.tensor_copy(w, w1).then_inc(dve_ready.sem, dve_ready.inc("dt_w"))
                    v.scalar_tensor_tensor(out=u, in0=w1, scalar=-1.0, in1=u, op0=ALU.add,
                                                    op1=ALU.subtract).then_inc(dve_link.sem, 1)
                    dve.wait_ge(dve_link.sem, dve_link.next())
                    v.reciprocal(w1, w1).then_inc(dve_link.sem, 1)
                    dve.wait_ge(dve_link.sem, dve_link.next())
                    v.tensor_tensor(u, u, w1, ALU.mult).then_inc(dve_link.sem, 1)
                    dve.wait_ge(dve_link.sem, dve_link.next())
                    v.scalar_tensor_tensor(out=x_, in0=x_, scalar=0.0, in1=u, op0=ALU.max,
                                                    op1=ALU.subtract).then_inc(dve_link.sem, 1)
                    dve.wait_ge(dve_link.sem, dve_link.next())
                    dve.wait_ge(act_ready.sem, act_ready.at(layer, "dt_ln"))
                    v.tensor_tensor(x_, x_, w, ALU.add).then_inc(dve_link.sem, 1)
                    dve.wait_ge(dve_link.sem, dve_link.next())
                    v.scalar_tensor_tensor(
                        out=log_decay.rearrange("p (t h) -> p t h", t=T), in0=x_.rearrange("p (t h) -> p t h", t=T),
                        scalar=-1.0, in1=stat[:, 112:120].unsqueeze(1).broadcast_to((P, T, 8)),
                        op0=ALU.mult, op1=ALU.mult).then_inc(dve_ready.sem, dve_ready.inc("log_decay"))
                if name == "ssd_turn":
                    b = full(layer, "G").rearrange("p (g n) -> p g n", g=4)
                    v.tensor_tensor(G, b, causal.unsqueeze(1).broadcast_to((P, 4, P)), ALU.mult).then_inc(job_read.sem, job_read.inc("G"))
                    for t in range(T):
                        b = full(layer, f"xs{t}")
                        v.tensor_copy(xs[:, t, :], b).then_inc(job_read.sem, job_read.inc(f"xs{t}"))
                    dve.wait_ge(job_read.sem, job_read.at(layer, "xs1"))
                    v.tensor_tensor(split_heads(xdt, 8), split_heads(xs, 8),
                                           heads(stat[:, 64:80], 16, 64), ALU.mult).then_inc(dve_ready.sem, dve_ready.inc("xdt"))
                    v.tensor_copy(B_tok.rearrange("p a b -> p (a b)"), full(layer, "B")[:, 0:256]).then_inc(job_read.sem, job_read.inc("B"))
                    dve.wait_ge(act_ready.sem, act_ready.at(layer, "ends"))
                    dve.wait_ge(dve_ready.sem, dve_ready.at(layer, "xdt"))
                    v.tensor_tensor(x_end.rearrange("p (h d) -> p h d", h=8),
                                           xdt[:, 0, :].rearrange("p (h d) -> p h d", h=8),
                                           heads(stat[:, 96:104], 8, 64), ALU.mult).then_inc(dve_ready.sem, dve_ready.inc("x_end"))
                    v.tensor_tensor(split_heads(sy, 8)[:, 0:8], split_heads(xs, 8)[:, 0:8],
                                    heads(head_rows[:, 16:24], 8, 64), ALU.mult)
                    v.tensor_tensor(split_heads(sy, 8)[:, 8:16], split_heads(xs, 8)[:, 8:16],
                                             heads(head_rows[:, 16:24], 8, 64), ALU.mult).then_inc(dve_link.sem, 1)
                    dve.wait_ge(dve_link.sem, dve_link.next())
                if name.startswith("ssd_decay"):
                    i = int(name[9:])
                    t, g = i // 2, i % 2
                    s = L[:, 4 * g:4 * g + 4, :]
                    b = full(layer, f"R{i}").rearrange("p (h n) -> p h n", h=4)
                    if i == 0:
                        dve.wait_ge(pool_ready.sem, pool_ready.at(layer, "z_silu"))
                    if i >= 2:
                        dve.wait_ge(job_full.sem, job_full.at(layer, "Y0"))
                    v.tensor_tensor(s, b, heads(c_cum(t, g), 4, P), ALU.subtract).then_inc(job_read.sem, job_read.inc(f"R{i}"))
                    dve.wait_ge(job_read.sem, job_read.at(layer, f"R{i}"))
                    v.tensor_scalar(s, s, 0.0, None, ALU.min).then_inc(dve_ready.sem, dve_ready.inc(f"seg{i}"))
                    dve.wait_ge(act_ready.sem, act_ready.at(layer, f"decay{i}"))
                    v.tensor_tensor(s, s, G[:, 2 * t + g, :].unsqueeze(1).broadcast_to((P, 4, P)),
                                           ALU.mult).then_inc(dve_ready.sem, dve_ready.inc(f"weights{i}"))
                    if i == 1:
                        v.tensor_copy(s_state, full(layer, "S")).then_inc(job_read.sem, job_read.inc("S"))
                if name == "ssd_y0":
                    v.tensor_tensor(sy[:, 0, :], sy[:, 0, :], full(layer, "Y0"), ALU.add).then_inc(job_read.sem, job_read.inc("Y0"))
                if name == "ssd_y1":
                    b = full(layer, "off").rearrange("p (h d) -> p h d", h=8)
                    s = s_tmp.rearrange("p (h d) -> p h d", h=8)
                    v.tensor_tensor(s, b, heads(stat[:, 104:112], 8, 64), ALU.mult).then_inc(job_read.sem, job_read.inc("off"))
                    dve.wait_ge(job_read.sem, job_read.at(layer, "off"))
                    v.tensor_tensor(sy[:, 1, :], sy[:, 1, :], s_tmp, ALU.add).then_inc(dve_link.sem, 1)
                    dve.wait_ge(dve_link.sem, dve_link.next())
                    v.tensor_tensor(sy[:, 1, :], sy[:, 1, :], full(layer, "Y1"), ALU.add).then_inc(job_read.sem, job_read.inc("Y1"))
                    dve.wait_ge(job_read.sem, job_read.at(layer, "Y1"))
                    v.memset(stat[:, 63:64], 0.0).then_inc(dve_ready.sem, dve_ready.inc("ssd_summed"))
                if name == "ssd_norm":
                    dve.wait_ge(pool_ready.sem, pool_ready.at(layer, "ssd_gated"))
                    squares(sy, 2, c_square_out, "ssd_squared")
                if name == "ssd_scale":
                    dve.wait_ge(act_ready.sem, act_ready.at(layer, "ssd_r"))
                    v.tensor_tensor(split_heads(sy, 2), split_heads(sy, 2), heads(stat[:, 8:12], 4, 256),
                                           ALU.mult).then_inc(dve_ready.sem, dve_ready.inc("ssd_out"))
                if name in ("ssd_y", "ret_y", "gla_y"):
                    for j in range(2):
                        s = slice(2 * j, 2 * j + 2)
                        turn_lo(layer, f"{name}{j}", y_hi[:, s, :], y_lo[:, s, :],
                                [chan_col(name[:3], 2 * j + i) for i in range(2)])
                if name == "ret_rope":
                    dve.wait_ge(read_act.sem, read_act.at(layer, f"fill{FILLS.index(('token', 'rqk', 1))}"))
                    dve.wait_ge(job_read.sem, job_read.at(layer, "mla_y1"))
                    for t in range(T):
                        q = rqk[:, t, :].rearrange("p (h d) -> p h d", h=8)
                        o = rr[:, t, :].rearrange("p (h d) -> p h d", h=8)
                        cos, sin = (trig[:, i, t, :].unsqueeze(1).broadcast_to((P, 8, 32)) for i in range(2))
                        ra, rb = (part(R1, 5120 + 512 * i + 256 * t, 8, 32) for i in range(2))
                        rope(q[:, :, 0:32], q[:, :, 32:64], cos, sin, o[:, :, 0:32], o[:, :, 32:64],
                                      ra, rb).then_inc(dve_link.sem, 1)
                        dve.wait_ge(dve_link.sem, dve_link.next())
                    for t in range(T):
                        o = rr[:, t, :].rearrange("p (h d) -> p h d", h=8)
                        ins = v.tensor_tensor(o, o, heads(cst("ret_scale", 8), 8, 64), ALU.mult)
                    ins.then_inc(dve_ready.sem, dve_ready.inc("r_scaled"))
                if name == "ret_turn":
                    for j, n in enumerate(("rq", "rk")):
                        v.tensor_copy(rT[:, 2 * j:2 * j + 2, :].rearrange("p a b -> p (a b)"),
                                                    full(layer, n)).then_inc(job_read.sem, job_read.inc(n))
                if name in ("ret_s0", "ret_s1"):
                    t = int(name[5])
                    b = full(layer, f"rs{t}").rearrange("p (h n) -> p h n", h=4)
                    s = rS[:, t, :].rearrange("p (h n) -> p h n", h=4)
                    v.tensor_tensor(s, b, causal.unsqueeze(1).broadcast_to((P, 4, P)), ALU.mult).then_inc(job_read.sem, job_read.inc(f"rs{t}"))
                    if t == 0:
                        b = full(layer, "rS")[:, 0:256].rearrange("p (h n) -> p h n", h=2)
                        v.tensor_tensor(r_state, b, heads(cst("ret_total", 2), 2, P), ALU.mult).then_inc(job_read.sem, job_read.inc("rS"))
                if name in ("ret_y0", "ret_y1"):
                    t = int(name[5])
                    v.tensor_copy(ry[:, t, :], full(layer, f"rY{t}")).then_inc(job_read.sem, job_read.inc(f"rY{t}"))
                if name == "ret_norm":
                    dve.wait_ge(job_read.sem, job_read.at(layer, "rY1"))
                    squares(ry, 4, rg_s, "ret_squared")
                    dve.wait_ge(pool_ready.sem, pool_ready.at(layer, "rg_silu"))
                    v.tensor_tensor(ry, ry, rg, ALU.mult).then_inc(dve_ready.sem, dve_ready.inc("ret_gated"))
                if name == "ret_scale":
                    dve.wait_ge(dve_ready.sem, dve_ready.at(layer, "ret_gated"))
                    dve.wait_ge(act_ready.sem, act_ready.at(layer, "ret_r"))
                    v.tensor_tensor(split_heads(ry, 4), split_heads(ry, 4), heads(stat[:, 8:16], 8, P),
                                           ALU.mult).then_inc(dve_ready.sem, dve_ready.inc("ret_out"))
                if name == "gla_low":
                    v.tensor_copy(g_low, full(layer, "low")[0:16, 0:SEQ]).then_inc(job_read.sem, job_read.inc("low"))
                if name == "gla_decay":
                    b = full(layer, "gate").rearrange("p (m n) -> p m n", m=2)
                    for m in range(2):
                        ins = v.tensor_scalar(g_cum[:, m, :], b[:, m, :], chan_col("gla_b", m), None, ALU.add)
                    ins.then_inc(job_read.sem, job_read.inc("gate"))
                    dve.wait_ge(job_read.sem, job_read.at(layer, "gate"))
                    v.scalar_tensor_tensor(out=g_ei, in0=g_cum, scalar=-1.0, in1=g_cum,
                                                  op0=ALU.mult, op1=ALU.min).then_inc(dve_ready.sem, dve_ready.inc("gate_n"))
                if name == "gla_sum":
                    dve.wait_ge(act_ready.sem, act_ready.at(layer, "gate_ln"))
                    v.scalar_tensor_tensor(out=g_end, in0=g_cum, scalar=0.0, in1=g_ei,
                                                    op0=ALU.min, op1=ALU.subtract).then_inc(dve_link.sem, 1)
                    dve.wait_ge(dve_link.sem, dve_link.next())
                    for m in range(2):
                        ins = v.tensor_tensor_scan(g_cum[:, m, :], cst("restart", SEQ), g_end[:, m, :], 0.0,
                                                   ALU.mult, ALU.add)
                    ins.then_inc(dve_link.sem, 1)
                    dve.wait_ge(dve_link.sem, dve_link.next())
                    cum = g_cum.rearrange("p m (c n) -> p (m c) n", n=64)
                    v.tensor_tensor(g_end.rearrange("p m (c n) -> p (m c) n", n=64),
                                           cum[:, :, 63:64].broadcast_to((P, 8, 64)), cum, ALU.subtract).then_inc(dve_ready.sem, dve_ready.inc("g_cum"))
                if name == "gla_scale":
                    dve.wait_ge(act_ready.sem, act_ready.at(layer, "g_exps"))
                    dve.wait_ge(read_act.sem, read_act.at(layer, f"fill{FILLS.index(('channel', 'gqk', 1))}"))
                    v.tensor_tensor(g_end, g_end, gqk[:, 2:4, :], ALU.mult).then_inc(dve_ready.sem, dve_ready.inc("k_end"))
                    v.scalar_tensor_tensor(out=gqk[:, 0:2, :], in0=gqk[:, 0:2, :], scalar=64 ** -0.5, in1=g_e,
                                           op0=ALU.mult, op1=ALU.mult)
                    v.tensor_tensor(gqk[:, 2:4, :], gqk[:, 2:4, :], g_ei, ALU.mult).then_inc(dve_ready.sem, dve_ready.inc("qk_in"))
                if name == "gla_turn":
                    dve.wait_ge(job_read.sem, job_read.at(layer, "ssd_y1"))
                    v.memset(gS, 0.0).then_inc(dve_ready.sem, dve_ready.inc("gS_zero"))
                    v.tensor_copy(k_tok.rearrange("p a b -> p (a b)"), full(layer, "kst")).then_inc(job_read.sem, job_read.inc("kst"))
                if name in ("gla_s0", "gla_s1"):
                    t = int(name[5])
                    b = full(layer, f"gs{t}").rearrange("p (h n) -> p h n", h=4)
                    s = gS[:, t, :].rearrange("p (h n) -> p h n", h=4)
                    dve.wait_ge(dve_ready.sem, dve_ready.at(layer, "gS_zero"))
                    mask = cst("block", P).bitcast(I32).unsqueeze(1).broadcast_to((P, 4, P))
                    v.memset(stat[:, 63:64], 0.0)
                    v.copy_predicated(s, mask, b).then_inc(job_read.sem, job_read.inc(f"gs{t}"))
                if name == "gla_state":
                    b = full(layer, "gS0")[:, 0:256]
                    v.tensor_copy(g_state[:, 0].rearrange("p a b -> p (a b)"), b).then_inc(job_read.sem, job_read.inc("gS0"))
                    for ch in (1, 2):
                        dve.wait_ge(job_read.sem, job_read.at(layer, f"gS{ch - 1}"))
                        b = full(layer, f"gS{ch}")[:, 0:256].rearrange("p (a b) -> p a b", a=2)
                        for m in range(2):
                            ins = v.scalar_tensor_tensor(out=g_state[:, ch, m, :], in0=g_state[:, ch - 1, m, :],
                                                         scalar=g_e[:, m, 64 * ch + 63:64 * ch + 64],
                                                         in1=b[:, m, :], op0=ALU.mult, op1=ALU.add)
                        ins.then_inc(job_read.sem, job_read.inc(f"gS{ch}"))
                if name in ("gla_o0", "gla_o1"):
                    t = int(name[5])
                    v.tensor_copy(gy[:, t, :], full(layer, f"gY{t}")).then_inc(job_read.sem, job_read.inc(f"gY{t}"))
                if name == "gla_norm":
                    dve.wait_ge(job_read.sem, job_read.at(layer, "gY1"))
                    dve.wait_ge(pool_ready.sem, pool_ready.at(layer, "gg_silu"))
                    squares(gy, 4, gg_s, "gla_squared")
                    v.tensor_tensor(gy, gy, gg, ALU.mult).then_inc(dve_ready.sem, dve_ready.inc("gla_gated"))
                if name == "gla_scaled":
                    dve.wait_ge(dve_ready.sem, dve_ready.at(layer, "gla_gated"))
                    dve.wait_ge(act_ready.sem, act_ready.at(layer, "gla_r"))
                    v.tensor_tensor(split_heads(gy, 4), split_heads(gy, 4), heads(stat[:, 8:16], 8, P),
                                           ALU.mult).then_inc(dve_ready.sem, dve_ready.inc("gla_out"))


            def c_cum(t, g):
                return cum_keep[:, 8 * t + 4 * g:8 * t + 4 * g + 4]

            def cum_read(layer):
                b = full(layer, "cum")
                v.tensor_copy(cum_keep, b[:, 0:16])
                v.tensor_copy(stat[:, 96:112], b[:, 0:16])
                v.tensor_copy(stat[:, 80:88], b[:, 16:24]).then_inc(job_read.sem, job_read.inc("cum"))
                dve.wait_ge(job_read.sem, job_read.at(layer, "cum"))
                v.tensor_tensor(stat[:, 96:104], stat[:, 80:88], stat[:, 96:104], ALU.subtract).then_inc(dve_ready.sem, dve_ready.inc("cum"))

            def branch_read(layer, f):
                _, name, m = FILLS[f]
                dve.wait_ge(half_done.sem, half_done.at(layer, f"half{FILL_ENDS[f]}"))
                if name in LATE:
                    dve.wait_ge(read_act.sem, read_act.at(layer, f"fill{FILLS.index(('gate', name, m))}"))
                elif m == 0:
                    dve.wait_ge(act_ready.sem, act_ready.at(layer, f"{name}_gates"))
                pair = proj[:, 2 * (f % 2):2 * (f % 2) + 2, 0:SEQ]
                s = slice(2 * m, 2 * m + 2)
                if name == "mla":
                    v.tensor_tensor(merged[:, s, :], pair, gates[:, s, :], ALU.mult).then_inc(read_dve.sem, read_dve.inc(f"fill{f}"))
                    if m == 3:
                        v.memset(stat[:, 63:64], 0.0).then_inc(dve_ready.sem, dve_ready.inc("mla_merged"))
                    return
                v.tensor_tensor(gates[:, s, :], pair, gates[:, s, :], ALU.mult).then_inc(read_dve.sem, read_dve.inc(f"fill{f}"))
                dve.wait_ge(read_dve.sem, read_dve.at(layer, f"fill{f}"))
                ins = v.tensor_tensor(merged[:, s, :], merged[:, s, :], gates[:, s, :], ALU.add)
                if name == "gla":
                    ins.then_inc(merge_sum.sem, merge_sum.inc(f"m{m}"))
                    dve.wait_ge(merge_hi.sem, merge_hi.at(layer, f"m{m}"))
                    v.tensor_tensor(a_lo[:, s, :], merged[:, s, :], a_hi[:, s, :].bitcast(F32),
                                                  ALU.subtract).then_inc(merge_lo.sem, merge_lo.inc(f"m{m}"))
                elif m == 3:
                    ins.then_inc(dve_ready.sem, dve_ready.inc(f"{name}_merged"))

            def add_normed(layer, name, t, columns):
                dve.wait_ge(act_ready.sem, act_ready.at(layer, f"{name}_r{t}"))
                both = proj[:, 2 * t:2 * t + 2, :].rearrange("p a b -> p (a b)")
                v.scalar_tensor_tensor(out=update[:, t, columns], in0=both[:, columns], scalar=stat[:, t:t + 1],
                                       in1=post_gain[:, columns], op0=ALU.mult, op1=ALU.mult).then_inc(dve_link.sem, 1)
                dve.wait_ge(dve_link.sem, dve_link.next())
                return v.tensor_tensor(xs_res[:, t, columns], xs_res[:, t, columns], update[:, t, columns], ALU.add)

            v.memset(stat[:, 56:57], 0.0).then_inc(lo_even.sem, RAW)
            v.memset(stat[:, 62:63], 0.0).then_inc(lo_odd.sem, RAW)
            v.memset(stat[:, 57:58], 0.0).then_inc(half_done.sem, HL)
            v.memset(stat[:, 58:59], 0.0).then_inc(params_used.sem, 1)
            dve.wait_ge(s_input, 32)

            n = [0]

            def pre(ins):
                n[0] += 1
                ins.then_inc(s_pre, 1)
                dve.wait_ge(s_pre, n[0])

            ang, turns = part(R1, 0, T, ROPE), part(R1, 128, 2, T * ROPE)
            ang_both = part(R1, 0, T * ROPE).unsqueeze(1).broadcast_to((P, 2, T * ROPE))
            both = trig[:].rearrange("p i t n -> p i (t n)")
            pre(v.tensor_copy(stat[:, 60:62], pos_i[:]))
            for t in range(T):
                pre(v.tensor_scalar(ang[:, t, :], cst("freq", ROPE), stat[:, 60 + t:61 + t], None, ALU.mult))
            magic = 12582912.0
            for i, quarter in ((0, 0.25), (1, 0.0)):
                pre(v.tensor_scalar(turns[:, i, :], part(R1, 0, T * ROPE), 1 / (2 * np.pi), quarter,
                                    ALU.mult, ALU.add))
            pre(v.tensor_scalar(turns, turns, magic, -magic, ALU.add, ALU.add))
            rest = 2 * np.pi
            for k in range(4):
                bits = np.float64(rest) if k == 3 else np.float64(
                    np.floor(rest * 2.0 ** (6 + 9 * k)) / 2.0 ** (6 + 9 * k))
                rest -= bits
                pre(v.scalar_tensor_tensor(out=both, in0=turns, scalar=-float(bits), in1=both if k else ang_both,
                                           op0=ALU.mult, op1=ALU.add))
            pre(v.tensor_scalar(trig[:, 0], trig[:, 0], float(np.pi / 2), None, ALU.add))
            pre(v.tensor_scalar(both, both, PI, -PI, ALU.min, ALU.max))
            v.memset(stat[:, 59:60], 0.0).then_inc(s_rope, 1)
            for t in range(T):
                dve.wait_ge(s_x[t], 16)
                v.memset(stat[:, 54 + t:55 + t], 0.0).then_inc(x_done.sem, 1)
            dve.wait_ge(s_rope_act, 2)

            with dve.Fori(0, DEPTH) as layer:
                dve_link.bind(layer)
                for t in range(T):
                    dve.wait_ge(act_ready.sem, act_ready.at(layer, f"h_r{t}"))
                    v.tensor_scalar(normed[:, t, :], xs_res[:, t, :], stat[:, t:t + 1], None, ALU.mult).then_inc(
                        dve_ready.sem, dve_ready.inc(f"h_normed{t}"))
                lo_half(layer, 0)
                dve.wait_ge(s_chan, layer * 16 + 16)
                for t in range(T):
                    turn_lo_tile(layer, "h", t, "pre_mix")
                v.memset(xbc[:, :, 0:3], 0.0).then_inc(dve_ready.sem, dve_ready.inc("pad"))
                for u in range(NU):
                    kind, name, i = UNITS[u]
                    if u + 1 < NU:
                        lo_half(layer, u + 1)
                    for f in fills_of.get(u, []):
                        if not READ_BY_ACT[f]:
                            branch_read(layer, f)
                    for s in STEPS.get(u, []):
                        step(s, layer)
                    if kind == "out" and i == 3:
                        for t in range(T):
                            for q in range(2):
                                add_normed(layer, "mix", t, slice(512 * q, 512 * q + 512)).then_inc(
                                    dve_ready.sem, dve_ready.inc(f"x_mixed{t}{q}"))
                        for t in range(T):
                            turn_lo_tile(layer, "u", t, "pre_mlp")
                    if kind == "up":
                        r, r2 = part(R2, 512 * (i % 2), 2, SEQ), part(R2, 1024 + 512 * (i % 2), 2, SEQ)
                        dve.wait_ge(up_read.sem, up_read.at(layer, f"up{i}"))
                        v.tensor_tensor(r2, r, r, ALU.mult).then_inc(dve_link.sem, 1)
                        dve.wait_ge(dve_link.sem, dve_link.next())
                        dve.wait_ge(up_hi.sem, up_hi.at(layer, f"up{i}"))
                        s = slice(2 * (i % 2), 2 * (i % 2) + 2)
                        v.tensor_tensor(y_lo[:, s, :], r2, y_hi[:, s, :].bitcast(F32), ALU.subtract).then_inc(up_lo.sem, up_lo.inc(f"up{i}"))
                dve.wait_ge(s_gain2, layer * 16 + 16)
                for t in range(T):
                    add_normed(layer, "mlp", t, slice(0, D)).then_inc(x_done.sem, x_done.inc(f"x{t}"))
                v.memset(stat[:, 58:59], 0.0).then_inc(params_used.sem, params_used.inc("all"))
            assert dve_link.n == DVE_LINKS, dve_link.n

        @block.tensor
        def _(pe):
            mm = nc.tensor.matmul

            def open_bank(layer, job):
                if JOB[job] >= 4:
                    pe.wait_ge(job_read.sem, job_read.at(layer, JOBS[JOB[job] - 4]))
                return bank(job)

            def rows_changed(last):
                last.then_inc(pe_link.sem, 1)
                pe.wait_ge(pe_link.sem, pe_link.next())

            def turn(layer, job, blocks):
                b = open_bank(layer, job)
                for src, at in blocks:
                    n = src.shape[1]
                    ins = nc.tensor.transpose(b[0:n, at:at + P], src, ident)
                ins.then_inc(job_full.sem, job_full.inc(job))

            def turn_tokens(layer, prefix, src, n):
                for j in range(n):
                    turn(layer, f"{prefix}{j}", [(src[:, t, P * (2 * j + i):P * (2 * j + i) + P], SEQ * i + P * t)
                                                 for i in range(2) for t in range(T)])

            def turn_tile(layer, name, t, q, src):
                turn(layer, f"{name}{t}{q}", [(src[:, t, P * (4 * q + i):P * (4 * q + i) + P], P * i) for i in range(4)])

            def split_product(dst, lhs, rhs, start, stop):
                mm(dst, lhs[1], rhs[0], start=start, stop=False)
                mm(dst, lhs[0], rhs[1], start=False, stop=False)
                return mm(dst, lhs[0], rhs[0], start=False, stop=stop)

            def pairs(hi, lo, *index):
                return hi[index], lo[index]

            def step(name, layer):
                if name == "mla_turn":
                    pe.wait_ge(dve_ready.sem, dve_ready.at(layer, "c_scaled"))
                    turn(layer, "cq", [(c[:, t, P * m:P * m + P], SEQ * m + P * t) for m in range(2) for t in range(T)])
                    pe.wait_ge(dve_ready.sem, dve_ready.at(layer, "k_rot"))
                    turn(layer, "ckv", [(c[:, t, 256:384], P * t) for t in range(T)]
                         + [(k_rot[:, t, :], SEQ + P * t) for t in range(T)])
                if name == "mla_q":
                    pe.wait_ge(job_read.sem, job_read.at(layer, "cq"))
                    pe.wait_ge(s_param, layer * (16 * n_params) + 16 * n_params)
                    b = open_bank(layer, "qpe")
                    for t in range(T):
                        for k in range(2):
                            ins = mm(b[:, 256 * t:256 * t + 256], cT[:, k, P * t:P * t + P], uq[:, k, 512:768],
                                     start=k == 0, stop=k == 1)
                    ins.then_inc(job_full.sem, job_full.inc("qpe"))
                    for j in range(2):
                        b = open_bank(layer, f"qn{j}")
                        for i in range(2):
                            for k in range(2):
                                h = 4 * j + 2 * i
                                ins = mm(b[:, SEQ * i:SEQ * i + SEQ], uq[:, k, 64 * h:64 * h + P], cT[:, k, :],
                                         start=k == 0, stop=k == 1)
                        ins.then_inc(job_full.sem, job_full.inc(f"qn{j}"))
                if name == "mla_kv":
                    pe.wait_ge(job_read.sem, job_read.at(layer, "ckv"))
                    for j in range(2):
                        b = open_bank(layer, f"kn{j}")
                        for i in range(2):
                            h = 4 * j + 2 * i
                            ins = mm(b[:, SEQ * i:SEQ * i + SEQ], ukv[:, 64 * h:64 * h + P], cT[:, 2, :],
                                     start=True, stop=True)
                        ins.then_inc(job_full.sem, job_full.inc(f"kn{j}"))
                    for t in range(T):
                        b = open_bank(layer, f"v{t}")
                        mm(b, cT[:, 2, P * t:P * t + P], ukv[:, 512:1024], start=True, stop=True).then_inc(job_full.sem, job_full.inc(f"v{t}"))
                if name == "mla_pe":
                    pe.wait_ge(dve_ready.sem, dve_ready.at(layer, "q_rot"))
                    turn(layer, "qpeT", [(q_rot[:, t, P * g:P * g + P], SEQ * g + P * t)
                                         for g in range(2) for t in range(T)])
                if name.startswith("mla_a"):
                    i = int(name[5:])
                    if i < NS:
                        t, h, n = SOFT[i]
                        w = P * (t + 1)
                        b = open_bank(layer, f"score{i}")
                        if i == 0:
                            pe.wait_ge(job_read.sem, job_read.at(layer, "qpeT"))
                        for k in range(n):
                            ins = mm(b[:, w * k:w * k + w], qT[0:96, h + k, P * t:P * t + P], kT[0:96, h + k, 0:w],
                                     start=True, stop=True)
                        ins.then_inc(job_full.sem, job_full.inc(f"score{i}"))
                    if 1 <= i <= NS:
                        pe.wait_ge(act_ready.sem, act_ready.at(layer, f"exp{i - 1}"))
                        turn(layer, f"turn{i - 1}", [(soft[:, (i - 1) % 2, P * k:P * k + P], P * k) for k in range(4)])
                    if i >= 2:
                        j = i - 2
                        t, h, n = SOFT[j]
                        b = open_bank(layer, f"pv{j}")
                        pe.wait_ge(job_read.sem, job_read.at(layer, f"turn{j}"))
                        for k in range(n):
                            for jt in range(t + 1):
                                at = P * (k * (t + 1) + jt)
                                ins = mm(b[:, 64 * k:64 * k + 64], probT[:, j % 2, at:at + P],
                                         v_mla[:, jt, 64 * (h + k):64 * (h + k) + 64], start=jt == 0, stop=jt == t)
                        ins.then_inc(job_full.sem, job_full.inc(f"pv{j}"))
                if name == "mla_y":
                    pe.wait_ge(job_read.sem, job_read.at(layer, f"pv{NS - 1}"))
                    turn_tokens(layer, "mla_y", o_mla, 2)
                if name == "ssd_cum":
                    pe.wait_ge(dve_ready.sem, dve_ready.at(layer, "log_decay"))
                    b = open_bank(layer, "cum")
                    for t in range(T):
                        mm(b[:, 8 * t:8 * t + 8], causal, log_decay[:, 8 * t:8 * t + 8], start=True, stop=True)
                    ins = mm(b[:, 16:24], causal[:, P - 1:P].broadcast_to((P, P)), log_decay[:, 0:8],
                             start=True, stop=True)
                    ins.then_inc(job_full.sem, job_full.inc("cum"))
                if name == "ssd_turn":
                    pe.wait_ge(pool_ready.sem, pool_ready.at(layer, "conv_silu"))
                    b = open_bank(layer, "G")
                    for t in range(T):
                        for g in range(2):
                            at = P * (2 * t + g)
                            ins = mm(b[:, at:at + P], conv[:, 4 + g, P * t:P * t + P], conv[:, 6 + g, P * t:P * t + P],
                                     start=True, stop=True)
                    ins.then_inc(job_full.sem, job_full.inc("G"))
                    for t in range(T):
                        turn(layer, f"xs{t}", [(conv[:, m, P * t:P * t + P], P * m) for m in range(4)])
                    turn(layer, "B", [(conv[:, 4 + g, 0:P], P * g) for g in range(2)])
                if name.startswith("ssd_decay"):
                    i = int(name[9:])
                    t, g = i // 2, i % 2
                    b = open_bank(layer, f"R{i}")
                    for k in range(4):
                        col = 8 * t + 4 * g + k
                        ins = mm(b[:, P * k:P * k + P], log_decay[:, col:col + 1].broadcast_to((P, P)), causal,
                                 start=True, stop=True)
                    ins.then_inc(job_full.sem, job_full.inc(f"R{i}"))
                if name == "ssd_state":
                    b = open_bank(layer, "S")
                    pe.wait_ge(dve_ready.sem, dve_ready.at(layer, "x_end"))
                    for g in range(2):
                        ins = mm(b[:, 256 * g:256 * g + 256], B_tok[:, g, :], x_end[:, 256 * g:256 * g + 256],
                                 start=True, stop=True)
                    ins.then_inc(job_full.sem, job_full.inc("S"))
                if name in ("ssd_y0", "ssd_y1"):
                    t = int(name[5])
                    if t == 1:
                        b = open_bank(layer, "off")
                        pe.wait_ge(job_read.sem, job_read.at(layer, "S"))
                        for g in range(2):
                            ins = mm(b[:, 256 * g:256 * g + 256], conv[:, 6 + g, P:2 * P],
                                     s_state[:, 256 * g:256 * g + 256], start=True, stop=True)
                        ins.then_inc(job_full.sem, job_full.inc("off"))
                    b = open_bank(layer, f"Y{t}")
                    pe.wait_ge(dve_ready.sem, dve_ready.at(layer, f"weights{2 * t + 1}"))
                    for h in range(8):
                        ins = mm(b[:, 64 * h:64 * h + 64], L[:, h, :], xdt[:, t, 64 * h:64 * h + 64],
                                 start=True, stop=True)
                    ins.then_inc(job_full.sem, job_full.inc(f"Y{t}"))
                if name in ("ssd_y", "ret_y", "gla_y"):
                    pe.wait_ge(dve_ready.sem, dve_ready.at(layer, f"{name[:3]}_out"))
                    turn_tokens(layer, name, {"ssd_y": sy, "ret_y": ry, "gla_y": gy}[name], 2)
                if name == "ret_turn":
                    pe.wait_ge(dve_ready.sem, dve_ready.at(layer, "r_scaled"))
                    for j, n in enumerate(("rq", "rk")):
                        turn(layer, n, [(rr[:, t, P * (2 * j + m):P * (2 * j + m) + P], SEQ * m + P * t)
                                        for m in range(2) for t in range(T)])
                if name in ("ret_s0", "ret_s1"):
                    t = int(name[5])
                    pe.wait_ge(job_read.sem, job_read.at(layer, "rk"))
                    b = open_bank(layer, f"rs{t}")
                    for h in (0, 2, 1, 3):
                        if h == 1:
                            rows_changed(ins)
                        r = slice(64 * (h % 2), 64 * (h % 2) + 64)
                        ins = mm(b[:, P * h:P * h + P], rT[r, 2 + h // 2, P * t:P * t + P],
                                 rT[r, h // 2, P * t:P * t + P], start=True, stop=True)
                    ins.then_inc(job_full.sem, job_full.inc(f"rs{t}"))
                    if t == 0:
                        pe.wait_ge(read_act.sem, read_act.at(layer, f"fill{FILLS.index(('token', 'rv', 1))}"))
                        b = open_bank(layer, "rS")
                        for h in range(4):
                            ins = mm(b[64 * (h % 2):64 * (h % 2) + 64, P * (h // 2):P * (h // 2) + P],
                                     rr[:, 0, 256 + 64 * h:320 + 64 * h], rv[:, 0, P * h:P * h + P],
                                     start=True, stop=True)
                        ins.then_inc(job_full.sem, job_full.inc("rS"))
                if name in ("ret_y0", "ret_y1"):
                    t = int(name[5])
                    b = open_bank(layer, f"rY{t}")
                    pe.wait_ge(job_read.sem, job_read.at(layer, f"rs{t}"))
                    for h in range(4):
                        o = slice(P * h, P * h + P)
                        ins = mm(b[:, o], rS[:, t, o], rv[:, t, o], start=h == 0, stop=t == 0, skip_group_check=True)
                    for h in (0, 2, 1, 3) if t == 1 else ():
                        if h == 1:
                            rows_changed(ins)
                        r = slice(64 * (h % 2), 64 * (h % 2) + 64)
                        ins = mm(b[:, P * h:P * h + P], rT[r, h // 2, P:2 * P], r_state[r, h // 2, :],
                                 start=False, stop=True, skip_group_check=True)
                    ins.then_inc(job_full.sem, job_full.inc(f"rY{t}"))
                if name == "gla_low":
                    turn(layer, "low", [(c[:, t, 424:440], P * t) for t in range(T)])
                if name == "gla_decay":
                    b = open_bank(layer, "gate")
                    pe.wait_ge(job_read.sem, job_read.at(layer, "low"))
                    for m in range(2):
                        ins = mm(b[:, SEQ * m:SEQ * m + SEQ], gk2[:, P * m:P * m + P], g_low, start=True, stop=True)
                    ins.then_inc(job_full.sem, job_full.inc("gate"))
                if name == "gla_turn":
                    pe.wait_ge(dve_ready.sem, dve_ready.at(layer, "k_end"))
                    turn(layer, "kst", [(g_end[:, m, P * t:P * t + P], 256 * t + P * m) for t in range(T) for m in range(2)])
                if name in ("gla_s0", "gla_s1"):
                    t = int(name[5])
                    b = open_bank(layer, f"gs{t}")
                    pe.wait_ge(dve_ready.sem, dve_ready.at(layer, "qk_in"))
                    for h in (0, 2, 1, 3):
                        if h == 1:
                            rows_changed(ins)
                        r = slice(64 * (h % 2), 64 * (h % 2) + 64)
                        ins = mm(b[:, P * h:P * h + P], gqk[r, 2 + h // 2, P * t:P * t + P],
                                 gqk[r, h // 2, P * t:P * t + P], start=True, stop=True)
                    ins.then_inc(job_full.sem, job_full.inc(f"gs{t}"))
                if name == "gla_state":
                    pe.wait_ge(job_read.sem, job_read.at(layer, "kst"))
                    pe.wait_ge(read_act.sem, read_act.at(layer, f"fill{FILLS.index(('token', 'gv', 1))}"))
                    for ch in range(3):
                        r, t = slice(64 * (ch % 2), 64 * (ch % 2) + 64), ch // 2
                        b = open_bank(layer, f"gS{ch}")
                        mm(b[:, 256:258], causal, causal[:, 0:2], start=True, stop=True)
                        for h in range(4):
                            ins = mm(b[64 * (h % 2):64 * (h % 2) + 64, P * (h // 2):P * (h // 2) + P],
                                     k_tok[r, t, 64 * h:64 * h + 64], gv[r, t, P * h:P * h + P],
                                     start=True, stop=True)
                        ins.then_inc(job_full.sem, job_full.inc(f"gS{ch}"))
                if name in ("gla_o0", "gla_o1"):
                    t = int(name[5])
                    b = open_bank(layer, f"gY{t}")
                    pe.wait_ge(job_read.sem, job_read.at(layer, "gS2"))
                    for h in (0, 2, 1, 3):
                        if h == 1:
                            rows_changed(ins)
                        for d in {0: (0, ), 2: (), 1: (1, 2, 3), 3: ()}[h]:
                            o = slice(P * d, P * d + P)
                            mm(b[:, o], gS[:, t, o], gv[:, t, o], start=d == 0, stop=False, skip_group_check=True)
                        r = slice(64 * (h % 2), 64 * (h % 2) + 64)
                        o = slice(P * h, P * h + P)
                        for ch in (2 * t, 2 * t + 1):
                            if ch:
                                ins = mm(b[64 * (ch % 2):64 * (ch % 2) + 64, o], gqk[r, h // 2, 64 * ch:64 * ch + 64],
                                         g_state[r, ch - 1, h // 2, :], start=False, stop=True, skip_group_check=True)
                    ins.then_inc(job_full.sem, job_full.inc(f"gY{t}"))

            def products(layer, u, half, b):
                kind, name, i = UNITS[u]
                _, hi, lo = half_views(u, half)
                if kind == "token":
                    f = fills_of[AT[(kind, name, 1)]][0]
                    if (i, half, b) == (0, 0, 0) and f >= 2:
                        wait_for_read(pe, layer, f - 2)
                    if u == 0 and half == 0:
                        pe.wait_ge(job_read.sem, job_read.at(layer, f"h{b}1"))
                    for k in range(2):
                        kk = 4 * i + 2 * half + k
                        s = slice(P * b, P * b + P)
                        ins = split_product(proj[:, 2 * (f % 2) + b, 0:hi.shape[2]], (a_hi[:, kk, s], a_lo[:, kk, s]),
                                            (hi[:, k, :], lo[:, k, :]), kk == 0, kk == 7)
                elif kind in ("channel", "gate"):
                    f = fills_of[u][0]
                    if (half, b) == (0, 0) and f >= 2:
                        wait_for_read(pe, layer, f - 2)
                    s = slice(P * b, P * b + P)
                    for k in range(4):
                        kk = 4 * half + k
                        ins = split_product(proj[:, 2 * (f % 2) + b, 0:SEQ], (hi[:, k, s], lo[:, k, s]),
                                            (a_hi[:, kk, :], a_lo[:, kk, :]), kk == 0, kk == 7)
                elif kind == "branch":
                    f = fills_of[u][half]
                    if b == 0:
                        wait_for_read(pe, layer, f - 2)
                    s = slice(P * b, P * b + P)
                    for k in range(4):
                        ins = split_product(proj[:, 2 * (f % 2) + b, 0:SEQ], (hi[:, k, s], lo[:, k, s]),
                                            (y_hi[:, k, :], y_lo[:, k, :]), k == 0, k == 3)
                elif kind == "up":
                    if i >= 2 and (half, b) == (0, 0):
                        pe.wait_ge(up_read.sem, up_read.at(layer, f"up{i - 2}"))
                    s = slice(P * b, P * b + P)
                    for k in range(4):
                        kk = 4 * half + k
                        ins = split_product(mix[:, 2 * (i % 2) + b, 0:SEQ], (hi[:, k, s], lo[:, k, s]),
                                            (a_hi[:, kk, :], a_lo[:, kk, :]), kk == 0, kk == 7)
                else:
                    if kind == "out" and i == 0 and half == 0:
                        wait_for_read(pe, layer, NF - 1 - b)
                    if kind == "out" and (half, b) == ORDER.get(u, BY_HALVES)[0]:
                        pe.wait_ge(merge_lo.sem, merge_lo.at(layer, f"m{i}"))
                    if kind == "down" and half == 0 and b == 0:
                        pe.wait_ge(up_lo.sem, up_lo.at(layer, f"up{i}"))
                    k = 2 * i + half if kind == "out" else 2 * (i % 2) + half
                    src_hi, src_lo = (a_hi, a_lo) if kind == "out" else (y_hi, y_lo)
                    s = slice(P * b, P * b + P)
                    for n in range(2):
                        cols = slice(512 * n, 512 * n + 512)
                        ins = split_product(proj[:, 2 * b + n, :], (src_hi[:, k, s], src_lo[:, k, s]),
                                            (hi[:, 0, cols], lo[:, 0, cols]), (i, half) == (0, 0),
                                            (i, half) == (3 if kind == "out" else 15, 1))
                return ins

            with pe.Fori(0, DEPTH) as layer:
                pe_link.bind(layer)
                for t in range(T):
                    pe.wait_ge(dve_ready.sem, dve_ready.at(layer, f"h_normed{t}"))
                    for q in range(2):
                        turn_tile(layer, "h", t, q, normed)
                for u in range(NU):
                    kind, name, i = UNITS[u]
                    if kind == "branch" and i == 0:
                        pe.wait_ge(job_read.sem, job_read.at(layer, f"{name}_y1"))
                    order = ORDER.get(u, BY_HALVES)
                    seen = []
                    for half, b in order:
                        if half not in seen and half == 0:
                            pe.wait_ge(lo_even.sem, lo_even.at(layer, f"unit{u}"))
                        if half not in seen and half == 1:
                            pe.wait_ge(lo_odd.sem, lo_odd.at(layer, f"unit{u}"))
                        seen.append(half)
                        ins = products(layer, u, half, b)
                        if seen.count(half) == 2:
                            ins.then_inc(half_done.sem, half_done.inc(f"half{2 * u + half}"))
                        elif half == 1 and (kind, i) in (("out", 3), ("down", 15)):
                            ins.then_inc(tile_done.sem, tile_done.inc(kind))
                    for s in STEPS.get(u, []):
                        step(s, layer)
                    if kind == "out" and i == 3:
                        for t in range(T):
                            for q in range(2):
                                pe.wait_ge(dve_ready.sem, dve_ready.at(layer, f"x_mixed{t}{q}"))
                                turn_tile(layer, "u", t, q, xs_res)
                        pe.wait_ge(job_read.sem, job_read.at(layer, "u11"))
            assert pe_link.n == PE_LINKS, pe_link.n


def kernel(**inputs):
    import concourse.bacc as bacc
    from concourse.bass_utils import run_bass_kernel_spmd

    def by_channel(name):
        a = np.asarray(inputs[name])
        return a.reshape(DEPTH, -1, P).transpose(0, 2, 1)

    def heads_apart(name):
        a = np.asarray(inputs[name])
        h = a.reshape(*a.shape[:2], 8, -1)
        return np.concatenate([h[..., :64].reshape(*a.shape[:2], -1), h[..., 64:].reshape(*a.shape[:2], -1)], 2)

    arrays = {
        "x": inputs["x"], "positions": np.asarray(inputs["positions"]).reshape(T, P).T, "w_in": inputs["w_in"],
        "w_branch": np.asarray(inputs["w_branch"]).reshape(DEPTH, 4 * 512, D),
        "w_out": inputs["w_out"], "w_up": inputs["w_mlp_in"], "w_down": inputs["w_mlp_out"],
        "w_uq": heads_apart("mla_w_uq"), "w_ukv": heads_apart("mla_w_ukv"), "w_gk2": inputs["gla_w_gk2"],
        "chan_in": np.concatenate([by_channel(n) for n in (
            "norm_pre_mix", "norm_pre_mlp", "ssd_conv_w", "ssd_conv_b", "b_gate", "gla_b_gk",
            "mla_q_norm", "mla_kv_norm", "ssd_norm", "ret_norm", "gla_norm")], 2)[[*range(DEPTH), DEPTH - 1]],
        "rows_in": np.concatenate([np.asarray(inputs[n]) for n in (
            "norm_post_mix", "norm_post_mlp", "ssd_dt_bias", "ssd_a_log", "ssd_d")], 1),
        "const_in": constants(),
    }
    nc = bacc.Bacc("TRN2", target_bir_lowering=False, num_devices=1)
    arrays = {f"in_{n}": np.ascontiguousarray(a) for n, a in arrays.items()}
    args = [nc.dram_tensor(n, a.shape, mybir.dt.from_np(a.dtype), kind="ExternalInput").ap()
            for n, a in arrays.items()]
    out = nc.dram_tensor("out", (1, SEQ, D), F32, kind="ExternalOutput").ap()
    hybrid_trunk(nc, *args, out)
    got = run_bass_kernel_spmd(nc, [arrays], core_ids=[0])
    return got.results[0]["out"]
```
